# Optimizing a Trainium2 kernel written in Bass

```python
import math
import jax, jax.numpy as jnp
from jax import lax
import numpy as np

D_MODEL = 1024
BATCH = 1
SEQ = 512
DEPTH = 2

F32 = jnp.float32
GRID_W = 64
HEAD_DIM = 64
BRANCH_WIDTH = 256
N_BRANCHES = 4
LN_EPS = 1e-5
RMS_EPS = 1e-6

HY_WIDTH = 256
HY_ORDER = 2
HY_POS_EMB = 33
HY_FILT_HID = 64
HY_TARGET = 1e-2
HY_SHORT_DECAY_PCT = 0.3
HY_LONG_DECAY_PCT = 1.5

DIL_GROUPS = ((128, 1), (512, 4), (2048, 16))
DIL_N_GROUPS = 3
DIL_HEADS_PER_GROUP = 4
DIL_N_HEADS = DIL_N_GROUPS * DIL_HEADS_PER_GROUP
DIL_WIDTH = DIL_N_HEADS * HEAD_DIM
DIL_BLOCK = 128

S5_WIDTH = 256
S5_GROUP = 16
S5_N_GROUPS = S5_WIDTH // S5_GROUP
S5_STATE = 64
S5_DT_MIN = 1e-3
S5_DT_MAX = 1e-1

GQA_HEADS = 4
GQA_KV_HEADS = 2
GQA_WIDTH = GQA_HEADS * HEAD_DIM
GQA_KV_WIDTH = GQA_KV_HEADS * HEAD_DIM
GQA_BLOCK = 128
ROPE_THETA = 10000.0

IN_SPLITS = (3 * HY_WIDTH, 3 * DIL_WIDTH, S5_WIDTH, GQA_WIDTH, GQA_KV_WIDTH, GQA_KV_WIDTH, N_BRANCHES * D_MODEL)
N_IN = sum(IN_SPLITS)

N_EXPERTS = 16
EC_CAPACITY = 2
EXPERT_FF = 1024

DN_ALPHA = (2 * DEPTH) ** 0.25
DN_BETA = (8 * DEPTH) ** -0.25

kernel_name = 'hybrid_parallel_gated_encoder'

def layer_norm(x, g, b):
    xf = x.astype(F32)
    mu = jnp.mean(xf, axis=-1, keepdims=True)
    var = jnp.mean(jnp.square(xf - mu), axis=-1, keepdims=True)
    return ((xf - mu) * lax.rsqrt(var + LN_EPS) * g + b).astype(x.dtype)

def rms_norm_heads(x, g):
    xf = x.astype(F32)
    return (xf * lax.rsqrt(jnp.mean(xf * xf, axis=-1, keepdims=True) + RMS_EPS) * g).astype(x.dtype)

def short_conv_centred(u, w, b):
    s = u.shape[1]
    up = jnp.pad(u, ((0, 0), (1, 1), (0, 0)))
    return up[:, :s] * w[0] + up[:, 1:s + 1] * w[1] + up[:, 2:] * w[2] + b

def hyena_pos_features(seq_len):
    t = jnp.linspace(0.0, 1.0, seq_len, dtype=F32)[:, None]
    bands = (HY_POS_EMB - 1) // 2
    f = jnp.linspace(1e-4, bands - 1, bands, dtype=F32)[None, :]
    w = 2.0 * math.pi * jnp.arange(seq_len, dtype=F32)[:, None] / seq_len
    z = jnp.concatenate([t, jnp.cos(f * w), -jnp.sin(f * w)], axis=-1)
    return t, z

def hyena_filters(t, z, w1, b1, w2, b2, w3, freq):
    seq_len = z.shape[0]
    f = jnp.sin(freq[0] * (z @ w1 + b1))
    f = jnp.sin(freq[1] * (f @ w2 + b2))
    f = (f @ w3).astype(F32).reshape(seq_len, 2, HY_ORDER, HY_WIDTH)
    max_decay = math.log(HY_TARGET) / HY_SHORT_DECAY_PCT
    min_decay = math.log(HY_TARGET) / HY_LONG_DECAY_PCT
    deltas = jnp.abs(jnp.linspace(min_decay, max_decay, HY_WIDTH, dtype=F32))
    f = f * jnp.exp(-t * deltas)[:, None, None, :]
    fwd, bwd = f[:, 0], f[:, 1]
    k = jnp.concatenate([fwd, jnp.zeros_like(fwd[:1]), bwd[:0:-1]], axis=0)
    return k * lax.rsqrt(jnp.sum(k * k, axis=0, keepdims=True))

def fft_long_conv(u, filt_freq, bias):
    s = u.shape[1]
    uf = u.astype(F32)
    y = jnp.fft.irfft(jnp.fft.rfft(uf, n=2 * s, axis=1) * filt_freq, n=2 * s, axis=1)[:, :s]
    return (y + uf * bias).astype(u.dtype)

def hyena_mixer(proj, conv_w, conv_b, filt, bias):
    u = short_conv_centred(proj, conv_w, conv_b)
    parts = jnp.split(u, HY_ORDER + 1, axis=-1)
    z = parts[0]
    filt_freq = jnp.fft.rfft(filt, axis=0)
    for n in range(HY_ORDER):
        z = parts[n + 1] * fft_long_conv(z, filt_freq[:, n], bias[n])
    return z

def dilated_attention(q, k, v):
    bsz, s = q.shape[0], q.shape[1]
    offs = np.stack([np.arange(-(w // 2), w // 2 + 1, d) for (w, d) in DIL_GROUPS])
    offs = np.repeat(offs, DIL_HEADS_PER_GROUP, axis=0)
    slopes = 2.0 ** (-8.0 * np.arange(1, DIL_N_HEADS + 1) / DIL_N_HEADS)
    off = jnp.asarray(offs, dtype=jnp.int32)
    alibi = jnp.asarray(-slopes[:, None] * np.abs(offs), dtype=F32)
    hidx = jnp.arange(DIL_N_HEADS)[:, None, None]
    scale = HEAD_DIM ** -0.5
    q = q.transpose(0, 2, 1, 3)
    k = k.transpose(0, 2, 1, 3)
    v = v.transpose(0, 2, 1, 3)
    nblk = s // DIL_BLOCK
    qb = q.reshape(bsz, DIL_N_HEADS, nblk, DIL_BLOCK, HEAD_DIM).transpose(2, 0, 1, 3, 4)
    starts = jnp.arange(nblk, dtype=jnp.int32) * DIL_BLOCK

    def one_block(args):
        qblk, start = args
        pos = start + jnp.arange(DIL_BLOCK, dtype=jnp.int32)[None, :, None] + off[:, None, :]
        valid = (pos >= 0) & (pos < s)
        pos = jnp.clip(pos, 0, s - 1)
        kg = k[:, hidx, pos]
        vg = v[:, hidx, pos]
        sc = jnp.einsum('bhqd,bhqkd->bhqk', qblk, kg).astype(F32) * scale + alibi[:, None, :]
        sc = jnp.where(valid[None], sc, -jnp.inf)
        lse = jax.nn.logsumexp(sc, axis=-1)
        p = jnp.exp(sc - lse[..., None]).astype(vg.dtype)
        o = jnp.einsum('bhqk,bhqkd->bhqd', p, vg)
        o = o.reshape(bsz, DIL_N_GROUPS, DIL_HEADS_PER_GROUP, DIL_BLOCK, HEAD_DIM)
        wgt = jax.nn.softmax(lse.reshape(bsz, DIL_N_GROUPS, DIL_HEADS_PER_GROUP, DIL_BLOCK), axis=1)
        return jnp.einsum('bghq,bghqd->bhqd', wgt.astype(o.dtype), o)

    out = lax.map(one_block, (qb, starts))
    return out.transpose(1, 0, 3, 2, 4).reshape(bsz, s, DIL_HEADS_PER_GROUP * HEAD_DIM)

def _ssm_combine(e1, e2):
    a1, b1 = e1
    a2, b2 = e2
    return a1 * a2, a2 * b1 + b2

def s5_mixer(u, lam_re, lam_im, log_dt, b_re, b_im, c_re, c_im, d, glu_w, glu_b):
    bsz, s = u.shape[0], u.shape[1]
    uf = u.astype(F32)
    ug = uf.reshape(bsz, s, S5_N_GROUPS, S5_GROUP).astype(jnp.complex64)
    y = d.astype(F32) * uf
    for direction in range(2):
        lam = lax.complex(lam_re[direction].astype(F32), lam_im[direction].astype(F32))
        dt = jnp.exp(log_dt[direction].astype(F32))[:, None]
        a_bar = jnp.exp(lam * dt)
        bmat = lax.complex(b_re[direction].astype(F32), b_im[direction].astype(F32))
        b_bar = ((a_bar - 1.0) / lam)[..., None] * bmat
        bu = jnp.einsum('bsgc,gpc->bsgp', ug, b_bar)
        a = jnp.broadcast_to(a_bar, bu.shape)
        _, xs = lax.associative_scan(_ssm_combine, (a, bu), axis=1, reverse=(direction == 1))
        cmat = lax.complex(c_re[direction].astype(F32), c_im[direction].astype(F32))
        y = y + jnp.real(jnp.einsum('bsgp,gcp->bsgc', xs, cmat)).reshape(bsz, s, S5_WIDTH)
    z = jax.nn.gelu(y)
    return (z * jax.nn.sigmoid(z @ glu_w + glu_b)).astype(u.dtype)

def axial_rope_angles(s):
    n_rows = s // GRID_W
    rows = jnp.repeat(jnp.arange(n_rows, dtype=F32), GRID_W)
    cols = (jnp.arange(s) % GRID_W).astype(F32)
    half = HEAD_DIM // 2
    inv = ROPE_THETA ** (-jnp.arange(0, half, 2, dtype=F32) / half)
    return rows[:, None] * inv, cols[:, None] * inv

def _rope_half(x, ang):
    c = jnp.cos(ang)[:, None, :]
    sn = jnp.sin(ang)[:, None, :]
    x1, x2 = jnp.split(x, 2, axis=-1)
    return jnp.concatenate([x1 * c - x2 * sn, x2 * c + x1 * sn], axis=-1)

def apply_axial_rope(x, ang_r, ang_c):
    xf = x.astype(F32)
    half = HEAD_DIM // 2
    return jnp.concatenate([_rope_half(xf[..., :half], ang_r), _rope_half(xf[..., half:], ang_c)], axis=-1).astype(x.dtype)

def gqa_attention(q, k, v, q_norm, k_norm, ang_r, ang_c):
    bsz, s = q.shape[0], q.shape[1]
    rep = GQA_HEADS // GQA_KV_HEADS
    q = apply_axial_rope(rms_norm_heads(q, q_norm), ang_r, ang_c)
    k = apply_axial_rope(rms_norm_heads(k, k_norm), ang_r, ang_c)
    nblk = s // GQA_BLOCK
    qb = q.reshape(bsz, nblk, GQA_BLOCK, GQA_KV_HEADS, rep, HEAD_DIM).transpose(1, 0, 3, 4, 2, 5)
    kt = k.transpose(0, 2, 1, 3)
    vt = v.transpose(0, 2, 1, 3)
    scale = HEAD_DIM ** -0.5

    def one_block(qblk):
        sc = jnp.einsum('bgrqd,bgkd->bgrqk', qblk, kt).astype(F32) * scale
        p = jax.nn.softmax(sc, axis=-1).astype(vt.dtype)
        return jnp.einsum('bgrqk,bgkd->bgrqd', p, vt)

    o = lax.map(one_block, qb)
    return o.transpose(1, 0, 4, 2, 3, 5).reshape(bsz, s, GQA_WIDTH)

def mixing_sublayer(h, w_in, hy_conv_w, hy_conv_b, hy_w1, hy_b1, hy_w2, hy_b2, hy_w3, hy_freq, hy_bias,
                    s5_lam_re, s5_lam_im, s5_log_dt, s5_b_re, s5_b_im, s5_c_re, s5_c_im, s5_d, s5_glu_w, s5_glu_b,
                    gqa_q_norm, gqa_k_norm, w_branch, w_out, pos_t, pos_z, ang_r, ang_c):
    bsz, s = h.shape[0], h.shape[1]
    proj = h @ w_in
    split_points = np.cumsum(IN_SPLITS)[:-1].tolist()
    hy_in, dil_qkv, s5_in, gq, gk, gv, gate_logits = jnp.split(proj, split_points, axis=-1)
    filt = hyena_filters(pos_t, pos_z, hy_w1, hy_b1, hy_w2, hy_b2, hy_w3, hy_freq)
    y_a = hyena_mixer(hy_in, hy_conv_w, hy_conv_b, filt, hy_bias)
    dq, dk, dv = [t.reshape(bsz, s, DIL_N_HEADS, HEAD_DIM) for t in jnp.split(dil_qkv, 3, axis=-1)]
    y_b = dilated_attention(dq, dk, dv)
    y_c = s5_mixer(s5_in, s5_lam_re, s5_lam_im, s5_log_dt, s5_b_re, s5_b_im, s5_c_re, s5_c_im, s5_d, s5_glu_w, s5_glu_b)
    y_d = gqa_attention(gq.reshape(bsz, s, GQA_HEADS, HEAD_DIM), gk.reshape(bsz, s, GQA_KV_HEADS, HEAD_DIM),
                        gv.reshape(bsz, s, GQA_KV_HEADS, HEAD_DIM), gqa_q_norm, gqa_k_norm, ang_r, ang_c)
    gate_logits = gate_logits.reshape(bsz, s, N_BRANCHES, D_MODEL)
    merged = None
    for i, y in enumerate((y_a, y_b, y_c, y_d)):
        term = jax.nn.sigmoid(gate_logits[:, :, i]) * (y @ w_branch[i])
        merged = term if merged is None else merged + term
    return merged @ w_out

def expert_choice_moe(h, router_w, w_gate, w_up, w_down):
    bsz, s = h.shape[0], h.shape[1]
    cap = (EC_CAPACITY * s) // N_EXPERTS
    aff = jax.nn.softmax((h @ router_w).astype(F32), axis=-1)
    g, idx = lax.top_k(aff.transpose(0, 2, 1), cap)
    bidx = jnp.arange(bsz)[:, None, None]
    xs = h[bidx, idx]
    hid = jax.nn.silu(jnp.einsum('becd,edf->becf', xs, w_gate)) * jnp.einsum('becd,edf->becf', xs, w_up)
    out = jnp.einsum('becf,efd->becd', hid, w_down) * g[..., None].astype(h.dtype)
    return jnp.zeros_like(h).at[bidx, idx].add(out)

def setup_inputs(seed: int = 0) -> dict:
    key = jax.random.key(seed)
    ks = iter(jax.random.split(key, 40))

    def nrm(shape, scale):
        return scale * jax.random.normal(next(ks), shape, F32)

    L = DEPTH
    G, P, CG = S5_N_GROUPS, S5_STATE, S5_GROUP
    lam_im0 = math.pi * jnp.arange(P, dtype=F32)
    return {
        'x': nrm((BATCH, SEQ, D_MODEL), 1.0),
        'ln_in_g': 1.0 + nrm((D_MODEL,), 0.02),
        'ln_in_b': nrm((D_MODEL,), 0.02),
        'w_in': nrm((L, D_MODEL, N_IN), D_MODEL ** -0.5),
        'hy_conv_w': nrm((L, 3, 3 * HY_WIDTH), 3 ** -0.5),
        'hy_conv_b': nrm((L, 3 * HY_WIDTH), 0.02),
        'hy_w1': nrm((L, HY_POS_EMB, HY_FILT_HID), HY_POS_EMB ** -0.5),
        'hy_b1': nrm((L, HY_FILT_HID), 0.1),
        'hy_w2': nrm((L, HY_FILT_HID, HY_FILT_HID), HY_FILT_HID ** -0.5),
        'hy_b2': nrm((L, HY_FILT_HID), 0.1),
        'hy_w3': nrm((L, HY_FILT_HID, 2 * HY_ORDER * HY_WIDTH), HY_FILT_HID ** -0.5),
        'hy_freq': 1.0 + nrm((L, 2, HY_FILT_HID), 0.02),
        'hy_bias': nrm((L, HY_ORDER, HY_WIDTH), 0.5),
        's5_lam_re': -0.5 + nrm((L, 2, G, P), 0.01),
        's5_lam_im': lam_im0 + nrm((L, 2, G, P), 0.01),
        's5_log_dt': jax.random.uniform(next(ks), (L, 2, G), F32, math.log(S5_DT_MIN), math.log(S5_DT_MAX)),
        's5_b_re': nrm((L, 2, G, P, CG), (2 * CG) ** -0.5),
        's5_b_im': nrm((L, 2, G, P, CG), (2 * CG) ** -0.5),
        's5_c_re': nrm((L, 2, G, CG, P), 0.5),
        's5_c_im': nrm((L, 2, G, CG, P), 0.5),
        's5_d': nrm((L, S5_WIDTH), 1.0),
        's5_glu_w': nrm((L, S5_WIDTH, S5_WIDTH), S5_WIDTH ** -0.5),
        's5_glu_b': nrm((L, S5_WIDTH), 0.02),
        'gqa_q_norm': 1.0 + nrm((L, HEAD_DIM), 0.02),
        'gqa_k_norm': 1.0 + nrm((L, HEAD_DIM), 0.02),
        'w_branch': nrm((L, N_BRANCHES, BRANCH_WIDTH, D_MODEL), BRANCH_WIDTH ** -0.5),
        'w_out': nrm((L, D_MODEL, D_MODEL), DN_BETA * D_MODEL ** -0.5),
        'ln1_g': 1.0 + nrm((L, D_MODEL), 0.02),
        'ln1_b': nrm((L, D_MODEL), 0.02),
        'router_w': nrm((L, D_MODEL, N_EXPERTS), D_MODEL ** -0.5),
        'exp_w_gate': nrm((L, N_EXPERTS, D_MODEL, EXPERT_FF), D_MODEL ** -0.5),
        'exp_w_up': nrm((L, N_EXPERTS, D_MODEL, EXPERT_FF), D_MODEL ** -0.5),
        'exp_w_down': nrm((L, N_EXPERTS, EXPERT_FF, D_MODEL), DN_BETA * EXPERT_FF ** -0.5),
        'ln2_g': 1.0 + nrm((L, D_MODEL), 0.02),
        'ln2_b': nrm((L, D_MODEL), 0.02),
    }

def reference(x, ln_in_g, ln_in_b, w_in, hy_conv_w, hy_conv_b, hy_w1, hy_b1, hy_w2, hy_b2, hy_w3, hy_freq, hy_bias,
              s5_lam_re, s5_lam_im, s5_log_dt, s5_b_re, s5_b_im, s5_c_re, s5_c_im, s5_d, s5_glu_w, s5_glu_b,
              gqa_q_norm, gqa_k_norm, w_branch, w_out, ln1_g, ln1_b,
              router_w, exp_w_gate, exp_w_up, exp_w_down, ln2_g, ln2_b):
    s = x.shape[1]
    pos_t, pos_z = hyena_pos_features(s)
    ang_r, ang_c = axial_rope_angles(s)
    h = layer_norm(x, ln_in_g, ln_in_b)
    for l in range(DEPTH):
        mix = mixing_sublayer(h, w_in[l], hy_conv_w[l], hy_conv_b[l], hy_w1[l], hy_b1[l], hy_w2[l], hy_b2[l],
                              hy_w3[l], hy_freq[l], hy_bias[l],
                              s5_lam_re[l], s5_lam_im[l], s5_log_dt[l], s5_b_re[l], s5_b_im[l], s5_c_re[l],
                              s5_c_im[l], s5_d[l], s5_glu_w[l], s5_glu_b[l],
                              gqa_q_norm[l], gqa_k_norm[l], w_branch[l], w_out[l], pos_t, pos_z, ang_r, ang_c)
        h = layer_norm(DN_ALPHA * h + mix, ln1_g[l], ln1_b[l])
        ffn = expert_choice_moe(h, router_w[l], exp_w_gate[l], exp_w_up[l], exp_w_down[l])
        h = layer_norm(DN_ALPHA * h + ffn, ln2_g[l], ln2_b[l])
    return h


_drawn_inputs = setup_inputs


def setup_inputs(seed=0):
    import zlib

    import numpy as np

    out = dict(_drawn_inputs(seed))
    spreads = {}
    factors = {'hy_freq': 5.403,
     's5_lam_re': 200.0,
     's5_glu_b': 39.226,
     'gqa_q_norm': 8.0,
     'gqa_k_norm': 8.0,
     's5_b_im': 2.713,
     's5_c_im': 2.737,
     's5_b_re': 3.642,
     's5_c_re': 3.364}
    for name, (base, spread) in spreads.items():
        noise = np.random.default_rng([zlib.crc32(name.encode()), seed]).standard_normal(out[name].shape)
        drawn = base * np.exp(spread * noise) if base else spread * noise
        out[name] = __import__('jax').numpy.asarray(drawn.astype(out[name].dtype))
    for name, factor in factors.items():
        out[name] = (out[name] * factor).astype(out[name].dtype)
    return out
```

```python
import math
from contextlib import ExitStack

import numpy as np

import concourse.bass as bass
from concourse import mybir

F32 = mybir.dt.float32
ALU = mybir.AluOpType
ACT = mybir.ActivationFunctionType
AX = mybir.AxisListType

P = 128
SEQ, DM, DEPTH = 512, 1024, 2
NT = SEQ // P
ND = DM // P
HD = 64
HYW, S5W = 256, 256
DILH, GROUPS, SLOTS = 12, 3, 4
GQH, GKV = 4, 2
NE, CAP, FF = 16, 64, 1024
NF = FF // P
CW = 256
ALPHA = (2 * DEPTH) ** 0.25
LN_EPS, RMS_EPS = 1e-5, 1e-6
ROUND = 12582912.0
TWO_PI = 2.0 * math.pi
BIG = 1e30

HY0, DQ0, DK0, DV0, S50, GQ0, GK0, GATE0 = 0, 3, 6, 9, 12, 13, 14, 15
FIRST_CHUNKS = [S50, GQ0, GK0, HY0, HY0 + 1, HY0 + 2]
SECOND_CHUNKS = list(range(DQ0, S50))
BRANCHES = [0, 2, 1, 3]
GATE_CHUNKS = [GATE0 + 4 * b + q for b in BRANCHES for q in range(4)]
RING = 4
OUT_CHUNKS = DM // CW
N_FIRST, N_SECOND, N_GATE = len(FIRST_CHUNKS), len(SECOND_CHUNKS), len(GATE_CHUNKS)
PER_LAYER = N_FIRST + N_SECOND + N_GATE + OUT_CHUNKS
S5_TILES = 16


def constants():
    t = np.arange(SEQ)
    ang = 2.0 * np.pi * ((t[:, None] * t[None, :]) % (2 * SEQ)) / (2 * SEQ)
    sign = np.where(t % 2 == 0, 1.0, -1.0)
    fc = np.cos(ang)
    fs = -np.sin(ang)
    fs[:, 0] = sign
    gs = -np.sin(ang)
    gs[0, :] = sign
    wf = np.full((SEQ,), 2.0 / (2 * SEQ))
    wf[0] = 1.0 / (2 * SEQ)
    tl = lambda a: np.ascontiguousarray(a.reshape(NT, P, -1).transpose(1, 0, 2)).astype(np.float32)
    lin = np.linspace(0.0, 1.0, SEQ, dtype=np.float32)
    bands = np.linspace(1e-4, 15, 16, dtype=np.float32)
    w = (2.0 * math.pi * np.arange(SEQ, dtype=np.float32) / SEQ).astype(np.float32)
    fw = (bands[None, :] * w[:, None]).astype(np.float32)
    z = np.concatenate([lin[:, None], np.cos(fw), -np.sin(fw)], axis=-1).astype(np.float32)
    deltas = np.abs(np.linspace(math.log(1e-2) / 1.5, math.log(1e-2) / 0.3, HYW, dtype=np.float32))
    decay = np.exp(-lin[:, None] * deltas[None, :]).astype(np.float32)
    inv = 10000.0 ** (-np.arange(0, 32, 2, dtype=np.float32) / 32)
    rows, cols = (t // 64).astype(np.float32), (t % 64).astype(np.float32)
    cs, sn = [], []
    for pos in (rows, cols):
        a = pos[:, None] * inv[None, :]
        cs += [np.cos(a), np.cos(a)]
        sn += [-np.sin(a), np.sin(a)]
    off = np.arange(SEQ + 384)[None, :] - 384 - np.arange(P)[:, None]
    far = np.zeros((DILH, P, SEQ + 384), np.float32)
    for g, (win, dil) in enumerate(((128, 1), (512, 4), (2048, 16))):
        ok = (np.abs(off) <= win // 2) & (off % dil == 0)
        for s in range(SLOTS):
            h = g * SLOTS + s
            far[h] = np.where(ok, 2.0 ** (-8.0 * (h + 1) / DILH) * np.abs(off), BIG)
    return {
        "c_fc": tl(fc), "c_fs": tl(fs), "c_gs": tl(gs),
        "c_wf": np.ascontiguousarray(wf.reshape(NT, P).T).astype(np.float32),
        "c_zt": np.ascontiguousarray(z.T), "c_decay": tl(decay),
        "c_cos": tl(np.concatenate(cs, -1)), "c_sin": tl(np.concatenate(sn, -1)),
        "c_far": far, "c_ident": np.eye(P, dtype=np.float32),
        "c_iota": np.broadcast_to(t.astype(np.float32), (P, SEQ)).copy(),
    }


class Link:

    def __init__(self, eng, sem):
        self.eng, self.sem, self.n = eng, sem, 0

    def __call__(self, ins):
        self.mark(ins)
        self.hold()

    def mark(self, ins):
        ins.then_inc(self.sem, 1)
        self.n += 1

    def hold(self):
        self.eng.wait_ge(self.sem, self.n)


def wide(ap, n):
    return ap.to_broadcast([ap.shape[0], n])


FIRST_STEPS = (
    [("project", 0), ("table", 0), ("mlp", 0), ("project", 1), ("mlp", 1), ("states", 0), ("table", 1)]
    + [("filter", 0), ("filter", 1), ("filter", 2), ("filter", 3), ("project", 2), ("output", 0)]
    + [("norm", 0), ("states", 1), ("table", 2), ("spectrum", 0), ("spectrum", 1), ("spectrum", 2)]
    + [("spectrum", 3), ("nyquist", 0), ("output", 1), ("project", 3), ("states", 2), ("table", 3)]
    + [("project", 4), ("conv", 0), ("output", 2), ("states", 3), ("table", 4)]
    + [("project", 5), ("conv", 1), ("output", 3), ("states", 4), ("table", 5), ("conv", 2)]
    + [("tokens", 0), ("tokens", 1), ("tokens", 2), ("tokens", 3), ("output", 4)]
    + [("states", 5), ("table", 6), ("forward", 0), ("product", 0), ("output", 5)]
    + [("states", 6), ("table", 7), ("back", 0), ("output", 6), ("forward", 1), ("product", 1)]
    + [("states", 7), ("output", 7), ("back", 1)]
)
UNIT_NAMES = []
for _step, _i in FIRST_STEPS:
    UNIT_NAMES += {
        "mlp": [("mlp", _i)],
        "filter": [("filter", _i, 0), ("filter", _i, 1)],
        "norm": [("norm",)],
        "spectrum": [("spectrum", _i, 0), ("spectrum", _i, 1)],
        "nyquist": [("nyquist",)],
        "tokens": [("tokens", _i)],
        "forward": [("forward", _i, f) for f in range(NT)],
        "back": [("back", _i, c) for c in range(2)],
    }.get(_step, [])
UNIT = {name: n for n, name in enumerate(UNIT_NAMES)}
assert len(UNIT) == len(UNIT_NAMES)


SECOND_STEPS = [("table", 8), ("rms", 0)]
for _n in range(8, 16):
    SECOND_STEPS += [("project", N_FIRST + _n - 8), ("states", _n)] + ([("table", _n + 1)] if _n < 15 else [])
    if _n >= 9:
        SECOND_STEPS += [("output", _n - 1)]
    if _n == 9:
        SECOND_STEPS += [("rope", 0)]
    if _n == 11:
        SECOND_STEPS += [("heads", 0), ("heads", 1), ("heads", 2)]
SECOND_STEPS += [("project", N_FIRST + 8), ("output", 15), ("gelu", 0), ("glu", 0), ("glu", 1)]

HEADS = [g * SLOTS + s for s in range(SLOTS) for g in range(GROUPS)]
N_SCORES = 4 * (DILH + GQH)
GATES_AT = {0: 0, 2: 1, 3: 2, 5: 3, 6: 4, 8: 5, 9: 6, 11: 7, 13: 8, 14: 9, 15: 10}
ATTEND_STEPS = []
for _w in range(N_SCORES + 2):
    if _w < N_SCORES:
        ATTEND_STEPS.append(("scores", _w))
    if _w < N_SCORES and _w % 4 in (1, 3) and _w // 4 in GATES_AT:
        ATTEND_STEPS.append(("gate", 2 * GATES_AT[_w // 4] + _w % 4 // 2))
    if 1 <= _w <= N_SCORES:
        ATTEND_STEPS.append(("turn", _w - 1))
    if _w >= 2:
        ATTEND_STEPS.append(("mix", _w - 2))
        if (_w - 2) % 12 == 11 and _w - 2 < 4 * DILH:
            ATTEND_STEPS.append(("combine", (_w - 2) // 12))
    if _w == 4 * DILH + 4:
        ATTEND_STEPS += [("features", (1, 0)), ("features", (1, 1))]
ATTEND_STEPS += [("gate", 22), ("gate", 23), ("features", (3, 0)), ("features", (3, 1))]
ATTEND_STEPS += [("gate", _i) for _i in range(24, 32)]
SIDE = {s: n for n, s in enumerate(x for x in ATTEND_STEPS if x[0] in ("gate", "features"))}
assert len(SIDE) == 36


def lay_out(inputs):
    g = {k: np.asarray(v) for k, v in inputs.items()}
    L = DEPTH
    d = {k: g[k] for k in ("ln_in_g", "ln_in_b", "w_in", "hy_w1", "hy_w2", "hy_w3", "w_branch", "w_out",
                           "ln1_g", "ln1_b", "router_w", "exp_w_gate", "exp_w_up", "exp_w_down", "ln2_g", "ln2_b")}
    d["x"] = g["x"][0]
    cols = lambda a: a.reshape(L, -1, P).transpose(0, 2, 1)
    d["hy_cols"] = np.stack([g["hy_freq"][:, 0], g["hy_freq"][:, 1], g["hy_b1"], g["hy_b2"]], -1)
    d["hy_conv"] = np.stack([cols(g["hy_conv_w"][:, 0]), cols(g["hy_conv_w"][:, 1]), cols(g["hy_conv_w"][:, 2]),
                             cols(g["hy_conv_b"])], -1)
    d["hy_bias_row"] = g["hy_bias"].reshape(L, 512)
    d["s5_dcol"] = cols(g["s5_d"])
    d["s5_glu_bcol"] = cols(g["s5_glu_b"])
    d["s5_glu_w"] = g["s5_glu_w"]
    tiles = lambda a: a.reshape(L, 2, 2, 4, P).transpose(0, 4, 2, 1, 3).reshape(L, P, S5_TILES)
    dt = np.repeat(g["s5_log_dt"][..., None], HD, axis=-1)
    d["s5_par"] = np.stack([tiles(g["s5_lam_re"]), tiles(g["s5_lam_im"]), tiles(dt)], 2).transpose(0, 1, 2, 3)
    bt = np.zeros((L, P, 2, 2, 2, P), np.float32)
    ct = np.zeros((L, P, 2, S5_TILES, 32), np.float32)
    for part, (b, c) in enumerate(((g["s5_b_re"], g["s5_c_re"]), (g["s5_b_im"], g["s5_c_im"]))):
        for n in range(S5_TILES):
            jc, dr, jj = n // 8, n % 8 // 4, n % 4
            for q in range(2):
                grp = 8 * jc + 2 * jj + q
                bt[:, 32 * jj + 16 * q:32 * jj + 16 * q + 16, part, dr, jc, 64 * q:64 * q + 64] = b[:, dr, grp].transpose(0, 2, 1)
                ct[:, 64 * q:64 * q + 64, part, n, 16 * q:16 * q + 16] = c[:, dr, grp].transpose(0, 2, 1)
    d["s5_b"], d["s5_c"] = bt, ct
    d["gq_norm_row"] = np.concatenate([g["gqa_q_norm"]] * GQH + [g["gqa_k_norm"]] * GKV, -1)
    return d


def build(nc, A, out, stage=99, depth=DEPTH):
    ctx = ExitStack()
    sems = []

    def sem(name):
        s = ctx.enter_context(nc.semaphore(name))
        sems.append(s)
        return s

    K = 1024

    class Area:

        def __init__(self, base, end):
            self.base, self.end = base, end

        def take(self, name, shape):
            n = (4 * int(np.prod(shape[1:])) + 31) // 32 * 32
            a = nc.alloc_sbuf_tensor_at(name, shape, F32, offset=FLOOR + self.base)
            self.base += n
            assert self.base <= self.end, (name, self.base, self.end)
            return a

    FLOOR = (nc.sbuf_base + 31) // 32 * 32
    END = 207 * K
    assert FLOOR + END <= nc.sbuf_usable_end
    m = Area(0, END)
    hT = m.take("hT", [P, ND, SEQ])
    ring = m.take("ring", [P, RING, ND, CW])
    ident = m.take("ident", [P, P])
    y_at = m.base
    ya, yb, yc, yd = (m.take(n, [P, 2, SEQ]) for n in ("ya", "yb", "yc", "yd"))
    yT = [ya, yb, yc, yd]
    ones = m.take("ones", [P, P])
    wf = m.take("wf", [P, NT])
    half_pi = m.take("half_pi", [P, 1])
    eps_ln = m.take("eps_ln", [P, 1])
    eps_rms = m.take("eps_rms", [P, 1])
    posT = m.take("posT", [P, NT, NE])
    aff = m.take("aff", [P, NT, NE])
    frq = m.take("frq", [HD, 4])
    frw = m.take("frw", [HD, 4])
    stat = m.take("stat", [P, 24])
    cw = m.take("cw", [P, 6, 4])
    base = m.base

    gtok = m.take("gtok", [P, NT, 512])
    iota = m.take("iota", [P, SEQ])
    uT = m.take("uT", [P, 2, SEQ])
    bT = m.take("bT", [P, 2, 2, 2, P])
    cT = m.take("cT", [P, 2, S5_TILES, 32])
    par = m.take("par", [P, 16, S5_TILES])
    s5d = m.take("s5d", [P, 2])
    turn = m.take("turn", [P, SEQ])
    frac = m.take("frac", [P, SEQ])
    trig = m.take("trig", [P, 2, 2, SEQ])
    rot = m.take("rot", [P, 2, 2, SEQ])
    zz = m.take("zz", [P, 2, SEQ])
    xx = m.take("xx", [P, 2, SEQ])
    s5_end = m.base
    fc = m.take("fc", [P, NT, SEQ])
    fs = m.take("fs", [P, NT, SEQ])
    gs = m.take("gs", [P, NT, SEQ])
    kre = m.take("kre", [P, NT, 512])
    kim = m.take("kim", [P, NT, 512])
    knyq = m.take("knyq", [P, 512])
    z0_at = m.base
    z0 = m.take("z0", [P, NT, HYW])
    x1 = m.take("x1", [P, NT, HYW])
    share = m.base
    m = Area(z0_at, share)
    zt = m.take("zt", [33, SEQ])
    w3 = m.take("w3", [HD, 1024])
    f1 = m.take("f1", [HD, SEQ])
    m = Area(share, END)
    fa = m.take("fa", [P, NT, 512])
    fb = m.take("fb", [P, NT, 512])
    decay = m.take("decay", [P, NT, HYW])
    bwd = m.take("bwd", [P, 512])
    sq = m.take("sq", [P, 2, 512])
    nsum = m.take("nsum", [P, 512])
    f2 = m.take("f2", [HD, SEQ])
    w1 = m.take("w1", [33, HD])
    w2 = m.take("w2", [HD, HD])
    hyb = m.take("hyb", [P, 512])
    rn = m.take("rn", [P, 512])
    m = Area(share, END)
    hyT = m.take("hyT", [P, 6, SEQ + 2])
    u01 = m.take("u01", [P, 4, SEQ])
    spec = m.take("spec", [P, NT, 2, HYW])
    prod = nc.alloc_sbuf_tensor_at("prod", [P, 4, NT, HYW], F32, offset=FLOOR + share)
    assert m.base <= END


    m = Area(s5_end, END)
    qd = m.take("qd", [P, 6, SEQ])
    kd = m.take("kd", [P, 6, SEQ])
    vd = m.take("vd", [P, NT, DILH * HD])
    qg = m.take("qg", [P, 2, SEQ])
    kg = m.take("kg", [P, SEQ])
    attend_at = m.base
    gnorm = m.take("gnorm", [P, 6 * HD])
    rcos = m.take("rcos", [P, NT, HD])
    rsin = m.take("rsin", [P, NT, HD])
    gluw = m.take("gluw", [P, 2, S5W])
    glub = m.take("glub", [P, 2])
    ra = m.take("ra", [P, NT, 6 * HD])
    rb = m.take("rb", [P, NT, 6 * HD])
    rp = m.take("rp", [P, NT, 6 * HD])
    zg = m.take("zg", [P, 2, SEQ])
    zs = m.take("zs", [P, 2, SEQ])
    m = Area(base + 16 * K, s5_end)
    merged = m.take("merged", [P, ND, SEQ])
    far = m.take("far", [P, 2, SEQ + 384])
    sm = m.take("sm", [P, 2, SEQ])
    pr = m.take("pr", [P, 2, SEQ])
    m = Area(attend_at, END)
    pT = m.take("pT", [P, 2, SEQ])
    wb = m.take("wb", [P, 4, 2, CW])
    th = m.take("th", [P, 2, SEQ])
    term = m.take("term", [P, SEQ])
    yt = m.take("yt", [P, NT, 256])
    obuf = m.take("obuf", [P, 3, 4, HD])
    low = m.take("low", [P, 64])
    ssum = m.take("ssum", [P, 64])
    ew = m.take("ew", [P, 12])
    es = m.take("es", [P, 12])
    rs = m.take("rs", [P, 4])
    m = Area(base, END)
    h = m.take("h", [P, NT, DM])
    assert m.base == base + 16 * K
    accx = m.take("accx", [P, NT, DM])
    ering = m.take("ering", [P, 6, ND, 512])
    lng = m.take("lng", [P, DM])
    lnb = m.take("lnb", [P, DM])
    lnst = m.take("lnst", [P, NT, 12])
    lnmv = m.take("lnmv", [P, NT, 2])
    lnrs = m.take("lnrs", [P, NT])
    rmax = m.take("rmax", [P, NT])
    rw = m.take("rw", [P, ND, NE])
    m = Area(y_at, y_at + 16 * K)
    affT = m.take("affT", [NE, SEQ])
    work = m.take("work", [NE, SEQ])
    gt = m.take("gt", [NE, SEQ])
    eq = m.take("eq", [NE, SEQ])
    top8 = m.take("top8", [NE, 8])
    left = m.take("left", [NE, 1])
    m = Area(16 * K, 48 * K)
    xs = m.take("xs", [P, ND, P])
    pp = m.take("pp", [P, NT, P])
    pg = m.take("pg", [P, NT, P])
    pgT = m.take("pgT", [P, 2, SEQ])
    sg = m.take("sg", [P, 2, 256])
    hid = m.take("hid", [P, 2, 512])
    oute = m.take("oute", [P, DM])
    slots = m.take("slots", [P, CAP])

    acc = ctx.enter_context(nc.psum_tensor("acc", [P, 2, 512], F32))
    pair = ctx.enter_context(nc.psum_tensor("pair", [P, 2, 512], F32))
    ys = ctx.enter_context(nc.psum_tensor("ys", [P, 2, 512], F32))
    misc = ctx.enter_context(nc.psum_tensor("misc", [P, 2, 512], F32))

    ring_in = [sem(f"ring_in{i}") for i in range(RING)]
    acc_full, acc_free = sem("acc_full"), sem("acc_free")
    s5_in, hy_in, tab_in, cw_in, row_in = (sem(n) for n in ("s5_in", "hy_in", "tab_in", "cw_in", "row_in"))
    act_link, dve_link = sem("act_link"), sem("dve_link")
    par_dve, par_act = sem("par_dve"), sem("par_act")
    turned, fracted, tabled, table_free = (sem(n) for n in ("turned", "fracted", "tabled", "table_free"))
    bu_full, bu_free, x_full, x_free = (sem(n) for n in ("bu_full", "bu_free", "x_full", "x_free"))
    ys_full, ys_free = sem("ys_full"), sem("ys_free")
    misc_full = sem("misc_full")
    misc_free = [sem("misc_free0"), sem("misc_free1")]
    mlp_arg, mlp_out, tap_pair, tap_sq, sq_used = (sem(n) for n in ("mlp_arg", "mlp_out", "tap_pair", "tap_sq", "sq_used"))
    sum_ready, root_ready, kre_raw, kre_ready = (sem(n) for n in ("sum_ready", "root_ready", "kre_raw", "kre_ready"))
    conv_done, tokens_out, spec_out, prod_out, z1_out = (sem(n) for n in ("conv_done", "tokens_out", "spec_out", "prod_out", "z1_out"))
    pads = sem("pads")

    act_link2 = sem("act_link2")
    dve_link2 = sem("dve_link2")
    dve_link3 = sem("dve_link3")
    dve_link4 = sem("dve_link4")
    dve_link5 = sem("dve_link5")
    rope_in = sem("rope_in")
    glu_in = sem("glu_in")
    rms_sum = sem("rms_sum")
    rms_root = sem("rms_root")
    rope_done = sem("rope_done")
    heads_full = sem("heads_full")
    heads_free = sem("heads_free")
    glu_z = sem("glu_z")
    glu_full = sem("glu_full")
    glu_gate = sem("glu_gate")
    glu_out = sem("glu_out")
    low_done = sem("low_done")
    exp_done = sem("exp_done")
    turn_full = sem("turn_full")
    turn_out = sem("turn_out")
    mix_full = sem("mix_full")
    score_full = sem("score_full")
    comb_arg = sem("comb_arg")
    comb_exp = sem("comb_exp")
    gate_out = sem("gate_out")
    side_full = sem("side_full")
    side_free = sem("side_free")
    yt_ready = sem("yt_ready")
    o_free = sem("o_free")
    ln_in = sem("ln_in")
    ln_var = sem("ln_var")
    ln_root = sem("ln_root")
    ln_out = sem("ln_out")
    ln_full = sem("ln_full")
    ln_free = sem("ln_free")
    stored = sem("stored")
    x_in = sem("x_in")
    consts = sem("consts")
    rw_in = sem("rw_in")
    route_full = sem("route_full")
    route_arg = sem("route_arg")
    route_exp = sem("route_exp")
    route_soft = sem("route_soft")
    route_turned = sem("route_turned")
    aff_out = sem("aff_out")
    pos_ready = sem("pos_ready")
    pos_turned = sem("pos_turned")
    pos_out = sem("pos_out")
    slots_in = sem("slots_in")
    gather_full = sem("gather_full")
    xs_out = sem("xs_out")
    pgT_full = sem("pgT_full")
    pgT_out = sem("pgT_out")
    spread_full = sem("spread_full")
    spread_free = sem("spread_free")
    hid_out = sem("hid_out")
    silu_out = sem("silu_out")
    oute_out = sem("oute_out")
    chosen = sem("chosen")
    far_in = [sem(f"far_in{i}") for i in range(2)]
    wb_in = [sem(f"wb_in{i}") for i in range(4)]
    slot_in = [sem(f"slot_in{i}") for i in range(6)]
    slot_used = [sem(f"slot_used{i}") for i in range(6)]

    C = A["const"]

    def chunk_arrived(eng, n):
        eng.wait_ge(ring_in[n % RING], 16 * (n // RING + 1))

    def ring_loads(sp, l, first, count):
        order = FIRST_CHUNKS + SECOND_CHUNKS + GATE_CHUNKS
        for n in range(first, first + count):
            if n >= RING:
                sp.wait_ge(acc_full, 2 * (n - RING + 1))
            if n < len(order):
                c = order[n]
                src = A["w_in"][l].rearrange("(c p) n -> p c n", p=P)[:, :, c * CW:(c + 1) * CW]
            else:
                c = n - len(order)
                src = A["w_out"][l].rearrange("(c p) n -> p c n", p=P)[:, :, c * CW:(c + 1) * CW]
            sp.dma_start(ring[:, n % RING], src).then_inc(ring_in[n % RING], 16)

    def project_features(pe, n, j):
        for c in range(ND):
            mm = pe.matmul(acc[:, j, :], ring[:, n % RING, c, j * P:(j + 1) * P], hT[:, c, :],
                           start=(c == 0), stop=(c == ND - 1))
        return mm

    def project_tokens(pe, n, j):
        for q in range(2):
            t = 2 * j + q
            for c in range(ND):
                mm = pe.matmul(acc[:, j, q * CW:(q + 1) * CW], hT[:, c, t * P:(t + 1) * P],
                               ring[:, n % RING, c, :], start=(c == 0), stop=(c == ND - 1))
        return mm

    def project(pe, n, by_tokens):
        chunk_arrived(pe, n)
        for j in range(2):
            if n >= 1:
                pe.wait_ge(acc_free, 2 * (n - 1) + j + 1)
            mm = (project_tokens if by_tokens else project_features)(pe, n, j)
            mm.then_inc(acc_full, 1)

    def s5_inputs(pe, n):
        jc, d, jj = n // 8, n % 8 // 4, n % 4
        rows = slice(32 * jj, 32 * jj + 32)
        if n >= 1:
            pe.wait_ge(bu_free, n)
        for part in range(2):
            u = uT[rows, jc, :] if d == 0 else uT[rows, jc, ::-1]
            mm = pe.matmul(pair[:, part, :], bT[rows, part, d, jc, :], u, start=True, stop=True)
        mm.then_inc(bu_full, 1)

    def s5_outputs(pe, n):
        jc, d, jj = n // 8, n % 8 // 4, n % 4
        rows = slice(32 * jj, 32 * jj + 32)
        pe.wait_ge(x_full, n + 1)
        if n == 8:
            pe.wait_ge(ys_free, 1)
        for part in range(2):
            mm = pe.matmul(ys[rows, d, :], cT[:, part, n, :], xx[:, part, :], start=(part == 0), stop=(part == 1))
        mm.then_inc(x_free, 1)

    def s5_turns(act, n):
        if n >= 1:
            act.wait_ge(tabled, n)
        act.activation(turn[:, :], iota[:, :], ACT.Copy, scale=par[:, 7, n:n + 1]).then_inc(turned, 1)

    def s5_trig(act, n, link):
        act.wait_ge(fracted, n + 1)
        if n >= 2:
            act.wait_ge(table_free, n - 1)
        link(act.activation(turn[:, :], frac[:, :], ACT.Abs))
        link(act.activation(trig[:, n % 2, 1, :], frac[:, :], ACT.Sin, scale=6.283185))
        act.activation(trig[:, n % 2, 0, :], turn[:, :], ACT.Sin, scale=-6.283185, bias=half_pi[:, :]).then_inc(tabled, 1)

    def s5_fractions(dve, n, link):
        dve.wait_ge(turned, n + 1)
        if n >= 1:
            dve.wait_ge(tabled, n)
        link(dve.tensor_scalar(frac[:, :], turn[:, :], ROUND, ROUND, ALU.add, ALU.subtract))
        dve.tensor_tensor(frac[:, :], turn[:, :], frac[:, :], ALU.subtract).then_inc(fracted, 1)

    def s5_scan(dve, n, link):
        cos = trig[:, n % 2, 0:1, :].to_broadcast([P, 2, SEQ])
        sin = trig[:, n % 2, 1:2, :].to_broadcast([P, 2, SEQ])
        dve.wait_ge(tabled, n + 1)
        dve.wait_ge(bu_full, n + 1)
        link.mark(dve.tensor_tensor(rot[:, 0], pair[:, :, :], cos, ALU.mult))
        link(dve.tensor_tensor(rot[:, 1], pair[:, :, :], sin, ALU.mult))
        dve.sem_inc(bu_free, 1)
        link.mark(dve.tensor_tensor(rot[:, 0, 0], rot[:, 0, 0], rot[:, 1, 1], ALU.add))
        link(dve.tensor_tensor(rot[:, 0, 1], rot[:, 0, 1], rot[:, 1, 0], ALU.subtract))
        for part in range(2):
            link.mark(dve.tensor_tensor_scan(zz[:, part, :], wide(par[:, 6, n:n + 1], SEQ), rot[:, 0, part],
                                             0.0, ALU.mult, ALU.add))
        link.hold()
        link.mark(dve.tensor_tensor(rot[:, 0], zz[:, :, :], cos, ALU.mult))
        link(dve.tensor_tensor(rot[:, 1], zz[:, :, :], sin, ALU.mult))
        dve.sem_inc(table_free, 1)
        if n >= 1:
            dve.wait_ge(x_free, n)
        dve.tensor_tensor(xx[:, 0], rot[:, 0, 0], rot[:, 1, 1], ALU.subtract)
        link(dve.tensor_tensor(xx[:, 1], rot[:, 0, 1], rot[:, 1, 0], ALU.add))
        dve.sem_inc(x_full, 1)

    def s5_collect(dve, jc, link):
        dve.wait_ge(x_free, 8 * jc + 8)
        link(dve.scalar_tensor_tensor(yc[:, jc, :], uT[:, jc, :], s5d[:, jc:jc + 1], ys[:, 0, :], ALU.mult, ALU.add))
        link(dve.tensor_tensor(yc[:, jc, :], yc[:, jc, :], ys[:, 1, ::-1], ALU.add))
        dve.sem_inc(ys_free, 1)

    def take_unit(pe, name):
        u = UNIT[name]
        if u >= 2:
            pe.wait_ge(misc_free[u % 2], u // 2)
        return misc[:, u % 2, :]

    def unit_full(eng, name):
        eng.wait_ge(misc_full, UNIT[name] + 1)
        return misc[:, UNIT[name] % 2, :]

    def unit_read(eng, link, ins, name):
        link(ins)
        eng.sem_inc(misc_free[UNIT[name] % 2], 1)

    def first_block(l):
        with nc.Block() as block:
            first_programs(l, block)

    def first_programs(l, block):
        @block.sync
        def _(sp):
            ring_loads(sp, l, 0, 2)
            sp.dma_start(par[:, 0:3, :], A["s5_par"][l]).then_inc(s5_in, 16)
            sp.dma_start(iota[:, :], C["c_iota"]).then_inc(s5_in, 16)
            sp.dma_start(frq[:, :], A["hy_cols"][l]).then_inc(hy_in, 16)
            sp.dma_start(zt[:, :], C["c_zt"]).then_inc(hy_in, 16)
            sp.dma_start(w1[:, :], A["hy_w1"][l]).then_inc(hy_in, 16)
            sp.dma_start(w2[:, :], A["hy_w2"][l]).then_inc(hy_in, 16)
            sp.dma_start(w3[:, :], A["hy_w3"][l]).then_inc(hy_in, 16)
            sp.dma_start(bT[:, :, :, :, :], A["s5_b"][l]).then_inc(s5_in, 16)
            sp.dma_start(cT[:, :, :, :], A["s5_c"][l]).then_inc(s5_in, 16)
            sp.dma_start(s5d[:, :], A["s5_dcol"][l]).then_inc(s5_in, 16)
            sp.dma_start(decay[:, :, :], C["c_decay"]).then_inc(tab_in, 16)
            sp.dma_start(hyb[:, :], A["hy_bias_row"][l].partition_broadcast(P)).then_inc(tab_in, 16)
            sp.dma_start(fc[:, :, :], C["c_fc"]).then_inc(tab_in, 16)
            sp.dma_start(fs[:, :, :], C["c_fs"]).then_inc(tab_in, 16)
            sp.dma_start(gs[:, :, :], C["c_gs"]).then_inc(tab_in, 16)
            sp.dma_start(cw[:, :, :], A["hy_conv"][l]).then_inc(cw_in, 16)
            ring_loads(sp, l, 2, N_FIRST - 2)

        @block.scalar
        def _(act):
            link = Link(act, act_link)
            act.wait_ge(s5_in, 80)
            act.activation(par[:, 3, :], par[:, 2, :], ACT.Exp).then_inc(par_act, 1)
            act.wait_ge(par_dve, 1)
            act.activation(par[:, 6, :], par[:, 4, :], ACT.Exp).then_inc(par_act, 1)
            act.wait_ge(par_dve, 2)
            link(act.activation(par[:, 10, :], par[:, 7, :], ACT.Abs))
            link(act.activation(par[:, 9, :], par[:, 7, :], ACT.Sin, scale=6.283185))
            act.activation(par[:, 10, :], par[:, 10, :], ACT.Sin, scale=-6.283185, bias=half_pi[:, :]).then_inc(par_act, 1)
            for step, i in FIRST_STEPS:
                if step == "project":
                    for j in range(2):
                        act.wait_ge(acc_full, 2 * i + j + 1)
                        if i == 0:
                            ins = act.activation(uT[:, j, :], acc[:, j, :], ACT.Copy)
                        elif i <= 2:
                            ins = act.activation(gtok[:, 2 * j:2 * j + 2, (i - 1) * CW:i * CW],
                                                 acc[:, j, :].rearrange("p (q n) -> p q n", q=2), ACT.Copy)
                        else:
                            if i == 3 and j == 0:
                                act.wait_ge(misc_full, UNIT[("nyquist",)] + 1)
                                act.wait_ge(kre_ready, 2)
                            ins = act.activation(hyT[:, 2 * (i - 3) + j, 1:SEQ + 1], acc[:, j, :], ACT.Copy)
                        ins.then_inc(acc_free, 1)
                elif step == "table":
                    s5_turns(act, i)
                    s5_trig(act, i, link)
                elif step == "mlp":
                    act.wait_ge(mlp_arg, i + 1)
                    f = (f1, f2)[i]
                    act.activation(f[:, :], sq[0:HD, 1, :], ACT.Sin, scale=6.283185).then_inc(mlp_out, 1)
                elif step == "filter":
                    act.wait_ge(tap_pair, i + 1)
                    if i >= 1:
                        act.wait_ge(sq_used, i)
                    link.mark(act.activation(sq[:, 0, :], fa[:, i, :], ACT.Square))
                    link(act.activation(sq[:, 1, :], fb[:, i, :], ACT.Square))
                    act.sem_inc(tap_sq, 1)
                elif step == "norm":
                    bank = unit_full(act, ("norm",))
                    unit_read(act, link, act.activation(rn[:, :], bank, ACT.Sqrt, scale=0.5), ("norm",))
                    act.sem_inc(root_ready, 1)
                elif step == "spectrum":
                    act.wait_ge(kre_raw, i + 1)
                    link(act.activation(kre[:, i, :], kre[:, i, :], ACT.Copy, scale=wf[:, i:i + 1]))
                    if i == 3:
                        act.sem_inc(kre_ready, 1)
                elif step == "tokens":
                    bank = unit_full(act, ("tokens", i))
                    dst = (z0, x1)[i // 2][:, 2 * (i % 2):2 * (i % 2) + 2, :]
                    ins = act.activation(dst, bank.rearrange("p (q n) -> p q n", q=2), ACT.Copy)
                    unit_read(act, link, ins, ("tokens", i))
                    act.sem_inc(tokens_out, 1)
                elif step == "forward":
                    for f in range(NT):
                        bank = unit_full(act, ("forward", i, f))
                        if i == 1 and f == 0:
                            act.wait_ge(prod_out, 1)
                        ins = act.activation(spec[:, f, :, :], bank.rearrange("p (q n) -> p q n", q=2), ACT.Copy)
                        unit_read(act, link, ins, ("forward", i, f))
                        act.sem_inc(spec_out, 1)

        @block.vector
        def _(dve):
            link = Link(dve, dve_link)
            pr = lambda i: par[:, i, :]
            dve.wait_ge(s5_in, 80)
            dve.wait_ge(par_act, 1)
            link.mark(dve.tensor_tensor(pr(4), pr(0), pr(3), ALU.mult))
            link(dve.tensor_tensor(pr(5), pr(1), pr(3), ALU.mult))
            dve.sem_inc(par_dve, 1)
            link(dve.tensor_scalar(pr(7), pr(5), 1.0 / TWO_PI, None, ALU.mult))
            link(dve.tensor_scalar(pr(8), pr(7), ROUND, ROUND, ALU.add, ALU.subtract))
            link(dve.tensor_tensor(pr(7), pr(7), pr(8), ALU.subtract))
            dve.sem_inc(par_dve, 1)
            dve.wait_ge(hy_in, 80)
            link.mark(dve.tensor_scalar(frw[:, 0:2], frq[:, 0:2], 1.0 / TWO_PI, None, ALU.mult))
            link(dve.tensor_tensor(frw[:, 2:4], frq[:, 0:2], frq[:, 2:4], ALU.mult))
            link(dve.tensor_scalar(frw[:, 2:4], frw[:, 2:4], 1.0 / TWO_PI, None, ALU.mult))
            dve.wait_ge(par_act, 3)
            link.mark(dve.tensor_tensor(pr(11), pr(6), pr(10), ALU.mult))
            link.mark(dve.tensor_tensor(pr(12), pr(6), pr(9), ALU.mult))
            link.mark(dve.tensor_tensor(pr(13), pr(0), pr(0), ALU.mult))
            link(dve.tensor_tensor(pr(8), pr(1), pr(1), ALU.mult))
            link.mark(dve.tensor_scalar(pr(11), pr(11), -1.0, None, ALU.add))
            link(dve.tensor_tensor(pr(13), pr(13), pr(8), ALU.add))
            link.mark(dve.reciprocal(pr(13), pr(13)))
            link.mark(dve.tensor_tensor(pr(14), pr(11), pr(0), ALU.mult))
            link.mark(dve.tensor_tensor(pr(8), pr(12), pr(1), ALU.mult))
            link.mark(dve.tensor_tensor(pr(15), pr(12), pr(0), ALU.mult))
            link(dve.tensor_tensor(pr(9), pr(11), pr(1), ALU.mult))
            link.mark(dve.tensor_tensor(pr(14), pr(14), pr(8), ALU.add))
            link(dve.tensor_tensor(pr(15), pr(15), pr(9), ALU.subtract))
            link.mark(dve.tensor_tensor(pr(14), pr(14), pr(13), ALU.mult))
            link(dve.tensor_tensor(pr(15), pr(15), pr(13), ALU.mult))
            cr, ci = cT[:, 0, :, :], cT[:, 1, :, :]
            fr = par[:, 14, :].unsqueeze(2).to_broadcast([P, S5_TILES, 32])
            fi = par[:, 15, :].unsqueeze(2).to_broadcast([P, S5_TILES, 32])
            r4 = [rot[:, a, b, :].rearrange("p (n c) -> p n c", c=32) for a in range(2) for b in range(2)]
            link.mark(dve.tensor_tensor(r4[0], cr, fr, ALU.mult))
            link.mark(dve.tensor_tensor(r4[1], ci, fi, ALU.mult))
            link.mark(dve.tensor_tensor(r4[2], cr, fi, ALU.mult))
            link(dve.tensor_tensor(r4[3], ci, fr, ALU.mult))
            link.mark(dve.tensor_tensor(cr, r4[0], r4[1], ALU.subtract))
            link(dve.scalar_tensor_tensor(ci, r4[2], -1.0, r4[3], ALU.mult, ALU.subtract))

            for step, i in FIRST_STEPS:
                if step == "table":
                    s5_fractions(dve, i, link)
                elif step == "states":
                    s5_scan(dve, i, link)
                elif step == "output":
                    if i == 7:
                        s5_collect(dve, 0, link)
                elif step == "mlp":
                    bank = unit_full(dve, ("mlp", i))[0:HD, :]
                    if i == 1:
                        dve.wait_ge(mlp_out, 1)
                    ins = dve.tensor_scalar(sq[0:HD, 0, :], bank, frw[:, i:i + 1], frw[:, 2 + i:3 + i], ALU.mult, ALU.add)
                    unit_read(dve, link, ins, ("mlp", i))
                    link(dve.tensor_scalar(sq[0:HD, 1, :], sq[0:HD, 0, :], ROUND, ROUND, ALU.add, ALU.subtract))
                    dve.tensor_tensor(sq[0:HD, 1, :], sq[0:HD, 0, :], sq[0:HD, 1, :], ALU.subtract).then_inc(mlp_arg, 1)
                elif step == "filter":
                    if i == 0:
                        dve.wait_ge(tab_in, 80)
                        dve.wait_ge(mlp_out, 2)
                    dec = decay[:, i:i + 1, :].to_broadcast([P, 2, HYW])
                    for d, dst in ((0, fa[:, i, :]), (1, bwd[:, :])):
                        bank = unit_full(dve, ("filter", i, d))
                        ins = dve.tensor_tensor(dst.rearrange("p (o n) -> p o n", o=2),
                                                bank.rearrange("p (o n) -> p o n", o=2), dec, ALU.mult)
                        unit_read(dve, link, ins, ("filter", i, d))
                    if i == 0:
                        link(dve.memset(bwd[0:1, :], 0.0))
                    link(dve.tensor_tensor(fb[:, i, :], fa[:, i, :], bwd[:, :], ALU.subtract))
                    link(dve.tensor_tensor(fa[:, i, :], fa[:, i, :], bwd[:, :], ALU.add))
                    dve.sem_inc(tap_pair, 1)
                    dve.wait_ge(tap_sq, i + 1)
                    if i == 0:
                        link(dve.tensor_tensor(nsum[:, :], sq[:, 0, :], sq[:, 1, :], ALU.add))
                    else:
                        link(dve.tensor_tensor(nsum[:, :], nsum[:, :], sq[:, 0, :], ALU.add))
                        link(dve.tensor_tensor(nsum[:, :], nsum[:, :], sq[:, 1, :], ALU.add))
                    dve.sem_inc(sq_used, 1)
                    if i == 3:
                        dve.sem_inc(sum_ready, 1)
                elif step == "norm":
                    dve.wait_ge(root_ready, 1)
                    link(dve.reciprocal(rn[:, :], rn[:, :]))
                elif step == "spectrum":
                    bank = unit_full(dve, ("spectrum", i, 0))
                    ins = dve.tensor_tensor(kre[:, i, :], bank, rn[:, :], ALU.mult)
                    unit_read(dve, link, ins, ("spectrum", i, 0))
                    dve.tensor_tensor(kre[:, i, :], kre[:, i, :], hyb[:, :], ALU.add).then_inc(kre_raw, 1)
                    bank = unit_full(dve, ("spectrum", i, 1))
                    ins = dve.scalar_tensor_tensor(kim[:, i, :], bank, wf[:, i:i + 1], rn[:, :], ALU.mult, ALU.mult)
                    unit_read(dve, link, ins, ("spectrum", i, 1))
                    if i == 0:
                        link(dve.memset(kim[0:1, 0, :], 0.0))
                elif step == "nyquist":
                    bank = unit_full(dve, ("nyquist",))[0:1, :]
                    dve.wait_ge(kre_ready, 1)
                    link(dve.tensor_copy(knyq[:, :], kre[:, 0, :]))
                    ins = dve.tensor_tensor(knyq[0:1, :], bank, rn[0:1, :], ALU.mult)
                    unit_read(dve, link, ins, ("nyquist",))
                    link(dve.tensor_tensor(knyq[0:1, :], knyq[0:1, :], hyb[0:1, :], ALU.add))
                    link(dve.tensor_scalar(knyq[0:1, :], knyq[0:1, :], 1.0 / (2 * SEQ), None, ALU.mult))
                    dve.wait_ge(misc_full, UNIT[("nyquist",)] + 1)
                    link.mark(dve.memset(hyT[:, :, 0:1], 0.0))
                    link(dve.memset(hyT[:, :, SEQ + 1:SEQ + 2], 0.0))
                    dve.sem_inc(kre_ready, 1)
                elif step == "conv":
                    if i == 0:
                        dve.wait_ge(cw_in, 16)
                    dve.wait_ge(acc_free, 2 * (i + 3) + 2)
                    dst = [u01[:, 2 * i + j, :] if i < 2 else ya[:, j, :] for j in range(2)]
                    q = [2 * i, 2 * i + 1]
                    for j in range(2):
                        link.mark(dve.tensor_scalar(dst[j], hyT[:, q[j], 0:SEQ], cw[:, q[j], 0:1], cw[:, q[j], 3:4], ALU.mult, ALU.add))
                    link.hold()
                    for k in (1, 2):
                        for j in range(2):
                            link.mark(dve.scalar_tensor_tensor(dst[j], hyT[:, q[j], k:k + SEQ], cw[:, q[j], k:k + 1], dst[j], ALU.mult, ALU.add))
                        link.hold()
                    dve.sem_inc(conv_done, 1)
                elif step == "product":
                    dve.wait_ge(spec_out, NT * (i + 1))
                    if i == 1:
                        dve.wait_ge(misc_full, UNIT[("back", 0, 1)] + 1)
                    else:
                        dve.wait_ge(tokens_out, 4)
                    o = slice(i * HYW, (i + 1) * HYW)
                    ure, uim = spec[:, :, 0, :], spec[:, :, 1, :]
                    link.mark(dve.tensor_tensor(prod[:, 0], ure, kre[:, :, o], ALU.mult))
                    link.mark(dve.tensor_tensor(prod[:, 1], uim, kim[:, :, o], ALU.mult))
                    link.mark(dve.tensor_tensor(prod[:, 2], ure, kim[:, :, o], ALU.mult))
                    link.mark(dve.tensor_tensor(prod[:, 3, 1:4], uim[:, 1:4], kre[:, 1:4, o], ALU.mult))
                    link(dve.tensor_tensor(prod[:, 3, 0], uim[:, 0], knyq[:, o], ALU.mult))
                    link.mark(dve.tensor_tensor(prod[:, 0], prod[:, 0], prod[:, 1], ALU.subtract))
                    link(dve.tensor_tensor(prod[:, 2], prod[:, 2], prod[:, 3], ALU.add))
                    dve.sem_inc(prod_out, 1)
                elif step == "back":
                    for c in range(2):
                        bank = unit_full(dve, ("back", i, c))
                        if i == 0:
                            ins = dve.tensor_tensor(z0[:, 2 * c:2 * c + 2, :], bank.rearrange("p (q n) -> p q n", q=2),
                                                    x1[:, 2 * c:2 * c + 2, :], ALU.mult)
                        else:
                            ins = dve.tensor_tensor(ya[:, c, :], bank, ya[:, c, :], ALU.mult)
                        unit_read(dve, link, ins, ("back", i, c))
                        dve.sem_inc(z1_out, 1)

        @block.tensor
        def _(pe):
            def close(mm):
                mm.then_inc(misc_full, 1)

            for step, i in FIRST_STEPS:
                if step == "project":
                    project(pe, i, by_tokens=i in (1, 2))
                elif step == "states":
                    if i == 0:
                        pe.wait_ge(s5_in, 80)
                        pe.wait_ge(acc_free, 2)
                    s5_inputs(pe, i)
                elif step == "output":
                    s5_outputs(pe, i)
                elif step == "mlp":
                    bank = take_unit(pe, ("mlp", i))
                    if i == 0:
                        pe.wait_ge(hy_in, 80)
                        close(pe.matmul(bank[0:HD, :], w1[:, :], zt[:, :], start=True, stop=True))
                    else:
                        pe.wait_ge(mlp_out, 1)
                        close(pe.matmul(bank[0:HD, :], w2[:, :], f1[:, :], start=True, stop=True))
                elif step == "filter":
                    if i == 0:
                        pe.wait_ge(mlp_out, 2)
                    for d in range(2):
                        bank = take_unit(pe, ("filter", i, d))
                        close(pe.matmul(bank, f2[:, i * P:(i + 1) * P], w3[:, d * 512:(d + 1) * 512], start=True, stop=True))
                elif step == "norm":
                    bank = take_unit(pe, ("norm",))
                    pe.wait_ge(sum_ready, 1)
                    close(pe.matmul(bank, ones[:, :], nsum[:, :], start=True, stop=True))
                elif step == "spectrum":
                    for part, (table, taps) in enumerate(((fc, fa), (fs, fb))):
                        bank = take_unit(pe, ("spectrum", i, part))
                        if i == 0 and part == 0:
                            pe.wait_ge(tab_in, 80)
                            pe.wait_ge(tap_pair, 4)
                        for t in range(NT):
                            mm = pe.matmul(bank, table[:, t, i * P:(i + 1) * P], taps[:, t, :], start=(t == 0), stop=(t == NT - 1))
                        close(mm)
                elif step == "nyquist":
                    bank = take_unit(pe, ("nyquist",))
                    for t in range(NT):
                        mm = pe.matmul(bank[0:1, :], fs[:, t, 0:1], fa[:, t, :], start=(t == 0), stop=(t == NT - 1))
                    close(mm)
                elif step == "tokens":
                    bank = take_unit(pe, ("tokens", i))
                    if i == 0:
                        pe.wait_ge(conv_done, 2)
                    for q in range(2):
                        t = 2 * (i % 2) + q
                        for c in range(2):
                            mm = pe.transpose(bank[:, q * HYW + c * P:q * HYW + (c + 1) * P],
                                              u01[:, 2 * (i // 2) + c, t * P:(t + 1) * P], ident[:, :])
                    close(mm)
                elif step == "forward":
                    for f in range(NT):
                        bank = take_unit(pe, ("forward", i, f))
                        if f == 0:
                            if i == 0:
                                pe.wait_ge(tokens_out, 4)
                            else:
                                pe.wait_ge(z1_out, 2)
                        for part, table in enumerate((fc, fs)):
                            for t in range(NT):
                                mm = pe.matmul(bank[:, part * HYW:(part + 1) * HYW], table[:, t, f * P:(f + 1) * P],
                                               z0[:, t, :], start=(t == 0), stop=(t == NT - 1))
                        close(mm)
                elif step == "back":
                    for c in range(2):
                        bank = take_unit(pe, ("back", i, c))
                        if c == 0:
                            pe.wait_ge(prod_out, i + 1)
                        if i == 0:
                            for q in range(2):
                                t = 2 * c + q
                                for f in range(NT):
                                    pe.matmul(bank[:, q * HYW:(q + 1) * HYW], fc[:, f, t * P:(t + 1) * P], prod[:, 0, f, :],
                                              start=(f == 0), stop=False)
                                    mm = pe.matmul(bank[:, q * HYW:(q + 1) * HYW], gs[:, f, t * P:(t + 1) * P], prod[:, 2, f, :],
                                                   start=False, stop=(f == NT - 1))
                        else:
                            for f in range(NT):
                                pe.matmul(bank, prod[:, 0, f, c * P:(c + 1) * P], fc[:, f, :], start=(f == 0), stop=False)
                                mm = pe.matmul(bank, prod[:, 2, f, c * P:(c + 1) * P], gs[:, f, :], start=False, stop=(f == NT - 1))
                        close(mm)

    def second_block(l):
        with nc.Block() as block:
            @block.sync
            def _(sp):
                ring_loads(sp, l, N_FIRST, 2)
                sp.dma_start(gnorm[:, :], A["gq_norm_row"][l].partition_broadcast(P)).then_inc(rope_in, 16)
                sp.dma_start(rcos[:, :, :], C["c_cos"]).then_inc(rope_in, 16)
                sp.dma_start(rsin[:, :, :], C["c_sin"]).then_inc(rope_in, 16)
                sp.dma_start(gluw[:, :, :], A["s5_glu_w"][l].rearrange("(k p) n -> p k n", p=P)).then_inc(glu_in, 16)
                sp.dma_start(glub[:, :], A["s5_glu_bcol"][l]).then_inc(glu_in, 16)
                ring_loads(sp, l, N_FIRST + 2, N_SECOND - 2)

            @block.scalar
            def _(act):
                link = Link(act, act_link2)
                for step, i in SECOND_STEPS:
                    if step == "project":
                        for j in range(2):
                            act.wait_ge(acc_full, 2 * i + j + 1)
                            c = i - N_FIRST
                            if c < 3:
                                ins = act.activation(qd[:, 2 * c + j, :], acc[:, j, :], ACT.Copy, scale=-(HD ** -0.5))
                            elif c < 6:
                                ins = act.activation(kd[:, 2 * (c - 3) + j, :], acc[:, j, :], ACT.Copy)
                            else:
                                ins = act.activation(vd[:, 2 * j:2 * j + 2, (c - 6) * CW:(c - 5) * CW],
                                                     acc[:, j, :].rearrange("p (q n) -> p q n", q=2), ACT.Copy)
                            ins.then_inc(acc_free, 1)
                    elif step == "table":
                        s5_turns(act, i)
                        s5_trig(act, i, link)
                    elif step == "rms":
                        act.wait_ge(rms_sum, 1)
                        act.activation(stat[:, :], stat[:, :], ACT.Sqrt, scale=1.0 / HD, bias=eps_rms[:, :]).then_inc(rms_root, 1)
                    elif step == "heads":
                        act.wait_ge(heads_full, i + 1)
                        dst = qg[:, i, :] if i < 2 else kg[:, :]
                        act.activation(dst, misc[:, i % 2, :], ACT.Copy, scale=-(HD ** -0.5) if i < 2 else 1.0).then_inc(heads_free, 1)
                    elif step == "gelu":
                        act.wait_ge(ys_free, 2)
                        act.activation(zg[:, :, :], yc[:, :, :], ACT.Gelu_apprx_tanh).then_inc(glu_z, 1)
                    elif step == "glu":
                        act.wait_ge(glu_full, i + 1)
                        if i == 0:
                            act.wait_ge(glu_in, 32)
                        act.activation(zs[:, i, :], misc[:, (i + 1) % 2, :], ACT.Sigmoid, bias=glub[:, i:i + 1]).then_inc(glu_gate, 1)

            @block.vector
            def _(dve):
                link = Link(dve, dve_link2)
                for step, i in SECOND_STEPS:
                    if step == "table":
                        s5_fractions(dve, i, link)
                    elif step == "states":
                        s5_scan(dve, i, link)
                    elif step == "output":
                        if i == S5_TILES - 1:
                            s5_collect(dve, 1, link)
                    elif step == "rms":
                        qk = gtok[:, :, 0:6 * HD]
                        link(dve.tensor_tensor(ra[:, :, :], qk, qk, ALU.mult))
                        link(dve.tensor_reduce(stat[:, :], ra[:, :, :].rearrange("p t (h d) -> p (t h) d", d=HD), AX.X, ALU.add))
                        dve.sem_inc(rms_sum, 1)
                    elif step == "rope":
                        dve.wait_ge(rms_root, 1)
                        link(dve.reciprocal(stat[:, :], stat[:, :]))
                        for t in range(NT):
                            link.mark(dve.tensor_tensor(
                                ra[:, t, :].rearrange("p (h d) -> p h d", d=HD), gtok[:, t, 0:6 * HD].rearrange("p (h d) -> p h d", d=HD),
                                stat[:, 6 * t:6 * t + 6].unsqueeze(2).to_broadcast([P, 6, HD]), ALU.mult))
                        link.hold()
                        dve.wait_ge(rope_in, 48)
                        link(dve.tensor_tensor(ra[:, :, :], ra[:, :, :], gnorm[:, :].unsqueeze(1).to_broadcast([P, NT, 6 * HD]), ALU.mult))
                        for t in range(NT):
                            x = ra[:, t, :].rearrange("p (h f b c) -> p h f b c", f=2, b=2, c=16)
                            y = rb[:, t, :].rearrange("p (h f b c) -> p h f b c", f=2, b=2, c=16)
                            s = rsin[:, t, :].rearrange("p (f b c) -> p f b c", f=2, b=2)
                            for b in range(2):
                                link.mark(dve.tensor_tensor(y[:, :, :, b, :], x[:, :, :, 1 - b, :],
                                                            s[:, :, b, :].unsqueeze(1).to_broadcast([P, 6, 2, 16]), ALU.mult))
                        link.hold()
                        for t in range(NT):
                            link.mark(dve.tensor_tensor(ra[:, t, :].rearrange("p (h d) -> p h d", d=HD),
                                                        ra[:, t, :].rearrange("p (h d) -> p h d", d=HD),
                                                        rcos[:, t:t + 1, :].to_broadcast([P, 6, HD]), ALU.mult))
                        link.hold()
                        for t in range(NT):
                            turn_heads = lambda a, s: a[:, t, 0:4 * HD].rearrange(s, a=2, b=2)
                            link.mark(dve.tensor_tensor(turn_heads(rp, "p (b a d) -> p a b d"), turn_heads(ra, "p (a b d) -> p a b d"),
                                                        turn_heads(rb, "p (a b d) -> p a b d"), ALU.add))
                        link(dve.tensor_tensor(rp[:, :, 4 * HD:], ra[:, :, 4 * HD:], rb[:, :, 4 * HD:], ALU.add))
                        dve.sem_inc(rope_done, 1)
                    elif step == "glu":
                        dve.wait_ge(glu_gate, i + 1)
                        dve.tensor_tensor(yc[:, i, :], zg[:, i, :], zs[:, i, :], ALU.mult).then_inc(glu_out, 1)

            @block.tensor
            def _(pe):
                for step, i in SECOND_STEPS:
                    if step == "project":
                        project(pe, i, by_tokens=i - N_FIRST >= 6)
                    elif step == "states":
                        s5_inputs(pe, i)
                    elif step == "output":
                        s5_outputs(pe, i)
                    elif step == "heads":
                        if i == 0:
                            pe.wait_ge(rope_done, 1)
                        if i == 2:
                            pe.wait_ge(heads_free, 1)
                        for t in range(NT):
                            mm = pe.transpose(misc[:, i % 2, t * P:(t + 1) * P], rp[:, t, i * P:(i + 1) * P], ident[:, :])
                        mm.then_inc(heads_full, 1)
                    elif step == "glu":
                        if i == 0:
                            pe.wait_ge(glu_z, 1)
                            pe.wait_ge(glu_in, 32)
                            pe.wait_ge(heads_free, 3)
                        for k in range(2):
                            mm = pe.matmul(misc[:, (i + 1) % 2, :], gluw[:, k, i * P:(i + 1) * P], zg[:, k, :], start=(k == 0), stop=(k == 1))
                        mm.then_inc(glu_full, 1)

    def attend_block(l):
        with nc.Block() as block:
            @block.sync
            def _(sp):
                def gate_loads(n):
                    ring_loads(sp, l, N_FIRST + N_SECOND + n, 1)
                    if n >= 4:
                        sp.wait_ge(side_full, SIDE[("gate", 2 * (n - 4) + 1)] + 1)
                    br, c = BRANCHES[n // 4], n % 4
                    src = A["w_branch"][l, br].rearrange("(k p) n -> p k n", p=P)[:, :, c * CW:(c + 1) * CW]
                    sp.dma_start(wb[:, n % 4], src).then_inc(wb_in[n % 4], 16)

                def far_load(n):
                    if n >= 2:
                        sp.wait_ge(low_done, 4 * (n - 1))
                    sp.dma_start(far[:, n % 2, :], C["c_far"][HEADS[n]]).then_inc(far_in[n % 2], 16)

                far_load(0)
                for n in range(RING):
                    gate_loads(n)
                far_load(1)
                for n in range(DILH + GQH):
                    if n in GATES_AT:
                        gate_loads(GATES_AT[n] + RING)
                    if n + 2 < DILH:
                        far_load(n + 2)
                for n in range(len(GATES_AT) + RING, N_GATE):
                    gate_loads(n)

            @block.scalar
            def _(act):
                for step, i in ATTEND_STEPS:
                    if step == "scores":
                        act.wait_ge(low_done, i + 1)
                        if i >= 2:
                            act.wait_ge(turn_full, i - 1)
                        src = sm[:, i % 2, :] if i // 4 < DILH else pair[:, i % 2, :]
                        act.activation(pr[:, i % 2, :], src, ACT.Exp, scale=-1.0, bias=low[:, i:i + 1],
                                       accum_out=ssum[:, i:i + 1]).then_inc(exp_done, 1)
                    elif step == "turn":
                        act.wait_ge(turn_full, i + 1)
                        if i >= 2:
                            act.wait_ge(mix_full, i - 1)
                        act.activation(pT[:, i % 2, :], ys[:, i % 2, :], ACT.Copy).then_inc(turn_out, 1)
                    elif step == "combine":
                        act.wait_ge(comb_arg, i + 1)
                        act.activation(ew[:, :], ew[:, :], ACT.Exp).then_inc(comb_exp, 1)
                    elif step == "gate":
                        n, j = N_FIRST + N_SECOND + i // 2, i % 2
                        act.wait_ge(acc_full, 2 * n + j + 1)
                        if i >= 2:
                            act.wait_ge(gate_out, i - 1)
                        act.activation(th[:, j, :], acc[:, j, :], ACT.Tanh, scale=0.5).then_inc(acc_free, 1)

            @block.vector
            def _(dve):
                link = Link(dve, dve_link3)
                for step, i in ATTEND_STEPS:
                    if step == "scores":
                        b = i % 4
                        dve.wait_ge(score_full, i + 1)
                        if i // 4 < DILH:
                            n = i // 4
                            dve.wait_ge(far_in[n % 2], 16 * (n // 2 + 1))
                            if i >= 2:
                                dve.wait_ge(exp_done, i - 1)
                            dve.tensor_tensor_reduce(out=sm[:, i % 2, :], in0=pair[:, i % 2, :],
                                                     in1=far[:, n % 2, 384 - P * b:384 - P * b + SEQ], scale=1.0, scalar=3e38,
                                                     op0=ALU.add, op1=ALU.min, accum_out=low[:, i:i + 1]).then_inc(low_done, 1)
                        else:
                            dve.tensor_reduce(low[:, i:i + 1], pair[:, i % 2, :], AX.X, ALU.min).then_inc(low_done, 1)
                    elif step == "mix" and i % 4 == 3:
                        n = i // 4
                        dve.wait_ge(mix_full, i + 1)
                        bank = misc[:, 0, 0:256].rearrange("p (b d) -> p b d", d=HD)
                        if n < DILH:
                            link(dve.tensor_copy(obuf[:, n % 3], bank))
                        else:
                            h = n - DILH
                            dve.wait_ge(exp_done, i + 1)
                            link(dve.reciprocal(rs[:, :], ssum[:, 4 * n:4 * n + 4]))
                            link(dve.tensor_tensor(yt[:, :, h * HD:(h + 1) * HD], bank, rs[:, :].unsqueeze(2).to_broadcast([P, 4, HD]), ALU.mult))
                        dve.sem_inc(o_free, 1)
                    elif step == "combine":
                        lo = low[:, 12 * i:12 * i + 12]
                        dve.wait_ge(exp_done, 12 * i + 12)
                        link(dve.tensor_tensor(rs[:, :], lo[:, 0:4], lo[:, 4:8], ALU.min))
                        link(dve.tensor_tensor(rs[:, :], rs[:, :], lo[:, 8:12], ALU.min))
                        v3 = lambda a: a.rearrange("p (g b) -> p g b", g=3)
                        link(dve.tensor_tensor(v3(ew[:, :]), rs[:, :].unsqueeze(1).to_broadcast([P, 3, 4]), v3(lo), ALU.subtract))
                        dve.sem_inc(comb_arg, 1)
                        dve.wait_ge(comb_exp, i + 1)
                        link(dve.tensor_tensor(es[:, :], ew[:, :], ssum[:, 12 * i:12 * i + 12], ALU.mult))
                        link(dve.tensor_tensor(rs[:, :], es[:, 0:4], es[:, 4:8], ALU.add))
                        link(dve.tensor_tensor(rs[:, :], rs[:, :], es[:, 8:12], ALU.add))
                        link(dve.reciprocal(rs[:, :], rs[:, :]))
                        link(dve.tensor_tensor(v3(es[:, :]), v3(ew[:, :]), rs[:, :].unsqueeze(1).to_broadcast([P, 3, 4]), ALU.mult))
                        flat = obuf[:, :, :, :].rearrange("p g b d -> p (g b) d")
                        link(dve.tensor_tensor(flat, flat, es[:, :].unsqueeze(2).to_broadcast([P, 12, HD]), ALU.mult))
                        link(dve.tensor_tensor(obuf[:, 0], obuf[:, 0], obuf[:, 1], ALU.add))
                        link(dve.tensor_tensor(yt[:, :, i * HD:(i + 1) * HD], obuf[:, 0], obuf[:, 2], ALU.add))
                    elif step == "features":
                        br, c = i
                        if c == 0:
                            dve.sem_inc(yt_ready, 1)
                        dve.wait_ge(side_full, SIDE[("features", i)] + 1)
                        link(dve.tensor_copy(yT[br][:, c, :], misc[:, 1, :]))
                        dve.sem_inc(side_free, 1)
                    elif step == "gate":
                        br, d = i // 8, i % 8
                        dve.wait_ge(acc_free, 2 * (N_FIRST + N_SECOND) + i + 1)
                        dve.wait_ge(side_full, SIDE[("gate", i)] + 1)
                        if br == 0:
                            link(dve.scalar_tensor_tensor(merged[:, d, :], th[:, i % 2, :], 1.0, misc[:, 1, :], ALU.add, ALU.mult))
                            dve.sem_inc(side_free, 1)
                        else:
                            link(dve.scalar_tensor_tensor(term[:, :], th[:, i % 2, :], 1.0, misc[:, 1, :], ALU.add, ALU.mult))
                            dve.sem_inc(side_free, 1)
                            link(dve.tensor_tensor(merged[:, d, :], merged[:, d, :], term[:, :], ALU.add))
                        if br == 3:
                            link(dve.tensor_scalar(merged[:, d, :], merged[:, d, :], 0.5, None, ALU.mult))
                        dve.sem_inc(gate_out, 1)

            @block.tensor
            def _(pe):
                for step, i in ATTEND_STEPS:
                    if step == "scores":
                        n, b = i // 4, i % 4
                        if i >= 2:
                            pe.wait_ge(low_done if (i - 2) // 4 < DILH else exp_done, i - 1)
                        if n < DILH:
                            h = HEADS[n]
                            rows = slice(64 * (h % 2), 64 * (h % 2) + 64)
                            q, k = qd[rows, h // 2, :], kd[rows, h // 2, :]
                        else:
                            h = n - DILH
                            rows = slice(64 * (h // 2), 64 * (h // 2) + 64)
                            q, k = qg[rows, h % 2, :], kg[rows, :]
                        pe.matmul(pair[:, i % 2, :], q[:, b * P:(b + 1) * P], k, start=True, stop=True).then_inc(score_full, 1)
                    elif step == "turn":
                        pe.wait_ge(exp_done, i + 1)
                        if i >= 2:
                            pe.wait_ge(turn_out, i - 1)
                        for kc in range(NT):
                            mm = pe.transpose(ys[:, i % 2, kc * P:(kc + 1) * P], pr[:, i % 2, kc * P:(kc + 1) * P], ident[:, :])
                        mm.then_inc(turn_full, 1)
                    elif step == "mix":
                        n, b = i // 4, i % 4
                        pe.wait_ge(turn_out, i + 1)
                        if b == 0 and n >= 1:
                            pe.wait_ge(o_free, n)
                        if n < DILH:
                            h = HEADS[n]
                            v = vd[:, :, h * HD:(h + 1) * HD]
                        else:
                            g = (n - DILH) // 2
                            v = gtok[:, :, 6 * HD + g * HD:6 * HD + (g + 1) * HD]
                        o = b * HD
                        for kc in range(NT):
                            mm = pe.matmul(misc[:, 0, o:o + HD], pT[:, i % 2, kc * P:(kc + 1) * P], v[:, kc, :], start=(kc == 0), stop=(kc == NT - 1))
                        mm.then_inc(mix_full, 1)
                    elif step == "features":
                        br, c = i
                        if c == 0:
                            pe.wait_ge(yt_ready, 1 if br == 1 else 2)
                        if SIDE[("features", i)] >= 1:
                            pe.wait_ge(side_free, SIDE[("features", i)])
                        for b in range(NT):
                            mm = pe.transpose(misc[:, 1, b * P:(b + 1) * P], yt[:, b, c * P:(c + 1) * P], ident[:, :])
                        mm.then_inc(side_full, 1)
                    elif step == "gate":
                        n, j = N_FIRST + N_SECOND + i // 2, i % 2
                        if j == 0:
                            chunk_arrived(pe, n)
                        pe.wait_ge(acc_free, 2 * (n - 1) + j + 1)
                        project_features(pe, n, j).then_inc(acc_full, 1)
                        br = BRANCHES[i // 8]
                        if j == 0:
                            pe.wait_ge(wb_in[i // 2 % 4], 16 * (i // 8 + 1))
                        if SIDE[("gate", i)] >= 1:
                            pe.wait_ge(side_free, SIDE[("gate", i)])
                        for k in range(2):
                            mm = pe.matmul(misc[:, 1, :], wb[:, i // 2 % 4, k, j * P:(j + 1) * P], yT[br][:, k, :], start=(k == 0), stop=(k == 1))
                        mm.then_inc(side_full, 1)

    def norm_loads(eng, g, b):
        eng.dma_start(lng[:, :], g.partition_broadcast(P)).then_inc(ln_in, 16)
        eng.dma_start(lnb[:, :], b.partition_broadcast(P)).then_inc(ln_in, 16)

    def norm_vector(dve, link, x):
        for t in range(NT):
            for s in range(2):
                link.mark(dve.bn_stats(lnst[:, t, 6 * s:6 * s + 6], x[:, t, s * 512:(s + 1) * 512]))
        link.hold()
        for t in range(NT):
            link.mark(dve.bn_aggr(lnmv[:, t, :], lnst[:, t, :]))
        link.hold()
        dve.sem_inc(ln_var, 1)
        dve.wait_ge(ln_root, 1)
        link(dve.reciprocal(lnrs[:, :], lnrs[:, :]))
        dve.wait_ge(ln_in, 32)
        for t in range(NT):
            link(dve.tensor_scalar(h[:, t, :], x[:, t, :], lnmv[:, t, 0:1], lnrs[:, t:t + 1], ALU.subtract, ALU.mult))
            link(dve.tensor_tensor(h[:, t, :], h[:, t, :], lng[:, :], ALU.mult))
            link(dve.tensor_tensor(h[:, t, :], h[:, t, :], lnb[:, :], ALU.add))
            dve.sem_inc(ln_out, 1)

    def norm_scalar(act):
        act.wait_ge(ln_var, 1)
        act.activation(lnrs[:, :], lnmv[:, :, 1], ACT.Sqrt, bias=eps_ln[:, :]).then_inc(ln_root, 1)
        for u in range(2 * NT):
            t, s = u // 2, u % 2
            act.wait_ge(ln_full, u + 1)
            act.activation(hT[:, 4 * s:4 * s + 4, t * P:(t + 1) * P], misc[:, u % 2, :].rearrange("p (c n) -> p c n", c=4),
                           ACT.Copy).then_inc(ln_free, 1)

    def norm_tensor(pe):
        for u in range(2 * NT):
            t, s = u // 2, u % 2
            if s == 0:
                pe.wait_ge(ln_out, t + 1)
            if u >= 2:
                pe.wait_ge(ln_free, u - 1)
            for c in range(4):
                mm = pe.transpose(misc[:, u % 2, c * P:(c + 1) * P], h[:, t, (4 * s + c) * P:(4 * s + c + 1) * P], ident[:, :])
            mm.then_inc(ln_full, 1)

    def norm_store(sp):
        for t in range(NT):
            sp.wait_ge(ln_out, t + 1)
            sp.dma_start(out[t * P:(t + 1) * P, :], h[:, t, :]).then_inc(stored, 16)
        sp.wait_ge(stored, 16 * NT)

    def start_block():
        with nc.Block() as block:
            @block.sync
            def _(sp):
                sp.dma_start(h[:, :, :], A["x"].rearrange("(t p) n -> p t n", p=P)).then_inc(x_in, 16)
                sp.dma_start(ident[:, :], C["c_ident"]).then_inc(x_in, 16)
                sp.dma_start(wf[:, :], C["c_wf"]).then_inc(x_in, 16)
                norm_loads(sp, A["ln_in_g"], A["ln_in_b"])
                norm_store(sp)

            @block.gpsimd
            def _(pool):
                pool.memset(ones[:, :], 1.0)
                pool.memset(half_pi[:, :], math.pi / 2)
                pool.memset(eps_ln[:, :], LN_EPS).then_inc(consts, 1)
                pool.memset(eps_rms[:, :], RMS_EPS)

            @block.scalar
            def _(act):
                act.wait_ge(consts, 1)
                norm_scalar(act)

            @block.vector
            def _(dve):
                link = Link(dve, dve_link4)
                dve.wait_ge(x_in, 48)
                norm_vector(dve, link, h)

            @block.tensor
            def _(pe):
                pe.wait_ge(x_in, 48)
                norm_tensor(pe)

    def finish_block(l):
        with nc.Block() as block:
            @block.sync
            def _(sp):
                sp.dma_start(h[:, :, :], out.rearrange("(t p) n -> p t n", p=P)).then_inc(x_in, 16)
                ring_loads(sp, l, N_FIRST + N_SECOND + N_GATE, OUT_CHUNKS)
                norm_loads(sp, A["ln1_g"][l], A["ln1_b"][l])
                sp.dma_start(rw[:, :, :], A["router_w"][l].rearrange("(c p) e -> p c e", p=P)).then_inc(rw_in, 16)

            @block.scalar
            def _(act):
                norm_scalar(act)
                act.wait_ge(route_arg, 1)
                act.activation(aff[:, :, :], aff[:, :, :], ACT.Exp).then_inc(route_exp, 1)
                act.wait_ge(route_turned, 1)
                act.activation(affT[:, :], pair[0:NE, 1, :], ACT.Copy).then_inc(aff_out, 1)
                act.wait_ge(pos_turned, 1)
                act.activation(posT[:, :, :], pair[:, 0, 0:NT * NE].rearrange("p (t e) -> p t e", e=NE), ACT.Copy).then_inc(pos_out, 1)

            @block.vector
            def _(dve):
                link = Link(dve, dve_link4)
                dve.wait_ge(x_in, 16)
                for c in range(OUT_CHUNKS):
                    n = N_FIRST + N_SECOND + N_GATE + c
                    for j in range(2):
                        dve.wait_ge(acc_full, 2 * n + j + 1)
                        hs = h[:, 2 * j:2 * j + 2, c * CW:(c + 1) * CW]
                        link.mark(dve.scalar_tensor_tensor(hs, hs, ALPHA, acc[:, j, :].rearrange("p (q n) -> p q n", q=2), ALU.mult, ALU.add))
                        link.hold()
                        dve.sem_inc(acc_free, 1)
                norm_vector(dve, link, h)
                dve.wait_ge(route_full, 1)
                lg = pair[:, 0, 0:NT * NE].rearrange("p (t e) -> p t e", e=NE)
                link(dve.tensor_reduce(rmax[:, :], lg, AX.X, ALU.max))
                link(dve.tensor_tensor(aff[:, :, :], lg, rmax[:, :].unsqueeze(2).to_broadcast([P, NT, NE]), ALU.subtract))
                dve.sem_inc(route_arg, 1)
                dve.wait_ge(route_exp, 1)
                link(dve.tensor_reduce(rmax[:, :], aff[:, :, :], AX.X, ALU.add))
                link(dve.reciprocal(rmax[:, :], rmax[:, :]))
                link(dve.tensor_tensor(aff[:, :, :], aff[:, :, :], rmax[:, :].unsqueeze(2).to_broadcast([P, NT, NE]), ALU.mult))
                dve.sem_inc(route_soft, 1)
                dve.wait_ge(aff_out, 1)
                link(dve.tensor_copy(work[:, :], affT[:, :]))
                for r in range(CAP // 8):
                    link(dve.max(top8[:, :], work[:, :]))
                    if r < CAP // 8 - 1:
                        link(dve.match_replace(work[:, :], top8[:, :], work[:, :], -1.0))
                kth = top8[:, 7:8]
                link(dve.tensor_scalar(gt[:, :], affT[:, :], kth, None, ALU.is_gt))
                link(dve.tensor_scalar(eq[:, :], affT[:, :], kth, None, ALU.is_equal))
                link(dve.tensor_reduce(left[:, :], gt[:, :], AX.X, ALU.add))
                link(dve.tensor_scalar(left[:, :], left[:, :], -1.0, float(CAP), ALU.mult, ALU.add))
                link(dve.tensor_tensor_scan(work[:, :], wide(ones[0:NE, 0:1], SEQ), eq[:, :], 0.0, ALU.mult, ALU.add))
                link(dve.tensor_scalar(work[:, :], work[:, :], left[:, 0:1], None, ALU.is_le))
                link(dve.tensor_tensor(eq[:, :], eq[:, :], work[:, :], ALU.mult))
                link(dve.tensor_tensor(gt[:, :], gt[:, :], eq[:, :], ALU.add))
                link(dve.tensor_tensor_scan(work[:, :], wide(ones[0:NE, 0:1], SEQ), gt[:, :], 0.0, ALU.mult, ALU.add))
                link(dve.tensor_tensor(work[:, :], work[:, :], gt[:, :], ALU.mult))
                link(dve.tensor_scalar(work[:, :], work[:, :], -1.0, None, ALU.add))
                dve.sem_inc(pos_ready, 1)

            @block.tensor
            def _(pe):
                for c in range(OUT_CHUNKS):
                    n = N_FIRST + N_SECOND + N_GATE + c
                    chunk_arrived(pe, n)
                    for j in range(2):
                        pe.wait_ge(acc_free, 2 * (n - 1) + j + 1)
                        for q in range(2):
                            t = 2 * j + q
                            for k in range(ND):
                                mm = pe.matmul(acc[:, j, q * CW:(q + 1) * CW], merged[:, k, t * P:(t + 1) * P],
                                               ring[:, n % RING, k, :], start=(k == 0), stop=(k == ND - 1))
                        mm.then_inc(acc_full, 1)
                norm_tensor(pe)
                pe.wait_ge(ln_free, 2 * NT)
                pe.wait_ge(rw_in, 16)
                for t in range(NT):
                    for k in range(ND):
                        mm = pe.matmul(pair[:, 0, t * NE:(t + 1) * NE], hT[:, k, t * P:(t + 1) * P], rw[:, k, :], start=(k == 0), stop=(k == ND - 1))
                mm.then_inc(route_full, 1)
                pe.wait_ge(route_soft, 1)
                for t in range(NT):
                    mm = pe.transpose(pair[0:NE, 1, t * P:(t + 1) * P], aff[:, t, :], ident[:, :])
                mm.then_inc(route_turned, 1)
                pe.wait_ge(pos_ready, 1)
                for t in range(NT):
                    mm = pe.transpose(pair[:, 0, t * NE:(t + 1) * NE], work[:, t * P:(t + 1) * P], ident[0:NE, 0:NE])
                mm.then_inc(pos_turned, 1)

    def experts_block(l):
        PAIRS = NE // 2
        with nc.Block() as block:
            @block.sync
            def _(sp):
                sp.dma_start(slots[:, :], C["c_iota"][:, 0:CAP]).then_inc(slots_in, 16)
                for v in range(NE):
                    for s in range(2):
                        for k, w in ((2 * s, "exp_w_gate"), (2 * s + 1, "exp_w_up")):
                            if v >= 1:
                                sp.wait_ge(slot_used[k], v)
                            sp.dma_start(ering[:, k], A[w][l, v].rearrange("(c p) f -> p c f", p=P)[:, :, s * 512:(s + 1) * 512]).then_inc(slot_in[k], 16)
                    for s in range(2):
                        k = 4 + s
                        if v >= 1:
                            sp.wait_ge(slot_used[k], v)
                        sp.dma_start(ering[:, k].rearrange("p c n -> p (c n)").rearrange("p (c n) -> p c n", c=4),
                                     A["exp_w_down"][l, v].rearrange("(c p) n -> p c n", p=P)[:, 4 * s:4 * s + 4, :]).then_inc(slot_in[k], 16)

            @block.scalar
            def _(act):
                for i in range(PAIRS + 1):
                    if i < PAIRS:
                        act.wait_ge(gather_full, i + 1)
                        if i >= 1:
                            act.wait_ge(slot_used[3], 2 * i)
                        act.activation(xs[:, :, :], misc[:, :, :].rearrange("p b (c n) -> p (b c) n", n=P), ACT.Copy).then_inc(xs_out, 1)
                        act.wait_ge(pgT_full, i + 1)
                        if i >= 2:
                            act.wait_ge(spread_full, 8 * (i - 1))
                        act.activation(pgT[:, i % 2, :], misc[:, 0, :], ACT.Copy).then_inc(pgT_out, 1)
                        for q in range(2):
                            v = 2 * i + q
                            for s in range(2):
                                act.wait_ge(slot_used[2 * s + 1], v + 1)
                                if 2 * v + s >= 2:
                                    act.wait_ge(hid_out, 2 * v + s - 1)
                                act.activation(sg[:, s, :], acc[:, s, 0:256], ACT.Silu).then_inc(silu_out, 1)
                        act.wait_ge(slot_used[5], 2 * i + 2)
                        if i >= 1:
                            act.wait_ge(spread_full, 8 * i)
                        act.activation(oute[:, :], ys[:, :, :].rearrange("p a n -> p (a n)"), ACT.Copy).then_inc(oute_out, 1)

            @block.vector
            def _(dve):
                link = Link(dve, dve_link4)
                dve.wait_ge(slots_in, 16)
                for t in range(NT):
                    link.mark(dve.tensor_scalar(accx[:, t, :], h[:, t, :], ALPHA, None, ALU.mult))
                link.hold()

                def choose(i):
                    if i >= 1:
                        dve.wait_ge(pgT_full, i)
                    e = slice(2 * i, 2 * i + 2)
                    pp4 = pp[:, :, :].rearrange("p t (e n) -> p t e n", e=2)
                    pg4 = pg[:, :, :].rearrange("p t (e n) -> p t e n", e=2)
                    for t in range(NT):
                        link.mark(dve.tensor_tensor(pp4[:, t], slots[:, :].unsqueeze(1).to_broadcast([P, 2, CAP]),
                                                    posT[:, t, e].unsqueeze(2).to_broadcast([P, 2, CAP]), ALU.is_equal))
                    link.hold()
                    for t in range(NT):
                        link.mark(dve.tensor_tensor(pg4[:, t], pp4[:, t], aff[:, t, e].unsqueeze(2).to_broadcast([P, 2, CAP]), ALU.mult))
                    link.hold()
                    dve.sem_inc(chosen, 1)

                choose(0)
                for i in range(PAIRS):
                    if i + 1 < PAIRS:
                        choose(i + 1)
                    for q in range(2):
                        v = 2 * i + q
                        for s in range(2):
                            dve.wait_ge(silu_out, 2 * v + s + 1)
                            if v >= 2:
                                dve.wait_ge(slot_used[5], v - 1)
                            dve.tensor_tensor(hid[:, v % 2, 256 * s:256 * s + 256], sg[:, s, :], acc[:, s, 256:512],
                                              ALU.mult).then_inc(hid_out, 1)
                    for u in range(8):
                        t, n = u // 2, u % 2
                        dve.wait_ge(spread_full, 8 * i + u + 1)
                        at = accx[:, t, n * 512:(n + 1) * 512]
                        dve.tensor_tensor(at, at, pair[:, u % 2, :], ALU.add).then_inc(spread_free, 1)
                dve.wait_ge(spread_free, 8 * PAIRS)

            @block.tensor
            def _(pe):
                def gather(i):
                    pe.wait_ge(chosen, i + 1)
                    if i >= 1:
                        pe.wait_ge(pgT_out, i)
                    for c in range(ND):
                        for t in range(NT):
                            mm = pe.matmul(misc[:, c // 4, (c % 4) * P:(c % 4 + 1) * P], h[:, t, c * P:(c + 1) * P], pp[:, t, :],
                                           start=(t == 0), stop=(t == NT - 1))
                    mm.then_inc(gather_full, 1)
                    pe.wait_ge(xs_out, i + 1)
                    for t in range(NT):
                        mm = pe.transpose(misc[:, 0, t * P:(t + 1) * P], pg[:, t, :], ident[:, :])
                    mm.then_inc(pgT_full, 1)

                def spread(i):
                    pe.wait_ge(oute_out, i + 1)
                    pe.wait_ge(pgT_out, i + 1)
                    for u in range(8):
                        t, n = u // 2, u % 2
                        if 8 * i + u >= 2:
                            pe.wait_ge(spread_free, 8 * i + u - 1)
                        mm = pe.matmul(pair[:, u % 2, :], pgT[:, i % 2, t * P:(t + 1) * P], oute[:, n * 512:(n + 1) * 512], start=True, stop=True)
                        mm.then_inc(spread_full, 1)

                gather(0)
                for i in range(PAIRS):
                    for q in range(2):
                        v = 2 * i + q
                        for s in range(2):
                            if 2 * v + s >= 2:
                                pe.wait_ge(hid_out, 2 * v + s - 1)
                            for m_, k in ((0, 2 * s), (1, 2 * s + 1)):
                                pe.wait_ge(slot_in[k], 16 * (v + 1))
                                for f in range(4):
                                    o = 256 * m_ + CAP * f
                                    for c in range(ND):
                                        mm = pe.matmul(acc[:, s, o:o + CAP], ering[:, k, c, f * P:(f + 1) * P], xs[:, c, q * CAP:(q + 1) * CAP],
                                                       start=(c == 0), stop=(c == ND - 1))
                                mm.then_inc(slot_used[k], 1)
                        if q == 0 and i >= 1:
                            spread(i - 1)
                        rows = slice(CAP * q, CAP * q + CAP)
                        if q == 0 and i >= 1:
                            pe.wait_ge(oute_out, i)
                        for s in range(2):
                            pe.wait_ge(hid_out, 2 * v + s + 1)
                            pe.wait_ge(slot_in[4 + s], 16 * (v + 1))
                            wd = ering[:, 4 + s].rearrange("p c n -> p (c n)").rearrange("p (c n) -> p c n", c=4)
                            for c in range(4):
                                f = 4 * s + c
                                for n in range(2):
                                    mm = pe.matmul(ys[rows, n, :], hid[:, v % 2, f * CAP:(f + 1) * CAP], wd[:, c, n * 512:(n + 1) * 512],
                                                   start=(f == 0), stop=(f == NF - 1))
                            mm.then_inc(slot_used[4 + s], 1)
                    if i + 1 < PAIRS:
                        gather(i + 1)
                spread(PAIRS - 1)

    def close_block(l):
        with nc.Block() as block:
            @block.sync
            def _(sp):
                norm_loads(sp, A["ln2_g"][l], A["ln2_b"][l])
                norm_store(sp)

            @block.scalar
            def _(act):
                norm_scalar(act)

            @block.vector
            def _(dve):
                link = Link(dve, dve_link5)
                norm_vector(dve, link, accx)

            @block.tensor
            def _(pe):
                norm_tensor(pe)

    def clear_block(which):
        with nc.Block() as block:
            @block.gpsimd
            def _(pool):
                for s in which:
                    pool.sem_clear(s)

    ln_sems = [ln_in, ln_var, ln_root, ln_out, ln_full, ln_free, stored, x_in, dve_link4]
    start_block()
    clear_block(ln_sems + [consts])
    with nc.Fori(0, depth) as l:
        first_block(l)
        if stage >= 2: second_block(l)
        if stage >= 3: attend_block(l)
        if stage >= 4: finish_block(l)
        if stage >= 5:
            clear_block(ln_sems)
            experts_block(l)
            clear_block(ln_sems)
            close_block(l)
            clear_block(sems)
    return


def kernel(**inputs):
    import numpy as _np
    import concourse.bacc as _bacc
    from concourse import mybir as _mybir
    from concourse.bass_utils import run_bass_kernel_spmd as _run

    nc = _bacc.Bacc("TRN2", target_bir_lowering=False, num_devices=1)
    arrays, A = {}, {}

    def give(name, a):
        a = _np.ascontiguousarray(a)
        arrays[f"in_{name}_dram"] = a
        return nc.dram_tensor(f"in_{name}_dram", a.shape, _mybir.dt.from_np(a.dtype), kind="ExternalInput").ap()

    for name, a in lay_out(inputs).items():
        A[name] = give(name, a)
    A["const"] = {name: give(name, a) for name, a in constants().items()}
    out = nc.dram_tensor("out_0_dram", (1, SEQ, DM), F32, kind="ExternalOutput").ap()
    build(nc, A, out[0])
    r = _run(nc, [arrays], core_ids=[0])
    return r.results[0]["out_0_dram"]
```

```python
import math
from contextlib import ExitStack

import numpy as np

import concourse.bass as bass
from concourse import mybir

F32 = mybir.dt.float32
ALU = mybir.AluOpType
ACT = mybir.ActivationFunctionType
AX = mybir.AxisListType

P = 128
SEQ, DM, DEPTH = 512, 1024, 2
NT = SEQ // P
ND = DM // P
HD = 64
HYW, S5W = 256, 256
DILH, GROUPS, SLOTS = 12, 3, 4
GQH, GKV = 4, 2
NE, CAP, FF = 16, 64, 1024
NF = FF // P
CW = 256
ALPHA = (2 * DEPTH) ** 0.25
LN_EPS, RMS_EPS = 1e-5, 1e-6
ROUND = 12582912.0
TWO_PI = 2.0 * math.pi
BIG = 1e30

HY0, DQ0, DK0, DV0, S50, GQ0, GK0, GATE0 = 0, 3, 6, 9, 12, 13, 14, 15
FIRST_CHUNKS = [S50, GQ0, GK0, HY0, HY0 + 1, HY0 + 2]
SECOND_CHUNKS = list(range(DQ0, S50))
BRANCHES = [0, 2, 1, 3]
GATE_CHUNKS = [GATE0 + 4 * b + q for b in BRANCHES for q in range(4)]
RING = 4
OUT_CHUNKS = DM // CW
N_FIRST, N_SECOND, N_GATE = len(FIRST_CHUNKS), len(SECOND_CHUNKS), len(GATE_CHUNKS)
PER_LAYER = N_FIRST + N_SECOND + N_GATE + OUT_CHUNKS
FARW = SEQ + NT
S5_TILES = 16


def constants():
    t = np.arange(SEQ)
    ang = 2.0 * np.pi * ((t[:, None] * t[None, :]) % (2 * SEQ)) / (2 * SEQ)
    sign = np.where(t % 2 == 0, 1.0, -1.0)
    fc = np.cos(ang)
    fs = -np.sin(ang)
    fs[:, 0] = sign
    gs = -np.sin(ang)
    gs[0, :] = sign
    wf = np.full((SEQ,), 2.0 / (2 * SEQ))
    wf[0] = 1.0 / (2 * SEQ)
    tl = lambda a: np.ascontiguousarray(a.reshape(NT, P, -1).transpose(1, 0, 2)).astype(np.float32)
    lin = np.linspace(0.0, 1.0, SEQ, dtype=np.float32)
    bands = np.linspace(1e-4, 15, 16, dtype=np.float32)
    w = (2.0 * math.pi * np.arange(SEQ, dtype=np.float32) / SEQ).astype(np.float32)
    fw = (bands[None, :] * w[:, None]).astype(np.float32)
    z = np.concatenate([lin[:, None], np.cos(fw), -np.sin(fw)], axis=-1).astype(np.float32)
    deltas = np.abs(np.linspace(math.log(1e-2) / 1.5, math.log(1e-2) / 0.3, HYW, dtype=np.float32))
    decay = np.exp(-lin[:, None] * deltas[None, :]).astype(np.float32)
    inv = 10000.0 ** (-np.arange(0, 32, 2, dtype=np.float32) / 32)
    rows, cols = (t // 64).astype(np.float32), (t % 64).astype(np.float32)
    cs, sn = [], []
    for pos in (rows, cols):
        a = pos[:, None] * inv[None, :]
        cs += [np.cos(a), np.cos(a)]
        sn += [-np.sin(a), np.sin(a)]
    far = np.zeros((DILH, P, FARW), np.float32)
    for g, (win, dil) in enumerate(((128, 1), (512, 4), (2048, 16))):
        col = np.arange(FARW)[None, :]
        off = (col - (NT - 1) if g == 0 else NT * col) - NT * np.arange(P)[:, None]
        ok = (np.abs(off) <= win // 2) & (off % dil == 0)
        for s in range(SLOTS):
            h = g * SLOTS + s
            far[h] = np.where(ok, 2.0 ** (-8.0 * (h + 1) / DILH) * np.abs(off), BIG)
    return {
        "c_fc": tl(fc), "c_fs": tl(fs), "c_gs": tl(gs),
        "c_wf": np.ascontiguousarray(wf.reshape(NT, P).T).astype(np.float32),
        "c_zt": np.ascontiguousarray(z.T), "c_decay": tl(decay),
        "c_cos": tl(np.concatenate(cs, -1)), "c_sin": tl(np.concatenate(sn, -1)),
        "c_far": far, "c_ident": np.eye(P, dtype=np.float32),
        "c_iota": np.broadcast_to(t.astype(np.float32), (P, SEQ)).copy(),
    }


class Link:

    def __init__(self, eng, sem):
        self.eng, self.sem, self.n = eng, sem, 0

    def __call__(self, ins):
        self.mark(ins)
        self.hold()

    def mark(self, ins):
        ins.then_inc(self.sem, 1)
        self.n += 1

    def hold(self):
        self.eng.wait_ge(self.sem, self.n)


def wide(ap, n):
    return ap.to_broadcast([ap.shape[0], n])


FIRST_STEPS = (
    [("project", 0), ("table", 0), ("mlp", 0), ("project", 1), ("mlp", 1), ("states", 0), ("table", 1)]
    + [("filter", 0), ("filter", 1), ("filter", 2), ("filter", 3), ("project", 2), ("output", 0)]
    + [("norm", 0), ("states", 1), ("table", 2), ("spectrum", 0), ("spectrum", 1), ("spectrum", 2)]
    + [("spectrum", 3), ("nyquist", 0), ("output", 1), ("project", 3), ("states", 2), ("table", 3)]
    + [("project", 4), ("conv", 0), ("output", 2), ("states", 3), ("table", 4)]
    + [("project", 5), ("conv", 1), ("output", 3), ("states", 4), ("table", 5), ("conv", 2)]
    + [("tokens", 0), ("tokens", 1), ("tokens", 2), ("tokens", 3), ("output", 4)]
    + [("states", 5), ("table", 6), ("forward", 0), ("product", 0), ("output", 5)]
    + [("states", 6), ("table", 7), ("back", 0), ("output", 6), ("forward", 1), ("product", 1)]
    + [("states", 7), ("output", 7), ("back", 1)]
)
UNIT_NAMES = []
for _step, _i in FIRST_STEPS:
    UNIT_NAMES += {
        "mlp": [("mlp", _i)],
        "filter": [("filter", _i, 0), ("filter", _i, 1)],
        "norm": [("norm",)],
        "spectrum": [("spectrum", _i, 0), ("spectrum", _i, 1)],
        "nyquist": [("nyquist",)],
        "tokens": [("tokens", _i)],
        "forward": [("forward", _i, f) for f in range(NT)],
        "back": [("back", _i, c) for c in range(2)],
    }.get(_step, [])
UNIT = {name: n for n, name in enumerate(UNIT_NAMES)}
assert len(UNIT) == len(UNIT_NAMES)


SECOND_STEPS = [("table", 8), ("rms", 0)]
for _n in range(8, 16):
    SECOND_STEPS += [("project", N_FIRST + _n - 8), ("states", _n)] + ([("table", _n + 1)] if _n < 15 else [])
    if _n >= 9:
        SECOND_STEPS += [("output", _n - 1)]
    if _n == 9:
        SECOND_STEPS += [("rope", 0)]
    if _n == 11:
        SECOND_STEPS += [("heads", 0), ("heads", 1), ("heads", 2)]
SECOND_STEPS += [("project", N_FIRST + 8), ("output", 15), ("gelu", 0), ("glu", 0), ("glu", 1)]

HEADS = [g * SLOTS + s for s in range(SLOTS) for g in range(GROUPS)]
UNITS = []
for _n in range(DILH + GQH):
    UNITS += [(_n, None)] if _n < DILH and HEADS[_n] >= SLOTS else [(_n, _b) for _b in range(NT)]
N_UNITS = len(UNITS)
UNITS_BY = [sum(1 for _u in UNITS if _u[0] <= _n) for _n in range(DILH + GQH)]
N_DIL = UNITS_BY[DILH - 1]
GATE_UNITS = [_w for _w in range(N_DIL - 2) if _w % 3] + list(range(N_DIL + 1, N_UNITS, 2))
ATTEND_STEPS = []
for _w in range(N_UNITS + 2):
    if _w < N_UNITS:
        ATTEND_STEPS.append(("scores", _w))
    if _w in GATE_UNITS:
        ATTEND_STEPS.append(("gate", GATE_UNITS.index(_w)))
    if 1 <= _w <= N_UNITS:
        ATTEND_STEPS.append(("turn", _w - 1))
    if _w >= 2:
        ATTEND_STEPS.append(("mix", _w - 2))
        _n = UNITS[_w - 2][0]
        if _n < DILH and _n % GROUPS == GROUPS - 1:
            ATTEND_STEPS.append(("combine", _n // GROUPS))
    if _w == N_DIL + 4:
        ATTEND_STEPS += [("features", (1, 0)), ("features", (1, 1))]
_gates = len(GATE_UNITS)
ATTEND_STEPS += [("gate", _i) for _i in range(_gates, 24)] + [("features", (3, 0)), ("features", (3, 1))]
ATTEND_STEPS += [("gate", _i) for _i in range(24, 32)]
SIDE = {s: n for n, s in enumerate(x for x in ATTEND_STEPS if x[0] in ("gate", "features"))}
assert len(SIDE) == 36


def lay_out(inputs):
    g = {k: np.asarray(v) for k, v in inputs.items()}
    L = DEPTH
    d = {k: g[k] for k in ("ln_in_g", "ln_in_b", "w_in", "hy_w1", "hy_w2", "hy_w3", "w_branch", "w_out",
                           "ln1_g", "ln1_b", "router_w", "exp_w_gate", "exp_w_up", "exp_w_down", "ln2_g", "ln2_b")}
    d["x"] = g["x"][0]
    cols = lambda a: a.reshape(L, -1, P).transpose(0, 2, 1)
    d["hy_cols"] = np.stack([g["hy_freq"][:, 0], g["hy_freq"][:, 1], g["hy_b1"], g["hy_b2"]], -1)
    d["hy_conv"] = np.stack([cols(g["hy_conv_w"][:, 0]), cols(g["hy_conv_w"][:, 1]), cols(g["hy_conv_w"][:, 2]),
                             cols(g["hy_conv_b"])], -1)
    d["hy_bias_row"] = g["hy_bias"].reshape(L, 512)
    d["s5_dcol"] = cols(g["s5_d"])
    d["s5_glu_bcol"] = cols(g["s5_glu_b"])
    d["s5_glu_w"] = g["s5_glu_w"]
    tiles = lambda a: a.reshape(L, 2, 2, 4, P).transpose(0, 4, 2, 1, 3).reshape(L, P, S5_TILES)
    dt = np.repeat(g["s5_log_dt"][..., None], HD, axis=-1)
    d["s5_par"] = np.stack([tiles(g["s5_lam_re"]), tiles(g["s5_lam_im"]), tiles(dt)], 2).transpose(0, 1, 2, 3)
    bt = np.zeros((L, S5_TILES, P, 2, P), np.float32)
    ct = np.zeros((L, P, 2, S5_TILES, 32), np.float32)
    for part, (b, c) in enumerate(((g["s5_b_re"], g["s5_c_re"]), (g["s5_b_im"], g["s5_c_im"]))):
        for n in range(S5_TILES):
            jc, dr, jj = n // 8, n % 8 // 4, n % 4
            for q in range(2):
                grp = 8 * jc + 2 * jj + q
                bt[:, n, 32 * jj + 16 * q:32 * jj + 16 * q + 16, part, 64 * q:64 * q + 64] = b[:, dr, grp].transpose(0, 2, 1)
                ct[:, 64 * q:64 * q + 64, part, n, 16 * q:16 * q + 16] = c[:, dr, grp].transpose(0, 2, 1)
    d["s5_b"], d["s5_c"] = bt, ct
    d["gq_norm_row"] = np.concatenate([g["gqa_q_norm"]] * GQH + [g["gqa_k_norm"]] * GKV, -1)
    return d


def build(nc, A, out, stage=99, depth=DEPTH):
    ctx = ExitStack()
    sems = []

    def sem(name):
        s = ctx.enter_context(nc.semaphore(name))
        sems.append(s)
        return s

    K = 1024

    class Area:

        def __init__(self, base, end):
            self.base, self.end = base, end

        def take(self, name, shape):
            n = (4 * int(np.prod(shape[1:])) + 31) // 32 * 32
            a = nc.alloc_sbuf_tensor_at(name, shape, F32, offset=FLOOR + self.base)
            self.base += n
            assert self.base <= self.end, (name, self.base, self.end)
            return a

    FLOOR = (nc.sbuf_base + 31) // 32 * 32
    END = 207 * K
    assert FLOOR + END <= nc.sbuf_usable_end
    m = Area(0, END)
    hT = m.take("hT", [P, ND, SEQ])
    ring = m.take("ring", [P, RING, ND, CW])
    ident = m.take("ident", [P, P])
    y_at = m.base
    ya, yb, yc, yd = (m.take(n, [P, 2, SEQ]) for n in ("ya", "yb", "yc", "yd"))
    yT = [ya, yb, yc, yd]
    ones = m.take("ones", [P, P])
    wf = m.take("wf", [P, NT])
    half_pi = m.take("half_pi", [P, 1])
    eps_ln = m.take("eps_ln", [P, 1])
    eps_rms = m.take("eps_rms", [P, 1])
    posT = m.take("posT", [P, NT, NE])
    aff = m.take("aff", [P, NT, NE])
    frq = m.take("frq", [HD, 4])
    frw = m.take("frw", [HD, 4])
    stat = m.take("stat", [P, 24])
    cw = m.take("cw", [P, 6, 4])
    base = m.base

    gtok = m.take("gtok", [P, NT, 512])
    iota = m.take("iota", [P, SEQ])
    uT = m.take("uT", [P, 2, SEQ])
    bT = m.take("bT", [P, 2, 2, P])
    cT = m.take("cT", [P, 2, S5_TILES, 32])
    par = m.take("par", [P, 16, S5_TILES])
    s5d = m.take("s5d", [P, 2])
    turn = m.take("turn", [P, SEQ])
    frac = m.take("frac", [P, SEQ])
    trig = m.take("trig", [P, 2, 2, SEQ])
    rot = m.take("rot", [P, 2, 2, SEQ])
    zz = m.take("zz", [P, 2, SEQ])
    xx = m.take("xx", [P, 2, SEQ])
    s5_end = m.base
    fc = m.take("fc", [P, NT, SEQ])
    fs = m.take("fs", [P, NT, SEQ])
    gs = m.take("gs", [P, NT, SEQ])
    kre = m.take("kre", [P, NT, 512])
    kim = m.take("kim", [P, NT, 512])
    knyq = m.take("knyq", [P, 512])
    z0_at = m.base
    z0 = m.take("z0", [P, NT, HYW])
    x1 = m.take("x1", [P, NT, HYW])
    share = m.base
    m = Area(z0_at, share)
    zt = m.take("zt", [33, SEQ])
    w3 = m.take("w3", [P, 1024])
    f1 = m.take("f1", [HD, SEQ])
    m = Area(share, END)
    fa = m.take("fa", [P, NT, 512])
    fb = m.take("fb", [P, NT, 512])
    decay = m.take("decay", [P, NT, HYW])
    bwd = m.take("bwd", [P, 512])
    sq = m.take("sq", [P, 2, 512])
    nsum = m.take("nsum", [P, 512])
    f2 = m.take("f2", [P, SEQ])
    w1 = m.take("w1", [33, HD])
    w2 = m.take("w2", [HD, HD])
    hyb = m.take("hyb", [P, 512])
    rn = m.take("rn", [P, 512])
    m = Area(share, END)
    hyT = m.take("hyT", [P, 6, SEQ + 2])
    u01 = m.take("u01", [P, 4, SEQ])
    spec = m.take("spec", [P, NT, 2, HYW])
    prod = nc.alloc_sbuf_tensor_at("prod", [P, 4, NT, HYW], F32, offset=FLOOR + share)
    assert m.base <= END


    m = Area(s5_end, END)
    qd = m.take("qd", [P, DILH, SEQ])
    kd = m.take("kd", [P, 6, SEQ])
    vd = m.take("vd", [P, NT, DILH * HD])
    qg = m.take("qg", [P, GQH, SEQ])
    kg = m.take("kg", [P, SEQ])
    attend_at = m.base
    gnorm = m.take("gnorm", [P, 6 * HD])
    rcos = m.take("rcos", [P, NT, HD])
    rsin = m.take("rsin", [P, NT, HD])
    gluw = m.take("gluw", [P, 2, S5W])
    glub = m.take("glub", [P, 2])
    ra_at = m.base
    ra = m.take("ra", [P, NT, 6 * HD])
    rb = m.take("rb", [P, NT, 6 * HD])
    rp = m.take("rp", [P, NT, 6 * HD])
    m = Area(ra_at, END)
    zg = m.take("zg", [P, 2, SEQ])
    zs = m.take("zs", [P, 2, SEQ])
    m = Area(base + 16 * K, s5_end)
    merged = m.take("merged", [P, ND, SEQ])
    far = m.take("far", [P, 2, FARW])
    sm = m.take("sm", [P, 2, SEQ])
    pr = m.take("pr", [P, 2, SEQ])
    m = Area(attend_at, END)
    pT = m.take("pT", [P, 2, SEQ])
    wb = m.take("wb", [P, 4, 2, CW])
    th = m.take("th", [P, 2, SEQ])
    term = m.take("term", [P, SEQ])
    yt = m.take("yt", [P, NT, 256])
    obuf = m.take("obuf", [P, 3, 4, HD])
    low = m.take("low", [P, 64])
    ssum = m.take("ssum", [P, 64])
    ew = m.take("ew", [P, 12])
    es = m.take("es", [P, 12])
    rs = m.take("rs", [P, 4])
    m = Area(base, END)
    h = m.take("h", [P, NT, DM])
    assert m.base == base + 16 * K
    accx = m.take("accx", [P, NT, DM])
    ering = m.take("ering", [P, 6, 4, DM])
    lng = m.take("lng", [P, DM])
    lnb = m.take("lnb", [P, DM])
    lnst = m.take("lnst", [P, NT, 12])
    lnmv = m.take("lnmv", [P, NT, 2])
    lnrs = m.take("lnrs", [P, NT])
    rmax = m.take("rmax", [P, NT])
    rw = m.take("rw", [P, ND, NE])
    m = Area(y_at, y_at + 16 * K)
    affT = m.take("affT", [NE, SEQ])
    work = m.take("work", [NE, SEQ])
    gt = m.take("gt", [NE, SEQ])
    eq = m.take("eq", [NE, SEQ])
    top8 = m.take("top8", [NE, 8])
    left = m.take("left", [NE, 1])
    m = Area(16 * K, 48 * K)
    xs = m.take("xs", [P, ND, P])
    pp = m.take("pp", [P, NT, P])
    pg = m.take("pg", [P, NT, P])
    pgT = m.take("pgT", [P, 2, SEQ])
    sg = m.take("sg", [P, 512])
    hid = m.take("hid", [P, 512])
    hidT = m.take("hidT", [P, 2, 512])
    oute = m.take("oute", [P, DM])
    slots = m.take("slots", [P, CAP])

    acc = ctx.enter_context(nc.psum_tensor("acc", [P, 2, 512], F32))
    pair = ctx.enter_context(nc.psum_tensor("pair", [P, 2, 512], F32))
    ys = ctx.enter_context(nc.psum_tensor("ys", [P, 2, 512], F32))
    misc = ctx.enter_context(nc.psum_tensor("misc", [P, 2, 512], F32))

    ring_in = [sem(f"ring_in{i}") for i in range(RING)]
    acc_full, acc_free = sem("acc_full"), sem("acc_free")
    s5_in, hy_in, tab_in, cw_in, row_in = (sem(n) for n in ("s5_in", "hy_in", "tab_in", "cw_in", "row_in"))
    act_link, dve_link = sem("act_link"), sem("dve_link")
    par_dve, par_act = sem("par_dve"), sem("par_act")
    turned, fracted, tabled, table_free = (sem(n) for n in ("turned", "fracted", "tabled", "table_free"))
    bu_full, bu_free, x_full, x_free = (sem(n) for n in ("bu_full", "bu_free", "x_full", "x_free"))
    ys_full, ys_free = sem("ys_full"), sem("ys_free")
    misc_full = sem("misc_full")
    misc_free = [sem("misc_free0"), sem("misc_free1")]
    mlp_arg, mlp_out, tap_pair, tap_sq, sq_used = (sem(n) for n in ("mlp_arg", "mlp_out", "tap_pair", "tap_sq", "sq_used"))
    sum_ready, root_ready, kre_raw, kre_ready = (sem(n) for n in ("sum_ready", "root_ready", "kre_raw", "kre_ready"))
    conv_done, tokens_out, spec_out, prod_out, z1_out = (sem(n) for n in ("conv_done", "tokens_out", "spec_out", "prod_out", "z1_out"))
    pads = sem("pads")

    act_link2 = sem("act_link2")
    dve_link2 = sem("dve_link2")
    dve_link3 = sem("dve_link3")
    dve_link4 = sem("dve_link4")
    dve_link5 = sem("dve_link5")
    rope_in = sem("rope_in")
    queries_clear = sem("queries_clear")
    glu_in = sem("glu_in")
    rms_sum = sem("rms_sum")
    rms_root = sem("rms_root")
    rope_done = sem("rope_done")
    heads_full = sem("heads_full")
    heads_free = sem("heads_free")
    glu_z = sem("glu_z")
    glu_full = sem("glu_full")
    glu_gate = sem("glu_gate")
    glu_out = sem("glu_out")
    low_done = sem("low_done")
    exp_done = sem("exp_done")
    turn_full = sem("turn_full")
    turn_out = sem("turn_out")
    mix_full = sem("mix_full")
    score_full = sem("score_full")
    comb_arg = sem("comb_arg")
    comb_exp = sem("comb_exp")
    gate_out = sem("gate_out")
    side_full = sem("side_full")
    side_free = sem("side_free")
    yt_ready = sem("yt_ready")
    o_free = sem("o_free")
    ln_in = sem("ln_in")
    ln_var = sem("ln_var")
    ln_root = sem("ln_root")
    ln_out = sem("ln_out")
    ln_full = sem("ln_full")
    ln_free = sem("ln_free")
    stored = sem("stored")
    x_in = sem("x_in")
    consts = sem("consts")
    rw_in = sem("rw_in")
    route_full = sem("route_full")
    route_arg = sem("route_arg")
    route_exp = sem("route_exp")
    route_soft = sem("route_soft")
    route_turned = sem("route_turned")
    aff_out = sem("aff_out")
    pos_ready = sem("pos_ready")
    pos_turned = sem("pos_turned")
    pos_out = sem("pos_out")
    slots_in = sem("slots_in")
    gather_full = sem("gather_full")
    xs_out = sem("xs_out")
    pgT_full = sem("pgT_full")
    pgT_out = sem("pgT_out")
    spread_full = sem("spread_full")
    spread_free = sem("spread_free")
    hid_out = sem("hid_out")
    silu_out = sem("silu_out")
    oute_out = sem("oute_out")
    hidT_full = sem("hidT_full")
    hidT_out = sem("hidT_out")
    chosen = sem("chosen")
    b_in = [sem(f"b_in{i}") for i in range(2)]
    far_in = [sem(f"far_in{i}") for i in range(2)]
    wb_in = [sem(f"wb_in{i}") for i in range(4)]
    slot_in = [sem(f"slot_in{i}") for i in range(6)]
    slot_used = [sem(f"slot_used{i}") for i in range(6)]

    C = A["const"]

    def chunk_arrived(eng, n):
        eng.wait_ge(ring_in[n % RING], 16 * (n // RING + 1))

    def b_load(sp, l, n):
        if n >= 2:
            sp.wait_ge(bu_full, n - 1)
        sp.dma_start(bT[:, n % 2], A["s5_b"][l, n]).then_inc(b_in[n % 2], 16)

    def ring_loads(sp, l, first, count):
        order = FIRST_CHUNKS + SECOND_CHUNKS + GATE_CHUNKS
        for n in range(first, first + count):
            if n >= RING:
                sp.wait_ge(acc_full, 2 * (n - RING + 1))
            if n < len(order):
                c = order[n]
                src = A["w_in"][l].rearrange("(c p) n -> p c n", p=P)[:, :, c * CW:(c + 1) * CW]
            else:
                c = n - len(order)
                src = A["w_out"][l].rearrange("(c p) n -> p c n", p=P)[:, :, c * CW:(c + 1) * CW]
            sp.dma_start(ring[:, n % RING], src).then_inc(ring_in[n % RING], 16)

    def project_features(pe, n, j):
        for c in range(ND):
            mm = pe.matmul(acc[:, j, :], ring[:, n % RING, c, j * P:(j + 1) * P], hT[:, c, :],
                           start=(c == 0), stop=(c == ND - 1))
        return mm

    def project_tokens(pe, n, j):
        apart = n in (N_FIRST + 7, N_FIRST + 8)
        for q in range(2):
            t = 2 * j + q
            for c in range(ND):
                rows = hT[:, c, t::NT] if apart else hT[:, c, t * P:(t + 1) * P]
                mm = pe.matmul(acc[:, j, q * CW:(q + 1) * CW], rows,
                               ring[:, n % RING, c, :], start=(c == 0), stop=(c == ND - 1))
        return mm

    def project(pe, n, by_tokens):
        chunk_arrived(pe, n)
        for j in range(2):
            if n >= 1:
                pe.wait_ge(acc_free, 2 * (n - 1) + j + 1)
            mm = (project_tokens if by_tokens else project_features)(pe, n, j)
            mm.then_inc(acc_full, 1)

    def apart(a):
        return a.rearrange("p (m t) -> p t m", t=NT)

    def s5_inputs(pe, n):
        jc, d = n // 8, n % 8 // 4
        pe.wait_ge(b_in[n % 2], 16 * (n // 2 + 1))
        if n >= 1:
            pe.wait_ge(bu_free, n)
        for part in range(2):
            u = uT[:, jc, :] if d == 0 else uT[:, jc, ::-1]
            mm = pe.matmul(pair[:, part, :], bT[:, n % 2, part, :], u, start=True, stop=True)
        mm.then_inc(bu_full, 1)

    def s5_outputs(pe, n):
        jc, d, jj = n // 8, n % 8 // 4, n % 4
        rows = slice(32 * jj, 32 * jj + 32)
        pe.wait_ge(x_full, n + 1)
        if n == 8:
            pe.wait_ge(ys_free, 1)
        for part in range(2):
            mm = pe.matmul(ys[rows, d, :], cT[:, part, n, :], xx[:, part, :], start=(part == 0), stop=(part == 1))
        mm.then_inc(x_free, 1)

    def s5_turns(act, n):
        if n >= 1:
            act.wait_ge(tabled, n)
        act.activation(turn[:, :], iota[:, :], ACT.Copy, scale=par[:, 7, n:n + 1]).then_inc(turned, 1)

    def s5_trig(act, n, link):
        act.wait_ge(fracted, n + 1)
        if n >= 2:
            act.wait_ge(table_free, n - 1)
        link(act.activation(turn[:, :], frac[:, :], ACT.Abs))
        link(act.activation(trig[:, n % 2, 1, :], frac[:, :], ACT.Sin, scale=6.283185))
        act.activation(trig[:, n % 2, 0, :], turn[:, :], ACT.Sin, scale=-6.283185, bias=half_pi[:, :]).then_inc(tabled, 1)

    def s5_fractions(dve, n, link):
        dve.wait_ge(turned, n + 1)
        if n >= 1:
            dve.wait_ge(tabled, n)
        link(dve.tensor_scalar(frac[:, :], turn[:, :], ROUND, ROUND, ALU.add, ALU.subtract))
        dve.tensor_tensor(frac[:, :], turn[:, :], frac[:, :], ALU.subtract).then_inc(fracted, 1)

    def s5_scan(dve, n, link):
        cos = trig[:, n % 2, 0:1, :].to_broadcast([P, 2, SEQ])
        sin = trig[:, n % 2, 1:2, :].to_broadcast([P, 2, SEQ])
        dve.wait_ge(tabled, n + 1)
        dve.wait_ge(bu_full, n + 1)
        link.mark(dve.tensor_tensor(rot[:, 0], pair[:, :, :], cos, ALU.mult))
        link(dve.tensor_tensor(rot[:, 1], pair[:, :, :], sin, ALU.mult))
        dve.sem_inc(bu_free, 1)
        link.mark(dve.tensor_tensor(rot[:, 0, 0], rot[:, 0, 0], rot[:, 1, 1], ALU.add))
        link(dve.tensor_tensor(rot[:, 0, 1], rot[:, 0, 1], rot[:, 1, 0], ALU.subtract))
        for part in range(2):
            link.mark(dve.tensor_tensor_scan(zz[:, part, :], wide(par[:, 6, n:n + 1], SEQ), rot[:, 0, part],
                                             0.0, ALU.mult, ALU.add))
        link.hold()
        link.mark(dve.tensor_tensor(rot[:, 0], zz[:, :, :], cos, ALU.mult))
        link(dve.tensor_tensor(rot[:, 1], zz[:, :, :], sin, ALU.mult))
        dve.sem_inc(table_free, 1)
        if n >= 1:
            dve.wait_ge(x_free, n)
        dve.tensor_tensor(xx[:, 0], rot[:, 0, 0], rot[:, 1, 1], ALU.subtract)
        link(dve.tensor_tensor(xx[:, 1], rot[:, 0, 1], rot[:, 1, 0], ALU.add))
        dve.sem_inc(x_full, 1)

    def s5_collect(dve, jc, link):
        dve.wait_ge(x_free, 8 * jc + 8)
        link(dve.scalar_tensor_tensor(yc[:, jc, :], uT[:, jc, :], s5d[:, jc:jc + 1], ys[:, 0, :], ALU.mult, ALU.add))
        link(dve.tensor_tensor(yc[:, jc, :], yc[:, jc, :], ys[:, 1, ::-1], ALU.add))
        dve.sem_inc(ys_free, 1)

    def take_unit(pe, name):
        u = UNIT[name]
        if u >= 2:
            pe.wait_ge(misc_free[u % 2], u // 2)
        return misc[:, u % 2, :]

    def unit_full(eng, name):
        eng.wait_ge(misc_full, UNIT[name] + 1)
        return misc[:, UNIT[name] % 2, :]

    def unit_read(eng, link, ins, name):
        link(ins)
        eng.sem_inc(misc_free[UNIT[name] % 2], 1)

    def first_block(l):
        with nc.Block() as block:
            first_programs(l, block)

    def first_programs(l, block):
        @block.sync
        def _(sp):
            ring_loads(sp, l, 0, 2)
            sp.dma_start(par[:, 0:3, :], A["s5_par"][l]).then_inc(s5_in, 16)
            sp.dma_start(iota[:, :], C["c_iota"]).then_inc(s5_in, 16)
            sp.dma_start(frq[:, :], A["hy_cols"][l]).then_inc(hy_in, 16)
            sp.dma_start(zt[:, :], C["c_zt"]).then_inc(hy_in, 16)
            sp.dma_start(w1[:, :], A["hy_w1"][l]).then_inc(hy_in, 16)
            sp.dma_start(w2[:, :], A["hy_w2"][l]).then_inc(hy_in, 16)
            sp.dma_start(w3[0:HD, :], A["hy_w3"][l]).then_inc(hy_in, 16)
            sp.dma_start(cT[:, :, :, :], A["s5_c"][l]).then_inc(s5_in, 16)
            sp.dma_start(s5d[:, :], A["s5_dcol"][l]).then_inc(s5_in, 16)
            sp.dma_start(decay[:, :, :], C["c_decay"]).then_inc(tab_in, 16)
            sp.dma_start(hyb[:, :], A["hy_bias_row"][l].partition_broadcast(P)).then_inc(tab_in, 16)
            sp.dma_start(fc[:, :, :], C["c_fc"]).then_inc(tab_in, 16)
            sp.dma_start(fs[:, :, :], C["c_fs"]).then_inc(tab_in, 16)
            sp.dma_start(gs[:, :, :], C["c_gs"]).then_inc(tab_in, 16)
            sp.dma_start(cw[:, :, :], A["hy_conv"][l]).then_inc(cw_in, 16)
            b_load(sp, l, 0)
            b_load(sp, l, 1)
            ring_loads(sp, l, 2, 2)
            b_load(sp, l, 2)
            ring_loads(sp, l, 4, 1)
            b_load(sp, l, 3)
            ring_loads(sp, l, 5, 1)
            for n in range(4, 8):
                b_load(sp, l, n)
            ring_loads(sp, l, N_FIRST, 2)
            b_load(sp, l, 8)
            b_load(sp, l, 9)

        @block.gpsimd
        def _(pool):
            pool.memset(f2[HD:P, :], 0.0)
            pool.memset(w3[HD:P, :], 0.0).then_inc(pads, 1)

        @block.scalar
        def _(act):
            link = Link(act, act_link)
            act.wait_ge(s5_in, 64)
            act.activation(par[:, 3, :], par[:, 2, :], ACT.Exp).then_inc(par_act, 1)
            act.wait_ge(par_dve, 1)
            act.activation(par[:, 6, :], par[:, 4, :], ACT.Exp).then_inc(par_act, 1)
            act.wait_ge(par_dve, 2)
            link(act.activation(par[:, 10, :], par[:, 7, :], ACT.Abs))
            link(act.activation(par[:, 9, :], par[:, 7, :], ACT.Sin, scale=6.283185))
            act.activation(par[:, 10, :], par[:, 10, :], ACT.Sin, scale=-6.283185, bias=half_pi[:, :]).then_inc(par_act, 1)
            for step, i in FIRST_STEPS:
                if step == "project":
                    for j in range(2):
                        act.wait_ge(acc_full, 2 * i + j + 1)
                        if i == 0:
                            ins = act.activation(uT[:, j, :], acc[:, j, :], ACT.Copy)
                        elif i <= 2:
                            ins = act.activation(gtok[:, 2 * j:2 * j + 2, (i - 1) * CW:i * CW],
                                                 acc[:, j, :].rearrange("p (q n) -> p q n", q=2), ACT.Copy)
                        else:
                            if i == 3 and j == 0:
                                act.wait_ge(misc_full, UNIT[("nyquist",)] + 1)
                                act.wait_ge(kre_ready, 2)
                            ins = act.activation(hyT[:, 2 * (i - 3) + j, 1:SEQ + 1], acc[:, j, :], ACT.Copy)
                        ins.then_inc(acc_free, 1)
                elif step == "table":
                    s5_turns(act, i)
                    s5_trig(act, i, link)
                elif step == "mlp":
                    act.wait_ge(mlp_arg, i + 1)
                    f = (f1, f2)[i]
                    act.activation(f[0:HD, :], sq[0:HD, 1, :], ACT.Sin, scale=6.283185).then_inc(mlp_out, 1)
                elif step == "filter":
                    act.wait_ge(tap_pair, i + 1)
                    if i >= 1:
                        act.wait_ge(sq_used, i)
                    link.mark(act.activation(sq[:, 0, :], fa[:, i, :], ACT.Square))
                    link(act.activation(sq[:, 1, :], fb[:, i, :], ACT.Square))
                    act.sem_inc(tap_sq, 1)
                elif step == "norm":
                    bank = unit_full(act, ("norm",))
                    unit_read(act, link, act.activation(rn[:, :], bank, ACT.Sqrt, scale=0.5), ("norm",))
                    act.sem_inc(root_ready, 1)
                elif step == "spectrum":
                    act.wait_ge(kre_raw, i + 1)
                    link(act.activation(kre[:, i, :], kre[:, i, :], ACT.Copy, scale=wf[:, i:i + 1]))
                    if i == 3:
                        act.sem_inc(kre_ready, 1)
                elif step == "tokens":
                    bank = unit_full(act, ("tokens", i))
                    dst = (z0, x1)[i // 2][:, 2 * (i % 2):2 * (i % 2) + 2, :]
                    ins = act.activation(dst, bank.rearrange("p (q n) -> p q n", q=2), ACT.Copy)
                    unit_read(act, link, ins, ("tokens", i))
                    act.sem_inc(tokens_out, 1)
                elif step == "forward":
                    for f in range(NT):
                        bank = unit_full(act, ("forward", i, f))
                        if i == 1 and f == 0:
                            act.wait_ge(prod_out, 1)
                        ins = act.activation(spec[:, f, :, :], bank.rearrange("p (q n) -> p q n", q=2), ACT.Copy)
                        unit_read(act, link, ins, ("forward", i, f))
                        act.sem_inc(spec_out, 1)

        @block.vector
        def _(dve):
            link = Link(dve, dve_link)
            pr = lambda i: par[:, i, :]
            dve.wait_ge(s5_in, 64)
            dve.wait_ge(par_act, 1)
            link.mark(dve.tensor_tensor(pr(4), pr(0), pr(3), ALU.mult))
            link(dve.tensor_tensor(pr(5), pr(1), pr(3), ALU.mult))
            dve.sem_inc(par_dve, 1)
            link(dve.tensor_scalar(pr(7), pr(5), 1.0 / TWO_PI, None, ALU.mult))
            link(dve.tensor_scalar(pr(8), pr(7), ROUND, ROUND, ALU.add, ALU.subtract))
            link(dve.tensor_tensor(pr(7), pr(7), pr(8), ALU.subtract))
            dve.sem_inc(par_dve, 1)
            dve.wait_ge(hy_in, 80)
            link.mark(dve.tensor_scalar(frw[:, 0:2], frq[:, 0:2], 1.0 / TWO_PI, None, ALU.mult))
            link(dve.tensor_tensor(frw[:, 2:4], frq[:, 0:2], frq[:, 2:4], ALU.mult))
            link(dve.tensor_scalar(frw[:, 2:4], frw[:, 2:4], 1.0 / TWO_PI, None, ALU.mult))
            dve.wait_ge(par_act, 3)
            link.mark(dve.tensor_tensor(pr(11), pr(6), pr(10), ALU.mult))
            link.mark(dve.tensor_tensor(pr(12), pr(6), pr(9), ALU.mult))
            link.mark(dve.tensor_tensor(pr(13), pr(0), pr(0), ALU.mult))
            link(dve.tensor_tensor(pr(8), pr(1), pr(1), ALU.mult))
            link.mark(dve.tensor_scalar(pr(11), pr(11), -1.0, None, ALU.add))
            link(dve.tensor_tensor(pr(13), pr(13), pr(8), ALU.add))
            link.mark(dve.reciprocal(pr(13), pr(13)))
            link.mark(dve.tensor_tensor(pr(14), pr(11), pr(0), ALU.mult))
            link.mark(dve.tensor_tensor(pr(8), pr(12), pr(1), ALU.mult))
            link.mark(dve.tensor_tensor(pr(15), pr(12), pr(0), ALU.mult))
            link(dve.tensor_tensor(pr(9), pr(11), pr(1), ALU.mult))
            link.mark(dve.tensor_tensor(pr(14), pr(14), pr(8), ALU.add))
            link(dve.tensor_tensor(pr(15), pr(15), pr(9), ALU.subtract))
            link.mark(dve.tensor_tensor(pr(14), pr(14), pr(13), ALU.mult))
            link(dve.tensor_tensor(pr(15), pr(15), pr(13), ALU.mult))
            cr, ci = cT[:, 0, :, :], cT[:, 1, :, :]
            fr = par[:, 14, :].unsqueeze(2).to_broadcast([P, S5_TILES, 32])
            fi = par[:, 15, :].unsqueeze(2).to_broadcast([P, S5_TILES, 32])
            r4 = [rot[:, a, b, :].rearrange("p (n c) -> p n c", c=32) for a in range(2) for b in range(2)]
            link.mark(dve.tensor_tensor(r4[0], cr, fr, ALU.mult))
            link.mark(dve.tensor_tensor(r4[1], ci, fi, ALU.mult))
            link.mark(dve.tensor_tensor(r4[2], cr, fi, ALU.mult))
            link(dve.tensor_tensor(r4[3], ci, fr, ALU.mult))
            link.mark(dve.tensor_tensor(cr, r4[0], r4[1], ALU.subtract))
            link(dve.scalar_tensor_tensor(ci, r4[2], -1.0, r4[3], ALU.mult, ALU.subtract))

            for step, i in FIRST_STEPS:
                if step == "table":
                    s5_fractions(dve, i, link)
                elif step == "states":
                    s5_scan(dve, i, link)
                elif step == "output":
                    if i == 7:
                        s5_collect(dve, 0, link)
                elif step == "mlp":
                    bank = unit_full(dve, ("mlp", i))[0:HD, :]
                    if i == 1:
                        dve.wait_ge(mlp_out, 1)
                    ins = dve.tensor_scalar(sq[0:HD, 0, :], bank, frw[:, i:i + 1], frw[:, 2 + i:3 + i], ALU.mult, ALU.add)
                    unit_read(dve, link, ins, ("mlp", i))
                    link(dve.tensor_scalar(sq[0:HD, 1, :], sq[0:HD, 0, :], ROUND, ROUND, ALU.add, ALU.subtract))
                    dve.tensor_tensor(sq[0:HD, 1, :], sq[0:HD, 0, :], sq[0:HD, 1, :], ALU.subtract).then_inc(mlp_arg, 1)
                elif step == "filter":
                    if i == 0:
                        dve.wait_ge(tab_in, 80)
                        dve.wait_ge(mlp_out, 2)
                    dec = decay[:, i:i + 1, :].to_broadcast([P, 2, HYW])
                    for d, dst in ((0, fa[:, i, :]), (1, bwd[:, :])):
                        bank = unit_full(dve, ("filter", i, d))
                        ins = dve.tensor_tensor(dst.rearrange("p (o n) -> p o n", o=2),
                                                bank.rearrange("p (o n) -> p o n", o=2), dec, ALU.mult)
                        unit_read(dve, link, ins, ("filter", i, d))
                    if i == 0:
                        link(dve.memset(bwd[0:1, :], 0.0))
                    link(dve.tensor_tensor(fb[:, i, :], fa[:, i, :], bwd[:, :], ALU.subtract))
                    link(dve.tensor_tensor(fa[:, i, :], fa[:, i, :], bwd[:, :], ALU.add))
                    dve.sem_inc(tap_pair, 1)
                    dve.wait_ge(tap_sq, i + 1)
                    if i == 0:
                        link(dve.tensor_tensor(nsum[:, :], sq[:, 0, :], sq[:, 1, :], ALU.add))
                    else:
                        link(dve.tensor_tensor(nsum[:, :], nsum[:, :], sq[:, 0, :], ALU.add))
                        link(dve.tensor_tensor(nsum[:, :], nsum[:, :], sq[:, 1, :], ALU.add))
                    dve.sem_inc(sq_used, 1)
                    if i == 3:
                        dve.sem_inc(sum_ready, 1)
                elif step == "norm":
                    dve.wait_ge(root_ready, 1)
                    link(dve.reciprocal(rn[:, :], rn[:, :]))
                elif step == "spectrum":
                    bank = unit_full(dve, ("spectrum", i, 0))
                    ins = dve.tensor_tensor(kre[:, i, :], bank, rn[:, :], ALU.mult)
                    unit_read(dve, link, ins, ("spectrum", i, 0))
                    dve.tensor_tensor(kre[:, i, :], kre[:, i, :], hyb[:, :], ALU.add).then_inc(kre_raw, 1)
                    bank = unit_full(dve, ("spectrum", i, 1))
                    ins = dve.scalar_tensor_tensor(kim[:, i, :], bank, wf[:, i:i + 1], rn[:, :], ALU.mult, ALU.mult)
                    unit_read(dve, link, ins, ("spectrum", i, 1))
                    if i == 0:
                        link(dve.memset(kim[0:1, 0, :], 0.0))
                elif step == "nyquist":
                    bank = unit_full(dve, ("nyquist",))[0:1, :]
                    dve.wait_ge(kre_ready, 1)
                    link(dve.tensor_copy(knyq[:, :], kre[:, 0, :]))
                    ins = dve.tensor_tensor(knyq[0:1, :], bank, rn[0:1, :], ALU.mult)
                    unit_read(dve, link, ins, ("nyquist",))
                    link(dve.tensor_tensor(knyq[0:1, :], knyq[0:1, :], hyb[0:1, :], ALU.add))
                    link(dve.tensor_scalar(knyq[0:1, :], knyq[0:1, :], 1.0 / (2 * SEQ), None, ALU.mult))
                    dve.wait_ge(misc_full, UNIT[("nyquist",)] + 1)
                    link.mark(dve.memset(hyT[:, :, 0:1], 0.0))
                    link(dve.memset(hyT[:, :, SEQ + 1:SEQ + 2], 0.0))
                    dve.sem_inc(kre_ready, 1)
                elif step == "conv":
                    if i == 0:
                        dve.wait_ge(cw_in, 16)
                    dve.wait_ge(acc_free, 2 * (i + 3) + 2)
                    dst = [u01[:, 2 * i + j, :] if i < 2 else ya[:, j, :] for j in range(2)]
                    q = [2 * i, 2 * i + 1]
                    for j in range(2):
                        link.mark(dve.tensor_scalar(dst[j], hyT[:, q[j], 0:SEQ], cw[:, q[j], 0:1], cw[:, q[j], 3:4], ALU.mult, ALU.add))
                    link.hold()
                    for k in (1, 2):
                        for j in range(2):
                            link.mark(dve.scalar_tensor_tensor(dst[j], hyT[:, q[j], k:k + SEQ], cw[:, q[j], k:k + 1], dst[j], ALU.mult, ALU.add))
                        link.hold()
                    dve.sem_inc(conv_done, 1)
                elif step == "product":
                    dve.wait_ge(spec_out, NT * (i + 1))
                    if i == 1:
                        dve.wait_ge(misc_full, UNIT[("back", 0, 1)] + 1)
                    else:
                        dve.wait_ge(tokens_out, 4)
                    o = slice(i * HYW, (i + 1) * HYW)
                    ure, uim = spec[:, :, 0, :], spec[:, :, 1, :]
                    link.mark(dve.tensor_tensor(prod[:, 0], ure, kre[:, :, o], ALU.mult))
                    link.mark(dve.tensor_tensor(prod[:, 1], uim, kim[:, :, o], ALU.mult))
                    link.mark(dve.tensor_tensor(prod[:, 2], ure, kim[:, :, o], ALU.mult))
                    link.mark(dve.tensor_tensor(prod[:, 3, 1:4], uim[:, 1:4], kre[:, 1:4, o], ALU.mult))
                    link(dve.tensor_tensor(prod[:, 3, 0], uim[:, 0], knyq[:, o], ALU.mult))
                    link.mark(dve.tensor_tensor(prod[:, 0], prod[:, 0], prod[:, 1], ALU.subtract))
                    link(dve.tensor_tensor(prod[:, 2], prod[:, 2], prod[:, 3], ALU.add))
                    dve.sem_inc(prod_out, 1)
                elif step == "back":
                    for c in range(2):
                        bank = unit_full(dve, ("back", i, c))
                        if i == 0:
                            ins = dve.tensor_tensor(z0[:, 2 * c:2 * c + 2, :], bank.rearrange("p (q n) -> p q n", q=2),
                                                    x1[:, 2 * c:2 * c + 2, :], ALU.mult)
                        else:
                            ins = dve.tensor_tensor(ya[:, c, :], bank, ya[:, c, :], ALU.mult)
                        unit_read(dve, link, ins, ("back", i, c))
                        dve.sem_inc(z1_out, 1)

        @block.tensor
        def _(pe):
            def close(mm):
                mm.then_inc(misc_full, 1)

            for step, i in FIRST_STEPS:
                if step == "project":
                    project(pe, i, by_tokens=i in (1, 2))
                elif step == "states":
                    if i == 0:
                        pe.wait_ge(s5_in, 64)
                        pe.wait_ge(acc_free, 2)
                    s5_inputs(pe, i)
                elif step == "output":
                    s5_outputs(pe, i)
                elif step == "mlp":
                    bank = take_unit(pe, ("mlp", i))
                    if i == 0:
                        pe.wait_ge(hy_in, 80)
                        close(pe.matmul(bank[0:HD, :], w1[:, :], zt[:, :], start=True, stop=True))
                    else:
                        pe.wait_ge(mlp_out, 1)
                        close(pe.matmul(bank[0:HD, :], w2[:, :], f1[:, :], start=True, stop=True))
                elif step == "filter":
                    if i == 0:
                        pe.wait_ge(mlp_out, 2)
                        pe.wait_ge(pads, 1)
                    for d in range(2):
                        bank = take_unit(pe, ("filter", i, d))
                        close(pe.matmul(bank, f2[:, i * P:(i + 1) * P], w3[:, d * 512:(d + 1) * 512], start=True, stop=True))
                elif step == "norm":
                    bank = take_unit(pe, ("norm",))
                    pe.wait_ge(sum_ready, 1)
                    close(pe.matmul(bank, ones[:, :], nsum[:, :], start=True, stop=True))
                elif step == "spectrum":
                    for part, (table, taps) in enumerate(((fc, fa), (fs, fb))):
                        bank = take_unit(pe, ("spectrum", i, part))
                        if i == 0 and part == 0:
                            pe.wait_ge(tab_in, 80)
                            pe.wait_ge(tap_pair, 4)
                        for t in range(NT):
                            mm = pe.matmul(bank, table[:, t, i * P:(i + 1) * P], taps[:, t, :], start=(t == 0), stop=(t == NT - 1))
                        close(mm)
                elif step == "nyquist":
                    bank = take_unit(pe, ("nyquist",))
                    for t in range(NT):
                        mm = pe.matmul(bank[0:1, :], fs[:, t, 0:1], fa[:, t, :], start=(t == 0), stop=(t == NT - 1))
                    close(mm)
                elif step == "tokens":
                    bank = take_unit(pe, ("tokens", i))
                    if i == 0:
                        pe.wait_ge(conv_done, 2)
                    for q in range(2):
                        t = 2 * (i % 2) + q
                        for c in range(2):
                            mm = pe.transpose(bank[:, q * HYW + c * P:q * HYW + (c + 1) * P],
                                              u01[:, 2 * (i // 2) + c, t * P:(t + 1) * P], ident[:, :])
                    close(mm)
                elif step == "forward":
                    for f in range(NT):
                        bank = take_unit(pe, ("forward", i, f))
                        if f == 0:
                            if i == 0:
                                pe.wait_ge(tokens_out, 4)
                            else:
                                pe.wait_ge(z1_out, 2)
                        for part, table in enumerate((fc, fs)):
                            for t in range(NT):
                                mm = pe.matmul(bank[:, part * HYW:(part + 1) * HYW], table[:, t, f * P:(f + 1) * P],
                                               z0[:, t, :], start=(t == 0), stop=(t == NT - 1))
                        close(mm)
                elif step == "back":
                    for c in range(2):
                        bank = take_unit(pe, ("back", i, c))
                        if c == 0:
                            pe.wait_ge(prod_out, i + 1)
                        if i == 0:
                            for q in range(2):
                                t = 2 * c + q
                                for f in range(NT):
                                    pe.matmul(bank[:, q * HYW:(q + 1) * HYW], fc[:, f, t * P:(t + 1) * P], prod[:, 0, f, :],
                                              start=(f == 0), stop=False)
                                    mm = pe.matmul(bank[:, q * HYW:(q + 1) * HYW], gs[:, f, t * P:(t + 1) * P], prod[:, 2, f, :],
                                                   start=False, stop=(f == NT - 1))
                        else:
                            for f in range(NT):
                                pe.matmul(bank, prod[:, 0, f, c * P:(c + 1) * P], fc[:, f, :], start=(f == 0), stop=False)
                                mm = pe.matmul(bank, prod[:, 2, f, c * P:(c + 1) * P], gs[:, f, :], start=False, stop=(f == NT - 1))
                        close(mm)

    def second_block(l):
        with nc.Block() as block:
            @block.sync
            def _(sp):
                sp.dma_start(gnorm[:, :], A["gq_norm_row"][l].partition_broadcast(P)).then_inc(rope_in, 16)
                sp.dma_start(rcos[:, :, :], C["c_cos"]).then_inc(rope_in, 16)
                sp.dma_start(rsin[:, :, :], C["c_sin"]).then_inc(rope_in, 16)
                sp.dma_start(gluw[:, :, :], A["s5_glu_w"][l].rearrange("(k p) n -> p k n", p=P)).then_inc(glu_in, 16)
                sp.dma_start(glub[:, :], A["s5_glu_bcol"][l]).then_inc(glu_in, 16)
                for n in range(2, N_SECOND):
                    ring_loads(sp, l, N_FIRST + n, 1)
                    if n + 8 < S5_TILES:
                        b_load(sp, l, n + 8)
                ring_loads(sp, l, N_FIRST + N_SECOND, 3)

            @block.gpsimd
            def _(pool):
                pool.memset(qd[:, :, :], 0.0)
                pool.memset(qg[:, :, :], 0.0).then_inc(queries_clear, 1)

            @block.scalar
            def _(act):
                link = Link(act, act_link2)
                for step, i in SECOND_STEPS:
                    if step == "project":
                        for j in range(2):
                            act.wait_ge(acc_full, 2 * i + j + 1)
                            c = i - N_FIRST
                            if c < 3:
                                if i == N_FIRST and j == 0:
                                    act.wait_ge(queries_clear, 1)
                                tiles = lambda a: a.rearrange("p (t m) -> p t m", t=NT)
                                link.mark(act.activation(tiles(qd[0:HD, 2 * (2 * c + j), :]), apart(acc[0:HD, j, :]), ACT.Copy, scale=-(HD ** -0.5)))
                                ins = act.activation(tiles(qd[HD:P, 2 * (2 * c + j) + 1, :]), apart(acc[HD:P, j, :]), ACT.Copy, scale=-(HD ** -0.5))
                            elif c == 3:
                                ins = act.activation(kd[:, j, :], acc[:, j, :], ACT.Copy)
                            elif c < 6:
                                ins = act.activation(kd[:, 2 * (c - 3) + j, :].rearrange("p (t m) -> p t m", t=NT), apart(acc[:, j, :]), ACT.Copy)
                            else:
                                ins = act.activation(vd[:, 2 * j:2 * j + 2, (c - 6) * CW:(c - 5) * CW],
                                                     acc[:, j, :].rearrange("p (q n) -> p q n", q=2), ACT.Copy)
                            ins.then_inc(acc_free, 1)
                    elif step == "table":
                        s5_turns(act, i)
                        s5_trig(act, i, link)
                    elif step == "rms":
                        act.wait_ge(rms_sum, 1)
                        act.activation(stat[:, :], stat[:, :], ACT.Sqrt, scale=1.0 / HD, bias=eps_rms[:, :]).then_inc(rms_root, 1)
                    elif step == "heads":
                        act.wait_ge(heads_full, i + 1)
                        if i < 2:
                            link.mark(act.activation(qg[0:HD, i, :], misc[0:HD, i % 2, :], ACT.Copy, scale=-(HD ** -0.5)))
                            ins = act.activation(qg[HD:P, i + 2, :], misc[HD:P, i % 2, :], ACT.Copy, scale=-(HD ** -0.5))
                        else:
                            ins = act.activation(kg[:, :], misc[:, i % 2, :], ACT.Copy)
                        ins.then_inc(heads_free, 1)
                    elif step == "gelu":
                        act.wait_ge(ys_free, 2)
                        act.wait_ge(rope_done, 1)
                        act.activation(zg[:, :, :], yc[:, :, :], ACT.Gelu_apprx_tanh).then_inc(glu_z, 1)
                    elif step == "glu":
                        act.wait_ge(glu_full, i + 1)
                        if i == 0:
                            act.wait_ge(glu_in, 32)
                        act.activation(zs[:, i, :], misc[:, (i + 1) % 2, :], ACT.Sigmoid, bias=glub[:, i:i + 1]).then_inc(glu_gate, 1)

            @block.vector
            def _(dve):
                link = Link(dve, dve_link2)
                for step, i in SECOND_STEPS:
                    if step == "table":
                        s5_fractions(dve, i, link)
                    elif step == "states":
                        s5_scan(dve, i, link)
                    elif step == "output":
                        if i == S5_TILES - 1:
                            s5_collect(dve, 1, link)
                    elif step == "rms":
                        qk = gtok[:, :, 0:6 * HD]
                        link(dve.tensor_tensor(ra[:, :, :], qk, qk, ALU.mult))
                        link(dve.tensor_reduce(stat[:, :], ra[:, :, :].rearrange("p t (h d) -> p (t h) d", d=HD), AX.X, ALU.add))
                        dve.sem_inc(rms_sum, 1)
                    elif step == "rope":
                        dve.wait_ge(rms_root, 1)
                        link(dve.reciprocal(stat[:, :], stat[:, :]))
                        for t in range(NT):
                            link.mark(dve.tensor_tensor(
                                ra[:, t, :].rearrange("p (h d) -> p h d", d=HD), gtok[:, t, 0:6 * HD].rearrange("p (h d) -> p h d", d=HD),
                                stat[:, 6 * t:6 * t + 6].unsqueeze(2).to_broadcast([P, 6, HD]), ALU.mult))
                        link.hold()
                        dve.wait_ge(rope_in, 48)
                        link(dve.tensor_tensor(ra[:, :, :], ra[:, :, :], gnorm[:, :].unsqueeze(1).to_broadcast([P, NT, 6 * HD]), ALU.mult))
                        for t in range(NT):
                            x = ra[:, t, :].rearrange("p (h f b c) -> p h f b c", f=2, b=2, c=16)
                            y = rb[:, t, :].rearrange("p (h f b c) -> p h f b c", f=2, b=2, c=16)
                            s = rsin[:, t, :].rearrange("p (f b c) -> p f b c", f=2, b=2)
                            for b in range(2):
                                link.mark(dve.tensor_tensor(y[:, :, :, b, :], x[:, :, :, 1 - b, :],
                                                            s[:, :, b, :].unsqueeze(1).to_broadcast([P, 6, 2, 16]), ALU.mult))
                        link.hold()
                        for t in range(NT):
                            link.mark(dve.tensor_tensor(ra[:, t, :].rearrange("p (h d) -> p h d", d=HD),
                                                        ra[:, t, :].rearrange("p (h d) -> p h d", d=HD),
                                                        rcos[:, t:t + 1, :].to_broadcast([P, 6, HD]), ALU.mult))
                        link.hold()
                        for t in range(NT):
                            turn_heads = lambda a, s: a[:, t, 0:4 * HD].rearrange(s, a=2, b=2)
                            link.mark(dve.tensor_tensor(turn_heads(rp, "p (b a d) -> p a b d"), turn_heads(ra, "p (a b d) -> p a b d"),
                                                        turn_heads(rb, "p (a b d) -> p a b d"), ALU.add))
                        link(dve.tensor_tensor(rp[:, :, 4 * HD:], ra[:, :, 4 * HD:], rb[:, :, 4 * HD:], ALU.add))
                        dve.sem_inc(rope_done, 1)
                    elif step == "glu":
                        dve.wait_ge(glu_gate, i + 1)
                        dve.tensor_tensor(yc[:, i, :], zg[:, i, :], zs[:, i, :], ALU.mult).then_inc(glu_out, 1)

            @block.tensor
            def _(pe):
                for step, i in SECOND_STEPS:
                    if step == "project":
                        project(pe, i, by_tokens=i - N_FIRST >= 6)
                    elif step == "states":
                        s5_inputs(pe, i)
                    elif step == "output":
                        s5_outputs(pe, i)
                    elif step == "heads":
                        if i == 0:
                            pe.wait_ge(rope_done, 1)
                        if i == 2:
                            pe.wait_ge(heads_free, 1)
                        for t in range(NT):
                            mm = pe.transpose(misc[:, i % 2, t * P:(t + 1) * P], rp[:, t, i * P:(i + 1) * P], ident[:, :])
                        mm.then_inc(heads_full, 1)
                    elif step == "glu":
                        if i == 0:
                            pe.wait_ge(glu_z, 1)
                            pe.wait_ge(glu_in, 32)
                            pe.wait_ge(heads_free, 3)
                        for k in range(2):
                            mm = pe.matmul(misc[:, (i + 1) % 2, :], gluw[:, k, i * P:(i + 1) * P], zg[:, k, :], start=(k == 0), stop=(k == 1))
                        mm.then_inc(glu_full, 1)

    def attend_block(l):
        with nc.Block() as block:
            @block.sync
            def _(sp):
                def gate_loads(n):
                    if n >= 3:
                        ring_loads(sp, l, N_FIRST + N_SECOND + n, 1)
                    if n >= 4:
                        sp.wait_ge(side_full, SIDE[("gate", 2 * (n - 4) + 1)] + 1)
                    br, c = BRANCHES[n // 4], n % 4
                    src = A["w_branch"][l, br].rearrange("(k p) n -> p k n", p=P)[:, :, c * CW:(c + 1) * CW]
                    sp.dma_start(wb[:, n % 4], src).then_inc(wb_in[n % 4], 16)

                def far_load(n):
                    if n >= 2:
                        sp.wait_ge(low_done, UNITS_BY[n - 2])
                    sp.dma_start(far[:, n % 2, :], C["c_far"][HEADS[n]]).then_inc(far_in[n % 2], 16)

                far_load(0)
                for n in range(RING):
                    gate_loads(n)
                far_load(1)
                for step, i in ATTEND_STEPS:
                    if step == "scores":
                        n = UNITS[i][0]
                        if i + 1 == UNITS_BY[n] and n + 2 < DILH:
                            far_load(n + 2)
                    elif step == "gate" and i % 2 and i // 2 + RING < N_GATE:
                        gate_loads(i // 2 + RING)
                ring_loads(sp, l, N_FIRST + N_SECOND + N_GATE, OUT_CHUNKS)

            @block.scalar
            def _(act):
                for step, i in ATTEND_STEPS:
                    if step == "scores":
                        act.wait_ge(low_done, i + 1)
                        if i >= 2:
                            act.wait_ge(turn_full, i - 1)
                        n, b = UNITS[i]
                        src = sm if n < DILH else pair
                        if b is None:
                            for t in range(NT):
                                keys = slice(t * P, (t + 1) * P)
                                ins = act.activation(pr[:, i % 2, keys], src[:, i % 2, keys], ACT.Exp, scale=-1.0,
                                                     bias=low[:, 4 * n + t:4 * n + t + 1], accum_out=ssum[:, 4 * n + t:4 * n + t + 1])
                        else:
                            at = slice(4 * n + b, 4 * n + b + 1)
                            ins = act.activation(pr[:, i % 2, :], src[:, i % 2, :], ACT.Exp, scale=-1.0, bias=low[:, at],
                                                 accum_out=ssum[:, at])
                        ins.then_inc(exp_done, 1)
                    elif step == "turn":
                        act.wait_ge(turn_full, i + 1)
                        if i >= 2:
                            act.wait_ge(mix_full, i - 1)
                        act.activation(pT[:, i % 2, :], ys[:, i % 2, :], ACT.Copy).then_inc(turn_out, 1)
                    elif step == "combine":
                        act.wait_ge(comb_arg, i + 1)
                        act.activation(ew[:, :], ew[:, :], ACT.Exp).then_inc(comb_exp, 1)
                    elif step == "gate":
                        n, j = N_FIRST + N_SECOND + i // 2, i % 2
                        act.wait_ge(acc_full, 2 * n + j + 1)
                        if i >= 2:
                            act.wait_ge(gate_out, i - 1)
                        act.activation(th[:, j, :], acc[:, j, :], ACT.Tanh, scale=0.5).then_inc(acc_free, 1)

            @block.vector
            def _(dve):
                link = Link(dve, dve_link3)
                for step, i in ATTEND_STEPS:
                    if step == "scores":
                        n, b = UNITS[i]
                        dve.wait_ge(score_full, i + 1)
                        if n < DILH:
                            dve.wait_ge(far_in[n % 2], 16 * (n // 2 + 1))
                            if i >= 2:
                                dve.wait_ge(exp_done, i - 1)
                            if b is None:
                                v = sm[:, i % 2, :].rearrange("p (t m) -> p t m", t=NT)
                                link(dve.tensor_tensor(v, pair[:, i % 2, :].rearrange("p (t m) -> p t m", t=NT),
                                                       far[:, n % 2, 0:P].unsqueeze(1).to_broadcast([P, NT, P]), ALU.add))
                                dve.tensor_reduce(low[:, 4 * n:4 * n + 4], v, AX.X, ALU.min).then_inc(low_done, 1)
                            else:
                                dve.tensor_tensor_reduce(out=sm[:, i % 2, :], in0=pair[:, i % 2, :],
                                                         in1=far[:, n % 2, NT - 1 - b:NT - 1 - b + SEQ], scale=1.0, scalar=3e38,
                                                         op0=ALU.add, op1=ALU.min, accum_out=low[:, 4 * n + b:4 * n + b + 1]).then_inc(low_done, 1)
                        else:
                            dve.tensor_reduce(low[:, 4 * n + b:4 * n + b + 1], pair[:, i % 2, :], AX.X, ALU.min).then_inc(low_done, 1)
                    elif step == "mix" and i + 1 == UNITS_BY[UNITS[i][0]]:
                        n = UNITS[i][0]
                        dve.wait_ge(mix_full, i + 1)
                        own = HD * (HEADS[n] % 2 if n < DILH else (n - DILH) // 2)
                        bank = misc[:, 0, :].rearrange("p (b d) -> p b d", d=P)[:, :, own:own + HD]
                        if n < DILH:
                            link(dve.tensor_copy(obuf[:, n % 3], bank))
                        else:
                            h = n - DILH
                            dve.wait_ge(exp_done, i + 1)
                            link(dve.reciprocal(rs[:, :], ssum[:, 4 * n:4 * n + 4]))
                            link(dve.tensor_tensor(yt[:, :, h * HD:(h + 1) * HD], bank, rs[:, :].unsqueeze(2).to_broadcast([P, 4, HD]), ALU.mult))
                        dve.sem_inc(o_free, 1)
                    elif step == "combine":
                        lo = low[:, 12 * i:12 * i + 12]
                        dve.wait_ge(exp_done, UNITS_BY[GROUPS * i + GROUPS - 1])
                        link(dve.tensor_tensor(rs[:, :], lo[:, 0:4], lo[:, 4:8], ALU.min))
                        link(dve.tensor_tensor(rs[:, :], rs[:, :], lo[:, 8:12], ALU.min))
                        v3 = lambda a: a.rearrange("p (g b) -> p g b", g=3)
                        link(dve.tensor_tensor(v3(ew[:, :]), rs[:, :].unsqueeze(1).to_broadcast([P, 3, 4]), v3(lo), ALU.subtract))
                        dve.sem_inc(comb_arg, 1)
                        dve.wait_ge(comb_exp, i + 1)
                        link(dve.tensor_tensor(es[:, :], ew[:, :], ssum[:, 12 * i:12 * i + 12], ALU.mult))
                        link(dve.tensor_tensor(rs[:, :], es[:, 0:4], es[:, 4:8], ALU.add))
                        link(dve.tensor_tensor(rs[:, :], rs[:, :], es[:, 8:12], ALU.add))
                        link(dve.reciprocal(rs[:, :], rs[:, :]))
                        link(dve.tensor_tensor(v3(es[:, :]), v3(ew[:, :]), rs[:, :].unsqueeze(1).to_broadcast([P, 3, 4]), ALU.mult))
                        flat = obuf[:, :, :, :].rearrange("p g b d -> p (g b) d")
                        link(dve.tensor_tensor(flat, flat, es[:, :].unsqueeze(2).to_broadcast([P, 12, HD]), ALU.mult))
                        link(dve.tensor_tensor(obuf[:, 0], obuf[:, 0], obuf[:, 1], ALU.add))
                        link(dve.tensor_tensor(yt[:, :, i * HD:(i + 1) * HD], obuf[:, 0], obuf[:, 2], ALU.add))
                    elif step == "features":
                        br, c = i
                        if c == 0:
                            dve.sem_inc(yt_ready, 1)
                        dve.wait_ge(side_full, SIDE[("features", i)] + 1)
                        if br == 1:
                            link(dve.tensor_copy(apart(yT[br][:, c, :]), misc[:, 1, :].rearrange("p (t m) -> p t m", t=NT)))
                        else:
                            link(dve.tensor_copy(yT[br][:, c, :], misc[:, 1, :]))
                        dve.sem_inc(side_free, 1)
                    elif step == "gate":
                        br, d = i // 8, i % 8
                        dve.wait_ge(acc_free, 2 * (N_FIRST + N_SECOND) + i + 1)
                        dve.wait_ge(side_full, SIDE[("gate", i)] + 1)
                        if br == 0:
                            link(dve.scalar_tensor_tensor(merged[:, d, :], th[:, i % 2, :], 1.0, misc[:, 1, :], ALU.add, ALU.mult))
                            dve.sem_inc(side_free, 1)
                        else:
                            link(dve.scalar_tensor_tensor(term[:, :], th[:, i % 2, :], 1.0, misc[:, 1, :], ALU.add, ALU.mult))
                            dve.sem_inc(side_free, 1)
                            link(dve.tensor_tensor(merged[:, d, :], merged[:, d, :], term[:, :], ALU.add))
                        if br == 3:
                            link(dve.tensor_scalar(merged[:, d, :], merged[:, d, :], 0.5, None, ALU.mult))
                        dve.sem_inc(gate_out, 1)

            @block.tensor
            def _(pe):
                for step, i in ATTEND_STEPS:
                    if step == "scores":
                        n, b = UNITS[i]
                        if i >= 2:
                            pe.wait_ge(low_done if i - 2 < N_DIL else exp_done, i - 1)
                        if n < DILH:
                            h = HEADS[n]
                            q, k = qd[:, h, :], kd[:, h // 2, :]
                        else:
                            h = n - DILH
                            q, k = qg[:, h, :], kg[:, :]
                        if b is None:
                            for t in range(NT):
                                own = slice(t * P, (t + 1) * P)
                                mm = pe.matmul(pair[:, i % 2, own], q[:, own], k[:, own], start=True, stop=True)
                        else:
                            mm = pe.matmul(pair[:, i % 2, :], q[:, b * P:(b + 1) * P], k, start=True, stop=True)
                        mm.then_inc(score_full, 1)
                    elif step == "turn":
                        pe.wait_ge(exp_done, i + 1)
                        if i >= 2:
                            pe.wait_ge(turn_out, i - 1)
                        for kc in range(NT):
                            mm = pe.transpose(ys[:, i % 2, kc * P:(kc + 1) * P], pr[:, i % 2, kc * P:(kc + 1) * P], ident[:, :])
                        mm.then_inc(turn_full, 1)
                    elif step == "mix":
                        n, b = UNITS[i]
                        pe.wait_ge(turn_out, i + 1)
                        if b in (0, None) and n >= 1:
                            pe.wait_ge(o_free, n)
                        if n < DILH:
                            h = HEADS[n]
                            v = vd[:, :, h // 2 * P:(h // 2 + 1) * P]
                        else:
                            v = gtok[:, :, 6 * HD:8 * HD]
                        for kc in range(NT):
                            if b is None:
                                mm = pe.matmul(misc[:, 0, kc * P:(kc + 1) * P], pT[:, i % 2, kc * P:(kc + 1) * P], v[:, kc, :], start=True, stop=True)
                            else:
                                mm = pe.matmul(misc[:, 0, b * P:(b + 1) * P], pT[:, i % 2, kc * P:(kc + 1) * P], v[:, kc, :], start=(kc == 0), stop=(kc == NT - 1))
                        mm.then_inc(mix_full, 1)
                    elif step == "features":
                        br, c = i
                        if c == 0:
                            pe.wait_ge(yt_ready, 1 if br == 1 else 2)
                        if SIDE[("features", i)] >= 1:
                            pe.wait_ge(side_free, SIDE[("features", i)])
                        for b in range(NT):
                            mm = pe.transpose(misc[:, 1, b * P:(b + 1) * P], yt[:, b, c * P:(c + 1) * P], ident[:, :])
                        mm.then_inc(side_full, 1)
                    elif step == "gate":
                        n, j = N_FIRST + N_SECOND + i // 2, i % 2
                        if j == 0:
                            chunk_arrived(pe, n)
                        pe.wait_ge(acc_free, 2 * (n - 1) + j + 1)
                        project_features(pe, n, j).then_inc(acc_full, 1)
                        br = BRANCHES[i // 8]
                        if j == 0:
                            pe.wait_ge(wb_in[i // 2 % 4], 16 * (i // 8 + 1))
                        if SIDE[("gate", i)] >= 1:
                            pe.wait_ge(side_free, SIDE[("gate", i)])
                        for k in range(2):
                            mm = pe.matmul(misc[:, 1, :], wb[:, i // 2 % 4, k, j * P:(j + 1) * P], yT[br][:, k, :], start=(k == 0), stop=(k == 1))
                        mm.then_inc(side_full, 1)

    def norm_loads(eng, g, b):
        eng.dma_start(lng[:, :], g.partition_broadcast(P)).then_inc(ln_in, 16)
        eng.dma_start(lnb[:, :], b.partition_broadcast(P)).then_inc(ln_in, 16)

    def norm_vector(dve, link, x):
        for t in range(NT):
            for s in range(2):
                link.mark(dve.bn_stats(lnst[:, t, 6 * s:6 * s + 6], x[:, t, s * 512:(s + 1) * 512]))
        link.hold()
        for t in range(NT):
            link.mark(dve.bn_aggr(lnmv[:, t, :], lnst[:, t, :]))
        link.hold()
        dve.sem_inc(ln_var, 1)
        dve.wait_ge(ln_root, 1)
        link(dve.reciprocal(lnrs[:, :], lnrs[:, :]))
        dve.wait_ge(ln_in, 32)
        for t in range(NT):
            link(dve.tensor_scalar(h[:, t, :], x[:, t, :], lnmv[:, t, 0:1], lnrs[:, t:t + 1], ALU.subtract, ALU.mult))
            link(dve.tensor_tensor(h[:, t, :], h[:, t, :], lng[:, :], ALU.mult))
            link(dve.tensor_tensor(h[:, t, :], h[:, t, :], lnb[:, :], ALU.add))
            dve.sem_inc(ln_out, 1)

    def norm_scalar(act):
        act.wait_ge(ln_var, 1)
        act.activation(lnrs[:, :], lnmv[:, :, 1], ACT.Sqrt, bias=eps_ln[:, :]).then_inc(ln_root, 1)
        for u in range(2 * NT):
            t, s = u // 2, u % 2
            act.wait_ge(ln_full, u + 1)
            act.activation(hT[:, 4 * s:4 * s + 4, t * P:(t + 1) * P], misc[:, u % 2, :].rearrange("p (c n) -> p c n", c=4),
                           ACT.Copy).then_inc(ln_free, 1)

    def norm_tensor(pe):
        for u in range(2 * NT):
            t, s = u // 2, u % 2
            if s == 0:
                pe.wait_ge(ln_out, t + 1)
            if u >= 2:
                pe.wait_ge(ln_free, u - 1)
            for c in range(4):
                mm = pe.transpose(misc[:, u % 2, c * P:(c + 1) * P], h[:, t, (4 * s + c) * P:(4 * s + c + 1) * P], ident[:, :])
            mm.then_inc(ln_full, 1)

    def norm_store(sp):
        for t in range(NT):
            sp.wait_ge(ln_out, t + 1)
            sp.dma_start(out[t * P:(t + 1) * P, :], h[:, t, :]).then_inc(stored, 16)
        sp.wait_ge(stored, 16 * NT)

    USES = [("exp_w_gate", 0, 0), ("exp_w_gate", 0, 1), ("exp_w_up", 0, 0), ("exp_w_up", 0, 1),
            ("exp_w_gate", 1, 0), ("exp_w_gate", 1, 1), ("exp_w_up", 1, 0), ("exp_w_up", 1, 1),
            ("exp_w_down", 0, 0), ("exp_w_down", 1, 0), ("exp_w_down", 0, 1), ("exp_w_down", 1, 1)]
    SLOTS_E = 6

    def uses(i, u):
        return 2 * i + u // SLOTS_E + 1

    def expert_load(sp, l, i, u):
        w, q, half = USES[u]
        k = u % SLOTS_E
        if uses(i, u) >= 2:
            sp.wait_ge(slot_used[k], uses(i, u) - 1)
        src = A[w][l, 2 * i + q].rearrange("(c p) n -> p c n", p=P)[:, 4 * half:4 * half + 4, :]
        sp.dma_start(ering[:, k], src).then_inc(slot_in[k], 16)

    def start_block():
        with nc.Block() as block:
            @block.sync
            def _(sp):
                sp.dma_start(h[:, :, :], A["x"].rearrange("(t p) n -> p t n", p=P)).then_inc(x_in, 16)
                sp.dma_start(ident[:, :], C["c_ident"]).then_inc(x_in, 16)
                sp.dma_start(wf[:, :], C["c_wf"]).then_inc(x_in, 16)
                norm_loads(sp, A["ln_in_g"], A["ln_in_b"])
                norm_store(sp)

            @block.gpsimd
            def _(pool):
                pool.memset(ones[:, :], 1.0)
                pool.memset(half_pi[:, :], math.pi / 2)
                pool.memset(eps_ln[:, :], LN_EPS).then_inc(consts, 1)
                pool.memset(eps_rms[:, :], RMS_EPS)

            @block.scalar
            def _(act):
                act.wait_ge(consts, 1)
                norm_scalar(act)

            @block.vector
            def _(dve):
                link = Link(dve, dve_link4)
                dve.wait_ge(x_in, 48)
                norm_vector(dve, link, h)

            @block.tensor
            def _(pe):
                pe.wait_ge(x_in, 48)
                norm_tensor(pe)

    def finish_block(l):
        with nc.Block() as block:
            @block.sync
            def _(sp):
                sp.dma_start(h[:, :, :], out.rearrange("(t p) n -> p t n", p=P)).then_inc(x_in, 16)
                norm_loads(sp, A["ln1_g"][l], A["ln1_b"][l])
                sp.dma_start(rw[:, :, :], A["router_w"][l].rearrange("(c p) e -> p c e", p=P)).then_inc(rw_in, 16)
                for u in range(SLOTS_E):
                    expert_load(sp, l, 0, u)

            @block.scalar
            def _(act):
                norm_scalar(act)
                act.wait_ge(route_arg, 1)
                act.activation(aff[:, :, :], aff[:, :, :], ACT.Exp).then_inc(route_exp, 1)
                act.wait_ge(route_turned, 1)
                act.activation(affT[:, :], pair[0:NE, 1, :], ACT.Copy).then_inc(aff_out, 1)
                act.wait_ge(pos_turned, 1)
                act.activation(posT[:, :, :], pair[:, 0, 0:NT * NE].rearrange("p (t e) -> p t e", e=NE), ACT.Copy).then_inc(pos_out, 1)

            @block.vector
            def _(dve):
                link = Link(dve, dve_link4)
                dve.wait_ge(x_in, 16)
                for c in range(OUT_CHUNKS):
                    n = N_FIRST + N_SECOND + N_GATE + c
                    for j in range(2):
                        dve.wait_ge(acc_full, 2 * n + j + 1)
                        hs = h[:, 2 * j:2 * j + 2, c * CW:(c + 1) * CW]
                        link.mark(dve.scalar_tensor_tensor(hs, hs, ALPHA, acc[:, j, :].rearrange("p (q n) -> p q n", q=2), ALU.mult, ALU.add))
                        link.hold()
                        dve.sem_inc(acc_free, 1)
                norm_vector(dve, link, h)
                dve.wait_ge(route_full, 1)
                lg = pair[:, 0, 0:NT * NE].rearrange("p (t e) -> p t e", e=NE)
                link(dve.tensor_reduce(rmax[:, :], lg, AX.X, ALU.max))
                link(dve.tensor_tensor(aff[:, :, :], lg, rmax[:, :].unsqueeze(2).to_broadcast([P, NT, NE]), ALU.subtract))
                dve.sem_inc(route_arg, 1)
                dve.wait_ge(route_exp, 1)
                link(dve.tensor_reduce(rmax[:, :], aff[:, :, :], AX.X, ALU.add))
                link(dve.reciprocal(rmax[:, :], rmax[:, :]))
                link(dve.tensor_tensor(aff[:, :, :], aff[:, :, :], rmax[:, :].unsqueeze(2).to_broadcast([P, NT, NE]), ALU.mult))
                dve.sem_inc(route_soft, 1)
                dve.wait_ge(aff_out, 1)
                link(dve.tensor_copy(work[:, :], affT[:, :]))
                for r in range(CAP // 8):
                    link(dve.max(top8[:, :], work[:, :]))
                    if r < CAP // 8 - 1:
                        link(dve.match_replace(work[:, :], top8[:, :], work[:, :], -1.0))
                kth = top8[:, 7:8]
                link(dve.tensor_scalar(gt[:, :], affT[:, :], kth, None, ALU.is_gt))
                link(dve.tensor_scalar(eq[:, :], affT[:, :], kth, None, ALU.is_equal))
                link(dve.tensor_reduce(left[:, :], gt[:, :], AX.X, ALU.add))
                link(dve.tensor_scalar(left[:, :], left[:, :], -1.0, float(CAP), ALU.mult, ALU.add))
                link(dve.tensor_tensor_scan(work[:, :], wide(ones[0:NE, 0:1], SEQ), eq[:, :], 0.0, ALU.mult, ALU.add))
                link(dve.tensor_scalar(work[:, :], work[:, :], left[:, 0:1], None, ALU.is_le))
                link(dve.tensor_tensor(eq[:, :], eq[:, :], work[:, :], ALU.mult))
                link(dve.tensor_tensor(gt[:, :], gt[:, :], eq[:, :], ALU.add))
                link(dve.tensor_tensor_scan(work[:, :], wide(ones[0:NE, 0:1], SEQ), gt[:, :], 0.0, ALU.mult, ALU.add))
                link(dve.tensor_tensor(work[:, :], work[:, :], gt[:, :], ALU.mult))
                link(dve.tensor_scalar(work[:, :], work[:, :], -1.0, None, ALU.add))
                dve.sem_inc(pos_ready, 1)

            @block.tensor
            def _(pe):
                for c in range(OUT_CHUNKS):
                    n = N_FIRST + N_SECOND + N_GATE + c
                    chunk_arrived(pe, n)
                    for j in range(2):
                        pe.wait_ge(acc_free, 2 * (n - 1) + j + 1)
                        for q in range(2):
                            t = 2 * j + q
                            for k in range(ND):
                                mm = pe.matmul(acc[:, j, q * CW:(q + 1) * CW], merged[:, k, t * P:(t + 1) * P],
                                               ring[:, n % RING, k, :], start=(k == 0), stop=(k == ND - 1))
                        mm.then_inc(acc_full, 1)
                norm_tensor(pe)
                pe.wait_ge(ln_free, 2 * NT)
                pe.wait_ge(rw_in, 16)
                for t in range(NT):
                    for k in range(ND):
                        mm = pe.matmul(pair[:, 0, t * NE:(t + 1) * NE], hT[:, k, t * P:(t + 1) * P], rw[:, k, :], start=(k == 0), stop=(k == ND - 1))
                mm.then_inc(route_full, 1)
                pe.wait_ge(route_soft, 1)
                for t in range(NT):
                    mm = pe.transpose(pair[0:NE, 1, t * P:(t + 1) * P], aff[:, t, :], ident[:, :])
                mm.then_inc(route_turned, 1)
                pe.wait_ge(pos_ready, 1)
                for t in range(NT):
                    mm = pe.transpose(pair[:, 0, t * NE:(t + 1) * NE], work[:, t * P:(t + 1) * P], ident[0:NE, 0:NE])
                mm.then_inc(pos_turned, 1)

    def experts_block(l):
        PAIRS = NE // 2

        with nc.Block() as block:
            @block.sync
            def _(sp):
                sp.dma_start(slots[:, :], C["c_iota"][:, 0:CAP]).then_inc(slots_in, 16)
                for i in range(PAIRS):
                    for u in range(SLOTS_E if i == 0 else 0, len(USES)):
                        expert_load(sp, l, i, u)

            @block.scalar
            def _(act):
                for i in range(PAIRS):
                    act.wait_ge(gather_full, i + 1)
                    act.activation(xs[:, :, :], misc[:, :, :].rearrange("p b (c n) -> p (b c) n", n=P), ACT.Copy).then_inc(xs_out, 1)
                    act.wait_ge(pgT_full, i + 1)
                    if i >= 2:
                        act.wait_ge(spread_full, 8 * (i - 1))
                    act.activation(pgT[:, i % 2, :], misc[:, 0, :], ACT.Copy).then_inc(pgT_out, 1)
                    for q in range(2):
                        v = 2 * i + q
                        act.wait_ge(slot_used[(3, 1)[q]], uses(i, (3, 7)[q]))
                        if v >= 1:
                            act.wait_ge(hid_out, v)
                        act.activation(sg[:, :], acc[:, 0, :], ACT.Silu).then_inc(silu_out, 1)
                        act.wait_ge(hidT_full, v + 1)
                        if v >= 2:
                            act.wait_ge(slot_used[5], uses(i - 1, 11))
                        act.activation(hidT[:, q, :], misc[:, q, :], ACT.Copy).then_inc(hidT_out, 1)
                    act.wait_ge(slot_used[5], uses(i, 11))
                    if i >= 1:
                        act.wait_ge(spread_full, 8 * i)
                    act.activation(oute[:, :], ys[:, :, :].rearrange("p a n -> p (a n)"), ACT.Copy).then_inc(oute_out, 1)

            @block.vector
            def _(dve):
                link = Link(dve, dve_link4)
                dve.wait_ge(slots_in, 16)
                for t in range(NT):
                    link.mark(dve.tensor_scalar(accx[:, t, :], h[:, t, :], ALPHA, None, ALU.mult))
                link.hold()

                def choose(i):
                    if i >= 1:
                        dve.wait_ge(pgT_full, i)
                    e = slice(2 * i, 2 * i + 2)
                    pp4 = pp[:, :, :].rearrange("p t (e n) -> p t e n", e=2)
                    pg4 = pg[:, :, :].rearrange("p t (e n) -> p t e n", e=2)
                    for t in range(NT):
                        link.mark(dve.tensor_tensor(pp4[:, t], slots[:, :].unsqueeze(1).to_broadcast([P, 2, CAP]),
                                                    posT[:, t, e].unsqueeze(2).to_broadcast([P, 2, CAP]), ALU.is_equal))
                    link.hold()
                    for t in range(NT):
                        link.mark(dve.tensor_tensor(pg4[:, t], pp4[:, t], aff[:, t, e].unsqueeze(2).to_broadcast([P, 2, CAP]), ALU.mult))
                    link.hold()
                    dve.sem_inc(chosen, 1)

                def add_spread(i):
                    for u in range(8):
                        t, n = u // 2, u % 2
                        dve.wait_ge(spread_full, 8 * i + u + 1)
                        at = accx[:, t, n * 512:(n + 1) * 512]
                        dve.tensor_tensor(at, at, pair[:, u % 2, :], ALU.add).then_inc(spread_free, 1)

                choose(0)
                for i in range(PAIRS):
                    if i + 1 < PAIRS:
                        choose(i + 1)
                    for q in range(2):
                        v = 2 * i + q
                        dve.wait_ge(silu_out, v + 1)
                        if v >= 1:
                            dve.wait_ge(hidT_full, v)
                        dve.tensor_tensor(hid[:, :], sg[:, :], acc[:, 1, :], ALU.mult).then_inc(hid_out, 1)
                        if q == 0 and i >= 1:
                            add_spread(i - 1)
                add_spread(PAIRS - 1)
                dve.wait_ge(spread_free, 8 * PAIRS)

            @block.tensor
            def _(pe):
                def gather(i):
                    pe.wait_ge(chosen, i + 1)
                    if i >= 1:
                        pe.wait_ge(hidT_out, 2 * i)
                    for c in range(ND):
                        for t in range(NT):
                            mm = pe.matmul(misc[:, c // 4, (c % 4) * P:(c % 4 + 1) * P], h[:, t, c * P:(c + 1) * P], pp[:, t, :],
                                           start=(t == 0), stop=(t == NT - 1))
                    mm.then_inc(gather_full, 1)
                    pe.wait_ge(xs_out, i + 1)
                    for t in range(NT):
                        mm = pe.transpose(misc[:, 0, t * P:(t + 1) * P], pg[:, t, :], ident[:, :])
                    mm.then_inc(pgT_full, 1)

                def hidden(i, q):
                    v = 2 * i + q
                    if v >= 1:
                        pe.wait_ge(hid_out, v)
                    for part in range(2):
                        for half in range(2):
                            u = 4 * q + 2 * part + half
                            k = u % SLOTS_E
                            pe.wait_ge(slot_in[k], 16 * uses(i, u))
                            for c in range(4):
                                for n in range(2):
                                    mm = pe.matmul(acc[CAP * n:CAP * n + CAP, part, :], xs[:, 4 * half + c, q * CAP:(q + 1) * CAP],
                                                   ering[:, k, c, n * 512:(n + 1) * 512],
                                                   start=(half == 0 and c == 0), stop=(half == 1 and c == 3))
                            mm.then_inc(slot_used[k], 1)

                def turn_hidden(i, q):
                    v = 2 * i + q
                    pe.wait_ge(hid_out, v + 1)
                    if q == 0:
                        pe.wait_ge(pgT_out, i + 1)
                    for j in range(4):
                        mm = pe.transpose(misc[:, q, j * P:(j + 1) * P], hid[:, j * P:(j + 1) * P], ident[:, :])
                    mm.then_inc(hidT_full, 1)

                def down(i):
                    pe.wait_ge(hidT_out, 2 * i + 2)
                    if i >= 1:
                        pe.wait_ge(oute_out, i)
                    for half in range(2):
                        for q in range(2):
                            u = 8 + 2 * half + q
                            pe.wait_ge(slot_in[u % SLOTS_E], 16 * uses(i, u))
                        for c in range(4):
                            for n in range(2):
                                for q in range(2):
                                    k = (8 + 2 * half + q) % SLOTS_E
                                    mm = pe.matmul(ys[CAP * q:CAP * q + CAP, n, :], hidT[:, q, c * P + half * CAP:c * P + half * CAP + CAP],
                                                   ering[:, k, c, n * 512:(n + 1) * 512],
                                                   start=(half == 0 and c == 0), stop=(half == 1 and c == 3))
                                    if c == 3 and n == 1:
                                        mm.then_inc(slot_used[k], 1)

                def spread(i):
                    pe.wait_ge(oute_out, i + 1)
                    for u in range(8):
                        t, n = u // 2, u % 2
                        if 8 * i + u >= 2:
                            pe.wait_ge(spread_free, 8 * i + u - 1)
                        mm = pe.matmul(pair[:, u % 2, :], pgT[:, i % 2, t * P:(t + 1) * P], oute[:, n * 512:(n + 1) * 512], start=True, stop=True)
                        mm.then_inc(spread_full, 1)

                gather(0)
                for i in range(PAIRS):
                    hidden(i, 0)
                    if i >= 1:
                        spread(i - 1)
                    turn_hidden(i, 0)
                    hidden(i, 1)
                    turn_hidden(i, 1)
                    down(i)
                    if i + 1 < PAIRS:
                        gather(i + 1)
                spread(PAIRS - 1)

    def close_block(l):
        with nc.Block() as block:
            @block.sync
            def _(sp):
                norm_loads(sp, A["ln2_g"][l], A["ln2_b"][l])
                norm_store(sp)

            @block.scalar
            def _(act):
                norm_scalar(act)

            @block.vector
            def _(dve):
                link = Link(dve, dve_link5)
                norm_vector(dve, link, accx)

            @block.tensor
            def _(pe):
                norm_tensor(pe)

    def clear_block(which):
        with nc.Block() as block:
            @block.gpsimd
            def _(pool):
                for s in which:
                    pool.sem_clear(s)

    ln_sems = [ln_in, ln_var, ln_root, ln_out, ln_full, ln_free, stored, x_in, dve_link4]
    start_block()
    clear_block(ln_sems + [consts])
    with nc.Fori(0, depth) as l:
        first_block(l)
        if stage >= 2: second_block(l)
        if stage >= 3: attend_block(l)
        if stage >= 4: finish_block(l)
        if stage >= 5:
            clear_block(ln_sems)
            experts_block(l)
            clear_block(ln_sems)
            close_block(l)
            clear_block(sems)
    return


def kernel(**inputs):
    import numpy as _np
    import concourse.bacc as _bacc
    from concourse import mybir as _mybir
    from concourse.bass_utils import run_bass_kernel_spmd as _run

    nc = _bacc.Bacc("TRN2", target_bir_lowering=False, num_devices=1)
    arrays, A = {}, {}

    def give(name, a):
        a = _np.ascontiguousarray(a)
        arrays[f"in_{name}_dram"] = a
        return nc.dram_tensor(f"in_{name}_dram", a.shape, _mybir.dt.from_np(a.dtype), kind="ExternalInput").ap()

    for name, a in lay_out(inputs).items():
        A[name] = give(name, a)
    A["const"] = {name: give(name, a) for name, a in constants().items()}
    out = nc.dram_tensor("out_0_dram", (1, SEQ, DM), F32, kind="ExternalOutput").ap()
    build(nc, A, out[0])
    r = _run(nc, [arrays], core_ids=[0])
    return r.results[0]["out_0_dram"]
```

```python
import math
from contextlib import ExitStack

import numpy as np

import concourse.bass as bass
from concourse import mybir

F32 = mybir.dt.float32
F32R = mybir.dt.float32r
ALU = mybir.AluOpType
ACT = mybir.ActivationFunctionType
AX = mybir.AxisListType

P = 128
SEQ, DM, DEPTH = 512, 1024, 2
NT = SEQ // P
ND = DM // P
HD = 64
HYW, S5W = 256, 256
DILH, GROUPS, SLOTS = 12, 3, 4
GQH, GKV = 4, 2
NE, CAP, FF = 16, 64, 1024
CW = 256
ALPHA = (2 * DEPTH) ** 0.25
LN_EPS, RMS_EPS = 1e-5, 1e-6
ROUND = 12582912.0
TWO_PI = 2.0 * math.pi
BIG = 1e30

HY0, DQ0, DK0, DV0, S50, GQ0, GK0, GATE0 = 0, 3, 6, 9, 12, 13, 14, 15
FIRST_CHUNKS = [S50, GQ0, GK0, HY0, HY0 + 1, HY0 + 2]
SECOND_CHUNKS = list(range(DQ0, S50))
BRANCHES = [0, 2, 1, 3]
GATE_CHUNKS = [GATE0 + 4 * b + q for b in BRANCHES for q in range(4)]
RING = 4
SLOTS_E = 8
WB = 2
SPLIT_CHUNKS = SECOND_CHUNKS + GATE_CHUNKS
OUT_CHUNKS = DM // CW
N_FIRST, N_SECOND, N_GATE = len(FIRST_CHUNKS), len(SECOND_CHUNKS), len(GATE_CHUNKS)
FARW = SEQ + NT
S5_TILES = 16


def constants():
    t = np.arange(SEQ)
    ang = 2.0 * np.pi * ((t[:, None] * t[None, :]) % (2 * SEQ)) / (2 * SEQ)
    sign = np.where(t % 2 == 0, 1.0, -1.0)
    fc = np.cos(ang)
    fs = -np.sin(ang)
    fs[:, 0] = sign
    gs = -np.sin(ang)
    gs[0, :] = sign
    wf = np.full((SEQ,), 2.0 / (2 * SEQ))
    wf[0] = 1.0 / (2 * SEQ)
    tl = lambda a: np.ascontiguousarray(a.reshape(NT, P, -1).transpose(1, 0, 2)).astype(np.float32)
    lin = np.linspace(0.0, 1.0, SEQ, dtype=np.float32)
    bands = np.linspace(1e-4, 15, 16, dtype=np.float32)
    w = (2.0 * math.pi * np.arange(SEQ, dtype=np.float32) / SEQ).astype(np.float32)
    fw = (bands[None, :] * w[:, None]).astype(np.float32)
    z = np.concatenate([lin[:, None], np.cos(fw), -np.sin(fw)], axis=-1).astype(np.float32)
    deltas = np.abs(np.linspace(math.log(1e-2) / 1.5, math.log(1e-2) / 0.3, HYW, dtype=np.float32))
    decay = np.exp(-lin[:, None] * deltas[None, :]).astype(np.float32)
    inv = 10000.0 ** (-np.arange(0, 32, 2, dtype=np.float32) / 32)
    rows, cols = (t // 64).astype(np.float32), (t % 64).astype(np.float32)
    cs, sn = [], []
    for pos in (rows, cols):
        a = pos[:, None] * inv[None, :]
        cs += [np.cos(a), np.cos(a)]
        sn += [-np.sin(a), np.sin(a)]
    far = np.zeros((DILH, P, FARW), np.float32)
    for g, (win, dil) in enumerate(((128, 1), (512, 4), (2048, 16))):
        col = np.arange(FARW)[None, :]
        off = (col - (NT - 1) if g == 0 else NT * col) - NT * np.arange(P)[:, None]
        ok = (np.abs(off) <= win // 2) & (off % dil == 0)
        for s in range(SLOTS):
            h = g * SLOTS + s
            far[h] = np.where(ok, 2.0 ** (-8.0 * (h + 1) / DILH) * np.abs(off), BIG)
    return {
        "c_fc": tl(fc), "c_fs": tl(fs), "c_gs": tl(gs),
        "c_wf": np.ascontiguousarray(wf.reshape(NT, P).T).astype(np.float32),
        "c_zt": np.ascontiguousarray(z.T), "c_decay": tl(decay),
        "c_cos": tl(np.concatenate(cs, -1)), "c_sin": tl(np.concatenate(sn, -1)),
        "c_far": far, "c_ident": np.eye(P, dtype=np.float32),
        "c_iota": np.broadcast_to(t.astype(np.float32), (P, SEQ)).copy(),
    }


class Link:

    def __init__(self, eng, sem):
        self.eng, self.sem, self.n = eng, sem, 0

    def __call__(self, ins):
        self.mark(ins)
        self.hold()

    def mark(self, ins):
        ins.then_inc(self.sem, 1)
        self.n += 1

    def hold(self):
        self.eng.wait_ge(self.sem, self.n)


def wide(ap, n):
    return ap.to_broadcast([ap.shape[0], n])


FIRST_STEPS = [
    ("table", 0), ("project", 0), ("mlp", 0), ("mlp", 1), ("filter", 0), ("table", 1), ("filter", 1), ("project", 1),
    ("filter", 2), ("filter", 3), ("states", 0), ("project", 2), ("norm", 0), ("table", 2), ("spectrum", 0),
    ("states", 1), ("output", 0), ("spectrum", 1), ("table", 3), ("output", 1), ("spectrum", 2), ("spectrum", 3),
    ("states", 2), ("table", 4), ("nyquist", 0), ("conv", 0), ("project", 3), ("states", 3), ("conv", 1),
    ("project", 4), ("states", 4), ("output", 2), ("project", 5), ("tokens", 0), ("tokens", 1), ("output", 3),
    ("tokens", 2), ("table", 5), ("conv", 2), ("output", 4), ("tokens", 3), ("states", 5), ("forward", 0),
    ("product", 0), ("output", 5), ("table", 6), ("states", 6), ("table", 7), ("back", 0), ("states", 7),
    ("output", 6), ("forward", 1), ("product", 1), ("output", 7), ("back", 1),
]
UNIT_NAMES = []
for _step, _i in FIRST_STEPS:
    UNIT_NAMES += {
        "mlp": [("mlp", _i)],
        "filter": [("filter", _i, 0), ("filter", _i, 1)],
        "norm": [("norm",)],
        "spectrum": [("spectrum", _i, 0), ("spectrum", _i, 1)],
        "nyquist": [("nyquist",)],
        "tokens": [("tokens", _i)],
        "forward": [("forward", _i, f) for f in range(NT)],
        "back": [("back", _i, c) for c in range(2)],
    }.get(_step, [])
UNIT = {name: n for n, name in enumerate(UNIT_NAMES)}
assert len(UNIT) == len(UNIT_NAMES)


SECOND_STEPS = [
    ("split", 0), ("split", 1), ("halves", 0), ("halves", 1), ("halves", 2), ("halves", 3), ("halves", 4),
    ("halves", 5), ("halves", 6), ("halves", 7), ("table", 8), ("states", 8), ("project", 0), ("table", 9),
    ("project", 1), ("rms", 0), ("states", 9), ("table", 10), ("output", 8), ("rope", 0), ("project", 2),
    ("table", 11), ("output", 9), ("states", 10), ("project", 3), ("states", 11), ("table", 12), ("output", 10),
    ("heads", 0), ("states", 12), ("project", 4), ("table", 13), ("output", 11), ("table", 14), ("states", 13),
    ("project", 5), ("output", 12), ("heads", 1), ("heads", 2), ("states", 14), ("project", 6), ("values", 6),
    ("table", 15), ("output", 13), ("project", 7), ("values", 7), ("states", 15), ("output", 14), ("split", 18),
    ("project", 8), ("output", 15), ("gelu", 0), ("values", 8), ("glu", 0), ("split", 19), ("glu", 1),
]

HEADS = [g * SLOTS + s for s in range(SLOTS) for g in range(GROUPS)]
UNITS = []
for _n in range(DILH + GQH):
    UNITS += [(_n, None)] if _n < DILH and HEADS[_n] >= SLOTS else [(_n, _b) for _b in range(NT)]
N_UNITS = len(UNITS)
UNITS_BY = [sum(1 for _u in UNITS if _u[0] <= _n) for _n in range(DILH + GQH)]
N_DIL = UNITS_BY[DILH - 1]
GATE_UNITS = [3, 5, 7, 8, 10, 11, 13, 14, 15, 17, 18, 19, 20, 27, 31, 33, 35, 37, 38, 39]
ATTEND_STEPS = []
for _w in range(N_UNITS + 2):
    if _w < N_UNITS:
        ATTEND_STEPS.append(("scores", _w))
    if _w < 2:
        ATTEND_STEPS += [("move", 2 * _w), ("move", 2 * _w + 1)]
    if _w in GATE_UNITS:
        _g = GATE_UNITS.index(_w)
        ATTEND_STEPS += [("gate", _g), ("split", _g + 2)]
    if 1 <= _w <= N_UNITS:
        ATTEND_STEPS.append(("turn", _w - 1))
    if _w >= 2:
        ATTEND_STEPS.append(("mix", _w - 2))
        _n = UNITS[_w - 2][0]
        if _n < DILH and _n % GROUPS == GROUPS - 1:
            ATTEND_STEPS.append(("combine", _n // GROUPS))
    if _w == N_DIL + 4:
        ATTEND_STEPS += [("features", (1, 0)), ("features", (1, 1))]
_gates = len(GATE_UNITS)
for _i in range(_gates, 2 * N_GATE):
    if _i == 24:
        ATTEND_STEPS += [("features", (3, 0)), ("features", (3, 1))]
    ATTEND_STEPS += [("gate", _i)] + ([("split", _i + 2)] if _i + 2 < 2 * N_GATE else [])
    if 27 <= _i < 27 + OUT_CHUNKS:
        ATTEND_STEPS += [("w_out", _i - 27)]
    if _i >= 2 * N_GATE - 2:
        ATTEND_STEPS += [("merged", _d) for _d in (range(6, 8) if _i % 2 else range(6))]
_steps, ATTEND_STEPS = ATTEND_STEPS, [("w_branch", 0)]
for _step, _i in _steps:
    if _step == "gate" and _i % 8 == 0:
        ATTEND_STEPS.append(("y", _i // 8))
    ATTEND_STEPS.append((_step, _i))
    if _step == "gate" and _i + 1 < 2 * N_GATE:
        ATTEND_STEPS.append(("w_branch", _i + 1))
SIDE = {s: n for n, s in enumerate(x for x in ATTEND_STEPS if x[0] in ("gate", "features"))}
assert len(SIDE) == 36


def lay_out(inputs):
    g = {k: np.asarray(v) for k, v in inputs.items()}
    L = DEPTH
    d = {k: g[k] for k in ("ln_in_g", "ln_in_b", "w_in", "hy_w1", "hy_w2", "hy_w3", "w_branch", "w_out",
                           "ln1_g", "ln1_b", "router_w", "exp_w_gate", "exp_w_up", "exp_w_down", "ln2_g", "ln2_b")}
    d["x"] = g["x"][0]
    cols = lambda a: a.reshape(L, -1, P).transpose(0, 2, 1)
    d["hy_cols"] = np.stack([g["hy_freq"][:, 0], g["hy_freq"][:, 1], g["hy_b1"], g["hy_b2"]], -1)
    d["hy_conv"] = np.stack([cols(g["hy_conv_w"][:, 0]), cols(g["hy_conv_w"][:, 1]), cols(g["hy_conv_w"][:, 2]),
                             cols(g["hy_conv_b"])], -1)
    d["hy_bias_row"] = g["hy_bias"].reshape(L, 512)
    d["s5_dcol"] = cols(g["s5_d"])
    d["s5_glu_bcol"] = cols(g["s5_glu_b"])
    d["s5_glu_w"] = g["s5_glu_w"]
    tiles = lambda a: a.reshape(L, 2, 2, 4, P).transpose(0, 4, 2, 1, 3).reshape(L, P, S5_TILES)
    dt = np.repeat(g["s5_log_dt"][..., None], HD, axis=-1)
    d["s5_par"] = np.stack([tiles(g["s5_lam_re"]), tiles(g["s5_lam_im"]), tiles(dt)], 2).transpose(0, 1, 2, 3)
    bt = np.zeros((L, S5_TILES, P, 2, P), np.float32)
    ct = np.zeros((L, P, 2, S5_TILES, 32), np.float32)
    for part, (b, c) in enumerate(((g["s5_b_re"], g["s5_c_re"]), (g["s5_b_im"], g["s5_c_im"]))):
        for n in range(S5_TILES):
            jc, dr, jj = n // 8, n % 8 // 4, n % 4
            for q in range(2):
                grp = 8 * jc + 2 * jj + q
                bt[:, n, 32 * jj + 16 * q:32 * jj + 16 * q + 16, part, 64 * q:64 * q + 64] = b[:, dr, grp].transpose(0, 2, 1)
                ct[:, 64 * q:64 * q + 64, part, n, 16 * q:16 * q + 16] = c[:, dr, grp].transpose(0, 2, 1)
    d["s5_b"], d["s5_c"] = bt, ct
    d["gq_norm_row"] = np.concatenate([g["gqa_q_norm"]] * GQH + [g["gqa_k_norm"]] * GKV, -1)
    return d


def build(nc, A, out):
    ctx = ExitStack()
    sems = []

    def sem(name):
        s = ctx.enter_context(nc.semaphore(name))
        sems.append(s)
        return s

    K = 1024

    class Area:

        def __init__(self, base, end):
            self.base, self.end = base, end

        def take(self, name, shape, dtype=F32):
            n = (4 * int(np.prod(shape[1:])) + 31) // 32 * 32
            a = nc.alloc_sbuf_tensor_at(name, shape, dtype, offset=FLOOR + self.base)
            self.base += n
            assert self.base <= self.end, (name, self.base, self.end)
            return a

    FLOOR = (nc.sbuf_base + 31) // 32 * 32
    END = 207 * K
    assert FLOOR + END <= nc.sbuf_usable_end
    m = Area(0, END)
    hT = m.take("hT", [P, ND, SEQ])
    ring = m.take("ring", [P, RING, ND, CW])
    ident = m.take("ident", [P, P])
    y_at = m.base
    ya, yc, yb, yd = (m.take(n, [P, 2, SEQ]) for n in ("ya", "yc", "yb", "yd"))
    yT = [ya, yb, yc, yd]
    y_lower = [nc.alloc_sbuf_tensor_at(f"y_lower{br}", [P, 2, SEQ], F32R, offset=FLOOR + y_at + 4 * K * at)
               for br, at in enumerate((0, 2, 1, 3))]
    ones = m.take("ones", [P, P])
    wf = m.take("wf", [P, NT])
    half_pi = m.take("half_pi", [P, 1])
    eps_ln = m.take("eps_ln", [P, 1])
    eps_rms = m.take("eps_rms", [P, 1])
    posT = m.take("posT", [P, NT, NE])
    aff = m.take("aff", [P, NT, NE])
    frq = m.take("frq", [HD, 4])
    frw = m.take("frw", [HD, 4])
    stat = m.take("stat", [P, 24])
    cw = m.take("cw", [P, 6, 4])
    base = m.base

    gtok = m.take("gtok", [P, NT, 512])
    iota = m.take("iota", [P, SEQ])
    uT = m.take("uT", [P, 2, SEQ])
    bT = m.take("bT", [P, 2, 2, P])
    cT = m.take("cT", [P, 2, S5_TILES, 32])
    par = m.take("par", [P, 16, S5_TILES])
    s5d = m.take("s5d", [P, 2])
    turn = m.take("turn", [P, SEQ])
    frac = m.take("frac", [P, SEQ])
    trig = m.take("trig", [P, 2, 2, SEQ])
    rot = m.take("rot", [P, 2, 2, SEQ])
    zz = m.take("zz", [P, 2, SEQ])
    xx = m.take("xx", [P, 2, SEQ])
    s5_end = m.base
    fc = m.take("fc", [P, NT, SEQ])
    fs = m.take("fs", [P, NT, SEQ])
    gs = m.take("gs", [P, NT, SEQ])
    kre = m.take("kre", [P, NT, 512])
    kim = m.take("kim", [P, NT, 512])
    knyq = m.take("knyq", [P, 512])
    z0_at = m.base
    z0 = m.take("z0", [P, NT, HYW])
    x1 = m.take("x1", [P, NT, HYW])
    share = m.base
    m = Area(z0_at, share)
    zt = m.take("zt", [33, SEQ])
    w3 = m.take("w3", [P, 1024])
    f1 = m.take("f1", [HD, SEQ])
    m = Area(share, END)
    fa = m.take("fa", [P, NT, 512])
    fb = m.take("fb", [P, NT, 512])
    decay = m.take("decay", [P, NT, HYW])
    bwd = m.take("bwd", [P, 512])
    sq = m.take("sq", [P, 2, 512])
    nsum = m.take("nsum", [P, 512])
    f2 = m.take("f2", [P, SEQ])
    w1 = m.take("w1", [33, HD])
    w2 = m.take("w2", [HD, HD])
    hyb = m.take("hyb", [P, 512])
    rn = m.take("rn", [P, 512])
    m = Area(share, END)
    hyT = m.take("hyT", [P, 6, SEQ + 2])
    u01 = m.take("u01", [P, 4, SEQ])
    spec = m.take("spec", [P, NT, 2, HYW])
    prod = nc.alloc_sbuf_tensor_at("prod", [P, 4, NT, HYW], F32, offset=FLOOR + share)
    assert m.base <= END

    m = Area(s5_end, END - 8 * K)
    qd = m.take("qd", [P, DILH, SEQ])
    kd = m.take("kd", [P, 6, SEQ])
    vd = m.take("vd", [P, NT, DILH * HD])
    qg = m.take("qg", [P, GQH, SEQ])
    kg = m.take("kg", [P, SEQ])
    attend_at = m.base
    gnorm = m.take("gnorm", [P, 6 * HD])
    rcos = m.take("rcos", [P, NT, HD])
    rsin = m.take("rsin", [P, NT, HD])
    gluw = m.take("gluw", [P, 2, S5W])
    glub = m.take("glub", [P, 2])
    ra_at = m.base
    ra = m.take("ra", [P, NT, 6 * HD])
    rb = m.take("rb", [P, NT, 6 * HD])
    vt = m.take("vt", [P, 2, SEQ])
    m = Area(ra_at, END - 8 * K)
    zg = m.take("zg", [P, 2, SEQ])
    zs = m.take("zs", [P, 2, SEQ])
    m = Area(0, 16 * K)
    h_lower = m.take("h_lower", [P, ND, SEQ], F32R)
    h_upper0 = Area(END - 8 * K, END).take("h_upper0", [P, ND // 2, SEQ], F32R)
    h_upper1 = Area(y_at + 8 * K, y_at + 16 * K).take("h_upper1", [P, ND // 2, SEQ], F32R)
    m = Area(16 * K, 48 * K)
    graw = m.take("graw", [P, 2, ND, CW])
    gsplit = m.take("gsplit", [P, 2, 2, ND, P], F32R)
    m = Area(base + 8 * K, base + 16 * K)
    h_upper1_moved = m.take("h_upper1_moved", [P, ND // 2, SEQ], F32R)
    m = Area(base + 16 * K, s5_end)
    merged_at = m.base
    merged = m.take("merged", [P, ND, SEQ])
    far_at = m.base
    far = m.take("far", [P, 2, FARW])
    sm = m.take("sm", [P, 2, SEQ])
    pr = m.take("pr", [P, 2, SEQ])
    y_upper = m.take("y_upper", [P, 2, SEQ], F32R)
    wb_upper1 = m.take("wb_upper1", [P, 2, P], F32R)
    m = Area(attend_at, END - 8 * K)
    pT = m.take("pT", [P, 2, SEQ])
    wb_at = m.base
    wb = m.take("wb", [P, WB, 2, CW])
    wb_lower = nc.alloc_sbuf_tensor_at("wb_lower", [P, WB, 2, CW], F32R, offset=FLOOR + wb_at)
    wb_upper = [m.take("wb_upper0", [P, 2, P], F32R), wb_upper1]
    th = m.take("th", [P, 2, SEQ])
    term = m.take("term", [P, SEQ])
    yt = m.take("yt", [P, NT, 256])
    obuf = m.take("obuf", [P, 3, 4, HD])
    low = m.take("low", [P, 64])
    ssum = m.take("ssum", [P, 64])
    ew = m.take("ew", [P, 12])
    es = m.take("es", [P, 12])
    rs = m.take("rs", [P, 4])
    m = Area(s5_end, attend_at)
    wo_raw = m.take("wo_raw", [P, OUT_CHUNKS, ND, CW])
    wo_lower = nc.alloc_sbuf_tensor_at("wo_lower", [P, OUT_CHUNKS, ND, CW], F32R, offset=FLOOR + s5_end)
    wo_upper = [m.take(f"wo_upper{c}", [P, ND, CW], F32R) for c in range(OUT_CHUNKS - 1)]
    wo_upper.append(Area(far_at, far_at + 8 * K).take("wo_upper_last", [P, ND, CW], F32R))
    merged_lower = nc.alloc_sbuf_tensor_at("merged_lower", [P, ND, SEQ], F32R, offset=FLOOR + merged_at)
    merged_upper = Area(16 * K, 32 * K).take("merged_upper", [P, ND, SEQ], F32R)
    m = Area(base, END)
    h = m.take("h", [P, NT, DM])
    assert m.base == base + 16 * K
    accx = m.take("accx", [P, NT, DM])
    ering = [m.take(f"ering{i}", [P, 4, DM]) for i in range(6)]
    ering.append(nc.alloc_sbuf_tensor_at("ering6", [P, 4, DM], F32, offset=FLOOR))
    ering.append(nc.alloc_sbuf_tensor_at("ering7", [P, 4, DM], F32, offset=FLOOR + y_at))
    lng = m.take("lng", [P, DM])
    lnb = m.take("lnb", [P, DM])
    lnst = m.take("lnst", [P, NT, 12])
    lnmv = m.take("lnmv", [P, NT, 2])
    lnrs = m.take("lnrs", [P, NT])
    lnsh = m.take("lnsh", [P, NT])
    rmax = m.take("rmax", [P, NT])
    rw = m.take("rw", [P, ND, NE])
    m = Area(y_at, y_at + 16 * K)
    affT = m.take("affT", [NE, SEQ])
    work = m.take("work", [NE, SEQ])
    gt = m.take("gt", [NE, SEQ])
    eq = m.take("eq", [NE, SEQ])
    top8 = m.take("top8", [NE, 8])
    left = m.take("left", [NE, 1])
    m = Area(16 * K, 48 * K)
    xs = m.take("xs", [P, ND, P])
    pp = m.take("pp", [P, NT, P])
    pg = m.take("pg", [P, NT, P])
    pgT = m.take("pgT", [P, 2, SEQ])
    sg = m.take("sg", [P, 512])
    hid = m.take("hid", [P, 512])
    hidT = m.take("hidT", [P, 2, 512])
    oute = m.take("oute", [P, DM])
    slots = m.take("slots", [P, CAP])

    acc = ctx.enter_context(nc.psum_tensor("acc", [P, 2, 512], F32))
    pair = ctx.enter_context(nc.psum_tensor("pair", [P, 2, 512], F32))
    ys = ctx.enter_context(nc.psum_tensor("ys", [P, 2, 512], F32))
    misc = ctx.enter_context(nc.psum_tensor("misc", [P, 2, 512], F32))

    ring_in = [sem(f"ring_in{i}") for i in range(RING)]
    acc_full, acc_free = sem("acc_full"), sem("acc_free")
    s5_in, hy_in, tab_in, cw_in = (sem(n) for n in ("s5_in", "hy_in", "tab_in", "cw_in"))
    act_link, dve_link = sem("act_link"), sem("dve_link")
    par_dve, par_act = sem("par_dve"), sem("par_act")
    turned, fracted, tabled, table_free = (sem(n) for n in ("turned", "fracted", "tabled", "table_free"))
    bu_full, bu_free, x_full, x_free = (sem(n) for n in ("bu_full", "bu_free", "x_full", "x_free"))
    ys_free = sem("ys_free")
    misc_full = sem("misc_full")
    misc_free = [sem("misc_free0"), sem("misc_free1")]
    mlp_arg, mlp_out, tap_pair, tap_sq, sq_used = (sem(n) for n in ("mlp_arg", "mlp_out", "tap_pair", "tap_sq", "sq_used"))
    sum_ready, root_ready, kre_raw, kre_ready = (sem(n) for n in ("sum_ready", "root_ready", "kre_raw", "kre_ready"))
    conv_done, tokens_out, spec_out, prod_out, z1_out = (sem(n) for n in ("conv_done", "tokens_out", "spec_out", "prod_out", "z1_out"))
    pads = sem("pads")

    act_link2 = sem("act_link2")
    dve_link2 = sem("dve_link2")
    dve_link3 = sem("dve_link3")
    dve_link4 = sem("dve_link4")
    rope_in = sem("rope_in")
    glu_in = sem("glu_in")
    rms_sum = sem("rms_sum")
    rms_root = sem("rms_root")
    rope_done = sem("rope_done")
    heads_full = sem("heads_full")
    heads_free = sem("heads_free")
    glu_z = sem("glu_z")
    glu_full = sem("glu_full")
    glu_gate = sem("glu_gate")
    glu_out = sem("glu_out")
    low_done = sem("low_done")
    exp_done = sem("exp_done")
    turn_full = sem("turn_full")
    turn_out = sem("turn_out")
    mix_full = sem("mix_full")
    score_full = sem("score_full")
    comb_arg = sem("comb_arg")
    comb_exp = sem("comb_exp")
    gate_out = sem("gate_out")
    side_full = sem("side_full")
    side_free = sem("side_free")
    yt_ready = sem("yt_ready")
    o_free = sem("o_free")
    rows_in = [sem(f"rows_in{t}") for t in range(NT)]
    wo_in = rows_in

    class Norm:

        def __init__(self, name):
            (self.loaded, self.var, self.root, self.scale, self.normed, self.product, self.out, self.full, self.free,
             self.stored) = self.all = [sem(name + n) for n in ("_loaded", "_var", "_root", "_scale", "_normed",
                                                                "_product", "_out", "_full", "_free", "_stored")]

    norm_1, norm_2 = Norm("norm_1"), Norm("norm_2")
    dve_link5 = sem("dve_link5")
    x_in = sem("x_in")
    rw_in = sem("rw_in")
    route_full = sem("route_full")
    route_arg = sem("route_arg")
    route_exp = sem("route_exp")
    route_soft = sem("route_soft")
    route_turned = sem("route_turned")
    aff_out = sem("aff_out")
    pos_ready = sem("pos_ready")
    pos_turned = sem("pos_turned")
    pos_out = sem("pos_out")
    slots_in = sem("slots_in")
    gather_full = sem("gather_full")
    xs_out = sem("xs_out")
    pgT_full = sem("pgT_full")
    pgT_out = sem("pgT_out")
    spread_full = sem("spread_full")
    spread_free = sem("spread_free")
    hid_out = sem("hid_out")
    silu_out = sem("silu_out")
    oute_out = sem("oute_out")
    hidT_full = sem("hidT_full")
    hidT_out = sem("hidT_out")
    chosen = sem("chosen")
    b_in = [sem(f"b_in{i}") for i in range(2)]
    far_in = [sem(f"far_in{i}") for i in range(2)]
    wb_in = [sem(f"wb_in{i}") for i in range(WB)]
    graw_in = [sem(f"graw_in{i}") for i in range(2)]
    moved = sem("moved")
    y_up, y_low, wb_up, wb_low = (sem(n) for n in ("y_up", "y_low", "wb_up", "wb_low"))
    parts_up, parts_low = sem("parts_up"), sem("parts_low")
    values_full, values_out = sem("values_full"), sem("values_out")
    halves_up, halves_low = sem("halves_up"), sem("halves_low")
    split_up, split_low = sem("split_up"), sem("split_low")
    slot_in = [sem(f"slot_in{i}") for i in range(SLOTS_E)]
    slot_used = [sem(f"slot_used{i}") for i in range(SLOTS_E)]

    late_sems = norm_2.all + slot_in + slot_used + [dve_link5, slots_in, gather_full, xs_out, pgT_full, pgT_out, spread_full,
                                                    spread_free, hid_out, silu_out, oute_out, hidT_full, hidT_out, chosen]
    C = A["const"]

    def chunk_arrived(eng, n):
        eng.wait_ge(ring_in[n % RING], 16 * (n // RING + 1))

    def b_load(sp, l, n):
        if n >= 2:
            sp.wait_ge(bu_full, n - 1)
        sp.dma_start(bT[:, n % 2], A["s5_b"][l, n]).then_inc(b_in[n % 2], 16)

    def ring_loads(sp, l, first, count):
        for n in range(first, first + count):
            if n >= RING:
                sp.wait_ge(acc_full, 2 * (n - RING + 1))
            src = A["w_in"][l].rearrange("(c p) n -> p c n", p=P)[:, :, FIRST_CHUNKS[n] * CW:(FIRST_CHUNKS[n] + 1) * CW]
            sp.dma_start(ring[:, n % RING], src).then_inc(ring_in[n % RING], 16)

    def raw_load(sp, l, m):
        if m < 2:
            last = max(n for n in range(N_FIRST) if n % RING == m)
            sp.wait_ge(acc_full, 2 * last + 2)
        else:
            sp.wait_ge(split_low, 2 * (m - 2) + 2)
        c = SPLIT_CHUNKS[m]
        src = A["w_in"][l].rearrange("(c p) n -> p c n", p=P)[:, :, c * CW:(c + 1) * CW]
        sp.dma_start(graw[:, m % 2], src).then_inc(graw_in[m % 2], 16)

    def raw_half(g):
        return graw[:, g // 2 % 2, :, g % 2 * P:(g % 2 + 1) * P]

    def split_upper(act, g):
        act.wait_ge(graw_in[g // 2 % 2], 16 * (g // 4 + 1))
        if g >= 2:
            act.wait_ge(acc_full, 2 * N_FIRST + g - 1)
        act.activation(gsplit[:, g % 2, 0], raw_half(g), ACT.Copy).then_inc(split_up, 1)

    def split_lower(eng, g):
        eng.wait_ge(split_up, g + 1)
        eng.tensor_tensor(gsplit[:, g % 2, 1], raw_half(g), gsplit[:, g % 2, 0], ALU.subtract).then_inc(split_low, 1)

    def three_passes(pe, out_, a, b, first, last):
        pe.matmul(out_, a[0], b[0], start=first, stop=False)
        pe.matmul(out_, a[0], b[1], start=False, stop=False)
        return pe.matmul(out_, a[1], b[0], start=False, stop=last)

    def split_features(pe, g, uppers):
        for c in range(ND):
            if g == 0:
                pe.wait_ge(halves_low, c + 1)
            w = [gsplit[:, g % 2, part, c, :] for part in range(2)]
            mm = three_passes(pe, acc[:, g % 2, :], w, (uppers[c // 4][:, c % 4, :], h_lower[:, c, :]), c == 0, c == ND - 1)
        return mm

    def out_load(sp, l, c):
        sp.wait_ge(mix_full, N_UNITS)
        src = A["w_out"][l].rearrange("(c p) n -> p c n", p=P)[:, :, c * CW:(c + 1) * CW]
        sp.dma_start(wo_raw[:, c], src).then_inc(wo_in[c], 16)

    def project_features(pe, n, j):
        for c in range(ND):
            mm = pe.matmul(acc[:, j, :], ring[:, n % RING, c, j * P:(j + 1) * P], hT[:, c, :],
                           start=(c == 0), stop=(c == ND - 1))
        return mm

    def project_tokens(pe, n, j):
        for q in range(2):
            t = 2 * j + q
            for c in range(ND):
                mm = pe.matmul(acc[:, j, q * CW:(q + 1) * CW], hT[:, c, t * P:(t + 1) * P],
                               ring[:, n % RING, c, :], start=(c == 0), stop=(c == ND - 1))
        return mm

    def project(pe, n, by_tokens):
        chunk_arrived(pe, n)
        for j in range(2):
            if n >= 1:
                pe.wait_ge(acc_free, 2 * (n - 1) + j + 1)
            mm = (project_tokens if by_tokens else project_features)(pe, n, j)
            mm.then_inc(acc_full, 1)

    def apart(a):
        return a.rearrange("p (m t) -> p t m", t=NT)

    def s5_inputs(pe, n):
        jc, d = n // 8, n % 8 // 4
        pe.wait_ge(b_in[n % 2], 16 * (n // 2 + 1))
        if n >= 1:
            pe.wait_ge(bu_free, n)
        for part in range(2):
            u = uT[:, jc, :] if d == 0 else uT[:, jc, ::-1]
            mm = pe.matmul(pair[:, part, :], bT[:, n % 2, part, :], u, start=True, stop=True)
        mm.then_inc(bu_full, 1)

    def s5_outputs(pe, n):
        jc, d, jj = n // 8, n % 8 // 4, n % 4
        rows = slice(32 * jj, 32 * jj + 32)
        pe.wait_ge(x_full, n + 1)
        if n == 8:
            pe.wait_ge(ys_free, 1)
        for part in range(2):
            mm = pe.matmul(ys[rows, d, :], cT[:, part, n, :], xx[:, part, :], start=(part == 0), stop=(part == 1))
        mm.then_inc(x_free, 1)

    def s5_turns(act, n):
        if n >= 1:
            act.wait_ge(tabled, n)
        act.activation(turn[:, :], iota[:, :], ACT.Copy, scale=par[:, 7, n:n + 1]).then_inc(turned, 1)

    def s5_trig(act, n, link):
        act.wait_ge(fracted, n + 1)
        if n >= 2:
            act.wait_ge(table_free, n - 1)
        link(act.activation(turn[:, :], frac[:, :], ACT.Abs))
        link(act.activation(trig[:, n % 2, 1, :], frac[:, :], ACT.Sin, scale=6.283185))
        act.activation(trig[:, n % 2, 0, :], turn[:, :], ACT.Sin, scale=-6.283185, bias=half_pi[:, :]).then_inc(tabled, 1)

    def s5_fractions(dve, n, link):
        dve.wait_ge(turned, n + 1)
        if n >= 1:
            dve.wait_ge(tabled, n)
        link(dve.tensor_scalar(frac[:, :], turn[:, :], ROUND, ROUND, ALU.add, ALU.subtract))
        dve.tensor_tensor(frac[:, :], turn[:, :], frac[:, :], ALU.subtract).then_inc(fracted, 1)

    def s5_scan(dve, n, link):
        cos = trig[:, n % 2, 0:1, :].to_broadcast([P, 2, SEQ])
        sin = trig[:, n % 2, 1:2, :].to_broadcast([P, 2, SEQ])
        dve.wait_ge(tabled, n + 1)
        dve.wait_ge(bu_full, n + 1)
        link.mark(dve.tensor_tensor(rot[:, 0], pair[:, :, :], cos, ALU.mult))
        link(dve.tensor_tensor(rot[:, 1], pair[:, :, :], sin, ALU.mult))
        dve.sem_inc(bu_free, 1)
        link.mark(dve.tensor_tensor(rot[:, 0, 0], rot[:, 0, 0], rot[:, 1, 1], ALU.add))
        link(dve.tensor_tensor(rot[:, 0, 1], rot[:, 0, 1], rot[:, 1, 0], ALU.subtract))
        for part in range(2):
            link.mark(dve.tensor_tensor_scan(zz[:, part, :], wide(par[:, 6, n:n + 1], SEQ), rot[:, 0, part],
                                             0.0, ALU.mult, ALU.add))
        link.hold()
        link.mark(dve.tensor_tensor(rot[:, 0], zz[:, :, :], cos, ALU.mult))
        link(dve.tensor_tensor(rot[:, 1], zz[:, :, :], sin, ALU.mult))
        dve.sem_inc(table_free, 1)
        if n >= 1:
            dve.wait_ge(x_free, n)
        dve.tensor_tensor(xx[:, 0], rot[:, 0, 0], rot[:, 1, 1], ALU.subtract)
        link(dve.tensor_tensor(xx[:, 1], rot[:, 0, 1], rot[:, 1, 0], ALU.add))
        dve.sem_inc(x_full, 1)

    def s5_collect(dve, jc, link):
        dve.wait_ge(x_free, 8 * jc + 8)
        link(dve.scalar_tensor_tensor(yc[:, jc, :], uT[:, jc, :], s5d[:, jc:jc + 1], ys[:, 0, :], ALU.mult, ALU.add))
        link(dve.tensor_tensor(yc[:, jc, :], yc[:, jc, :], ys[:, 1, ::-1], ALU.add))
        dve.sem_inc(ys_free, 1)

    def take_unit(pe, name):
        u = UNIT[name]
        if u >= 2:
            pe.wait_ge(misc_free[u % 2], u // 2)
        return misc[:, u % 2, :]

    def unit_full(eng, name):
        eng.wait_ge(misc_full, UNIT[name] + 1)
        return misc[:, UNIT[name] % 2, :]

    def unit_read(eng, link, ins, name):
        link(ins)
        eng.sem_inc(misc_free[UNIT[name] % 2], 1)

    def first_block(l):
        with nc.Block() as block:
            first_programs(l, block)

    def first_programs(l, block):
        @block.sync
        def _(sp):
            ring_loads(sp, l, 0, 2)
            sp.dma_start(par[:, 0:3, :], A["s5_par"][l]).then_inc(s5_in, 16)
            sp.dma_start(iota[:, :], C["c_iota"]).then_inc(s5_in, 16)
            sp.dma_start(frq[:, :], A["hy_cols"][l]).then_inc(hy_in, 16)
            sp.dma_start(zt[:, :], C["c_zt"]).then_inc(hy_in, 16)
            sp.dma_start(w1[:, :], A["hy_w1"][l]).then_inc(hy_in, 16)
            sp.dma_start(w2[:, :], A["hy_w2"][l]).then_inc(hy_in, 16)
            sp.dma_start(w3[0:HD, :], A["hy_w3"][l]).then_inc(hy_in, 16)
            sp.dma_start(cT[:, :, :, :], A["s5_c"][l]).then_inc(s5_in, 16)
            sp.dma_start(s5d[:, :], A["s5_dcol"][l]).then_inc(s5_in, 16)
            sp.dma_start(decay[:, :, :], C["c_decay"]).then_inc(tab_in, 16)
            sp.dma_start(hyb[:, :], A["hy_bias_row"][l].partition_broadcast(P)).then_inc(tab_in, 16)
            sp.dma_start(fc[:, :, :], C["c_fc"]).then_inc(tab_in, 16)
            sp.dma_start(fs[:, :, :], C["c_fs"]).then_inc(tab_in, 16)
            sp.dma_start(gs[:, :, :], C["c_gs"]).then_inc(tab_in, 16)
            sp.dma_start(cw[:, :, :], A["hy_conv"][l]).then_inc(cw_in, 16)
            b_load(sp, l, 0)
            b_load(sp, l, 1)
            ring_loads(sp, l, 2, 2)
            b_load(sp, l, 2)
            ring_loads(sp, l, 4, 1)
            b_load(sp, l, 3)
            ring_loads(sp, l, 5, 1)
            for n in range(4, 8):
                b_load(sp, l, n)
            for m in range(2):
                raw_load(sp, l, m)
            b_load(sp, l, 8)
            b_load(sp, l, 9)

        @block.gpsimd
        def _(pool):
            pool.memset(f2[HD:P, :], 0.0)
            pool.memset(w3[HD:P, :], 0.0).then_inc(pads, 1)

        @block.scalar
        def _(act):
            link = Link(act, act_link)
            act.wait_ge(s5_in, 64)
            act.activation(par[:, 3, :], par[:, 2, :], ACT.Exp).then_inc(par_act, 1)
            act.wait_ge(par_dve, 1)
            act.activation(par[:, 6, :], par[:, 4, :], ACT.Exp).then_inc(par_act, 1)
            act.wait_ge(par_dve, 2)
            link(act.activation(par[:, 10, :], par[:, 7, :], ACT.Abs))
            link(act.activation(par[:, 9, :], par[:, 7, :], ACT.Sin, scale=6.283185))
            act.activation(par[:, 10, :], par[:, 10, :], ACT.Sin, scale=-6.283185, bias=half_pi[:, :]).then_inc(par_act, 1)
            for step, i in FIRST_STEPS:
                if step == "project":
                    for j in range(2):
                        act.wait_ge(acc_full, 2 * i + j + 1)
                        if i == 0:
                            ins = act.activation(uT[:, j, :], acc[:, j, :], ACT.Copy)
                        elif i <= 2:
                            ins = act.activation(gtok[:, 2 * j:2 * j + 2, (i - 1) * CW:i * CW],
                                                 acc[:, j, :].rearrange("p (q n) -> p q n", q=2), ACT.Copy)
                        else:
                            if i == 3 and j == 0:
                                act.wait_ge(misc_full, UNIT[("nyquist",)] + 1)
                                act.wait_ge(kre_ready, 2)
                            ins = act.activation(hyT[:, 2 * (i - 3) + j, 1:SEQ + 1], acc[:, j, :], ACT.Copy)
                        ins.then_inc(acc_free, 1)
                elif step == "table":
                    s5_turns(act, i)
                    s5_trig(act, i, link)
                elif step == "mlp":
                    act.wait_ge(mlp_arg, i + 1)
                    f = (f1, f2)[i]
                    act.activation(f[0:HD, :], sq[0:HD, 1, :], ACT.Sin, scale=6.283185).then_inc(mlp_out, 1)
                elif step == "filter":
                    act.wait_ge(tap_pair, i + 1)
                    if i >= 1:
                        act.wait_ge(sq_used, i)
                    link.mark(act.activation(sq[:, 0, :], fa[:, i, :], ACT.Square))
                    link(act.activation(sq[:, 1, :], fb[:, i, :], ACT.Square))
                    act.sem_inc(tap_sq, 1)
                elif step == "norm":
                    bank = unit_full(act, ("norm",))
                    unit_read(act, link, act.activation(rn[:, :], bank, ACT.Sqrt, scale=0.5), ("norm",))
                    act.sem_inc(root_ready, 1)
                elif step == "spectrum":
                    act.wait_ge(kre_raw, i + 1)
                    link(act.activation(kre[:, i, :], kre[:, i, :], ACT.Copy, scale=wf[:, i:i + 1]))
                    if i == 3:
                        act.sem_inc(kre_ready, 1)
                elif step == "tokens":
                    bank = unit_full(act, ("tokens", i))
                    dst = (z0, x1)[i // 2][:, 2 * (i % 2):2 * (i % 2) + 2, :]
                    ins = act.activation(dst, bank.rearrange("p (q n) -> p q n", q=2), ACT.Copy)
                    unit_read(act, link, ins, ("tokens", i))
                    act.sem_inc(tokens_out, 1)
                elif step == "forward":
                    for f in range(NT):
                        bank = unit_full(act, ("forward", i, f))
                        if i == 1 and f == 0:
                            act.wait_ge(prod_out, 2)
                        ins = act.activation(spec[:, f, :, :], bank.rearrange("p (q n) -> p q n", q=2), ACT.Copy)
                        unit_read(act, link, ins, ("forward", i, f))
                        act.sem_inc(spec_out, 1)

        @block.vector
        def _(dve):
            link = Link(dve, dve_link)
            pr = lambda i: par[:, i, :]
            dve.wait_ge(s5_in, 64)
            dve.wait_ge(par_act, 1)
            link.mark(dve.tensor_tensor(pr(4), pr(0), pr(3), ALU.mult))
            link(dve.tensor_tensor(pr(5), pr(1), pr(3), ALU.mult))
            dve.sem_inc(par_dve, 1)
            link(dve.tensor_scalar(pr(7), pr(5), 1.0 / TWO_PI, None, ALU.mult))
            link(dve.tensor_scalar(pr(8), pr(7), ROUND, ROUND, ALU.add, ALU.subtract))
            link(dve.tensor_tensor(pr(7), pr(7), pr(8), ALU.subtract))
            dve.sem_inc(par_dve, 1)
            dve.wait_ge(hy_in, 80)
            link.mark(dve.tensor_scalar(frw[:, 0:2], frq[:, 0:2], 1.0 / TWO_PI, None, ALU.mult))
            link(dve.tensor_tensor(frw[:, 2:4], frq[:, 0:2], frq[:, 2:4], ALU.mult))
            link(dve.tensor_scalar(frw[:, 2:4], frw[:, 2:4], 1.0 / TWO_PI, None, ALU.mult))
            dve.wait_ge(par_act, 3)
            link.mark(dve.tensor_tensor(pr(11), pr(6), pr(10), ALU.mult))
            link.mark(dve.tensor_tensor(pr(12), pr(6), pr(9), ALU.mult))
            link.mark(dve.tensor_tensor(pr(13), pr(0), pr(0), ALU.mult))
            link(dve.tensor_tensor(pr(8), pr(1), pr(1), ALU.mult))
            link.mark(dve.tensor_scalar(pr(11), pr(11), -1.0, None, ALU.add))
            link(dve.tensor_tensor(pr(13), pr(13), pr(8), ALU.add))
            link.mark(dve.reciprocal(pr(13), pr(13)))
            link.mark(dve.tensor_tensor(pr(14), pr(11), pr(0), ALU.mult))
            link.mark(dve.tensor_tensor(pr(8), pr(12), pr(1), ALU.mult))
            link.mark(dve.tensor_tensor(pr(15), pr(12), pr(0), ALU.mult))
            link(dve.tensor_tensor(pr(9), pr(11), pr(1), ALU.mult))
            link.mark(dve.tensor_tensor(pr(14), pr(14), pr(8), ALU.add))
            link(dve.tensor_tensor(pr(15), pr(15), pr(9), ALU.subtract))
            link.mark(dve.tensor_tensor(pr(14), pr(14), pr(13), ALU.mult))
            link(dve.tensor_tensor(pr(15), pr(15), pr(13), ALU.mult))
            cr, ci = cT[:, 0, :, :], cT[:, 1, :, :]
            fr = par[:, 14, :].unsqueeze(2).to_broadcast([P, S5_TILES, 32])
            fi = par[:, 15, :].unsqueeze(2).to_broadcast([P, S5_TILES, 32])
            r4 = [rot[:, a, b, :].rearrange("p (n c) -> p n c", c=32) for a in range(2) for b in range(2)]
            link.mark(dve.tensor_tensor(r4[0], cr, fr, ALU.mult))
            link.mark(dve.tensor_tensor(r4[1], ci, fi, ALU.mult))
            link.mark(dve.tensor_tensor(r4[2], cr, fi, ALU.mult))
            link(dve.tensor_tensor(r4[3], ci, fr, ALU.mult))
            link.mark(dve.tensor_tensor(cr, r4[0], r4[1], ALU.subtract))
            link(dve.scalar_tensor_tensor(ci, r4[2], -1.0, r4[3], ALU.mult, ALU.subtract))

            for step, i in FIRST_STEPS:
                if step == "table":
                    s5_fractions(dve, i, link)
                elif step == "states":
                    s5_scan(dve, i, link)
                elif step == "output":
                    if i == 7:
                        s5_collect(dve, 0, link)
                elif step == "mlp":
                    bank = unit_full(dve, ("mlp", i))[0:HD, :]
                    if i == 1:
                        dve.wait_ge(mlp_out, 1)
                    ins = dve.tensor_scalar(sq[0:HD, 0, :], bank, frw[:, i:i + 1], frw[:, 2 + i:3 + i], ALU.mult, ALU.add)
                    unit_read(dve, link, ins, ("mlp", i))
                    link(dve.tensor_scalar(sq[0:HD, 1, :], sq[0:HD, 0, :], ROUND, ROUND, ALU.add, ALU.subtract))
                    dve.tensor_tensor(sq[0:HD, 1, :], sq[0:HD, 0, :], sq[0:HD, 1, :], ALU.subtract).then_inc(mlp_arg, 1)
                elif step == "filter":
                    if i == 0:
                        dve.wait_ge(tab_in, 80)
                        dve.wait_ge(mlp_out, 2)
                    dec = decay[:, i:i + 1, :].to_broadcast([P, 2, HYW])
                    for d, dst in ((0, fa[:, i, :]), (1, bwd[:, :])):
                        bank = unit_full(dve, ("filter", i, d))
                        ins = dve.tensor_tensor(dst.rearrange("p (o n) -> p o n", o=2),
                                                bank.rearrange("p (o n) -> p o n", o=2), dec, ALU.mult)
                        unit_read(dve, link, ins, ("filter", i, d))
                    if i == 0:
                        link(dve.memset(bwd[0:1, :], 0.0))
                    link(dve.tensor_tensor(fb[:, i, :], fa[:, i, :], bwd[:, :], ALU.subtract))
                    link(dve.tensor_tensor(fa[:, i, :], fa[:, i, :], bwd[:, :], ALU.add))
                    dve.sem_inc(tap_pair, 1)
                    dve.wait_ge(tap_sq, i + 1)
                    if i == 0:
                        link(dve.tensor_tensor(nsum[:, :], sq[:, 0, :], sq[:, 1, :], ALU.add))
                    else:
                        link(dve.tensor_tensor(nsum[:, :], nsum[:, :], sq[:, 0, :], ALU.add))
                        link(dve.tensor_tensor(nsum[:, :], nsum[:, :], sq[:, 1, :], ALU.add))
                    dve.sem_inc(sq_used, 1)
                    if i == 3:
                        dve.sem_inc(sum_ready, 1)
                elif step == "norm":
                    dve.wait_ge(root_ready, 1)
                    link(dve.reciprocal(rn[:, :], rn[:, :]))
                elif step == "spectrum":
                    bank = unit_full(dve, ("spectrum", i, 0))
                    ins = dve.tensor_tensor(kre[:, i, :], bank, rn[:, :], ALU.mult)
                    unit_read(dve, link, ins, ("spectrum", i, 0))
                    dve.tensor_tensor(kre[:, i, :], kre[:, i, :], hyb[:, :], ALU.add).then_inc(kre_raw, 1)
                    bank = unit_full(dve, ("spectrum", i, 1))
                    ins = dve.scalar_tensor_tensor(kim[:, i, :], bank, wf[:, i:i + 1], rn[:, :], ALU.mult, ALU.mult)
                    unit_read(dve, link, ins, ("spectrum", i, 1))
                    if i == 0:
                        link(dve.memset(kim[0:1, 0, :], 0.0))
                elif step == "nyquist":
                    bank = unit_full(dve, ("nyquist",))[0:1, :]
                    dve.wait_ge(kre_ready, 1)
                    link(dve.tensor_copy(knyq[:, :], kre[:, 0, :]))
                    ins = dve.tensor_tensor(knyq[0:1, :], bank, rn[0:1, :], ALU.mult)
                    unit_read(dve, link, ins, ("nyquist",))
                    link(dve.tensor_tensor(knyq[0:1, :], knyq[0:1, :], hyb[0:1, :], ALU.add))
                    link(dve.tensor_scalar(knyq[0:1, :], knyq[0:1, :], 1.0 / (2 * SEQ), None, ALU.mult))
                    dve.wait_ge(misc_full, UNIT[("nyquist",)] + 1)
                    link.mark(dve.memset(hyT[:, :, 0:1], 0.0))
                    link(dve.memset(hyT[:, :, SEQ + 1:SEQ + 2], 0.0))
                    dve.sem_inc(kre_ready, 1)
                elif step == "conv":
                    if i == 0:
                        dve.wait_ge(cw_in, 16)
                    dve.wait_ge(acc_free, 2 * (i + 3) + 2)
                    dst = [u01[:, 2 * i + j, :] if i < 2 else ya[:, j, :] for j in range(2)]
                    q = [2 * i, 2 * i + 1]
                    for j in range(2):
                        link.mark(dve.tensor_scalar(dst[j], hyT[:, q[j], 0:SEQ], cw[:, q[j], 0:1], cw[:, q[j], 3:4], ALU.mult, ALU.add))
                    link.hold()
                    for k in (1, 2):
                        for j in range(2):
                            link.mark(dve.scalar_tensor_tensor(dst[j], hyT[:, q[j], k:k + SEQ], cw[:, q[j], k:k + 1], dst[j], ALU.mult, ALU.add))
                        link.hold()
                    dve.sem_inc(conv_done, 1)
                elif step == "product":
                    if i == 1:
                        dve.wait_ge(misc_full, UNIT[("back", 0, 1)] + 1)
                    else:
                        dve.wait_ge(tokens_out, 4)
                    o = slice(i * HYW, (i + 1) * HYW)
                    for half in range(2):
                        dve.wait_ge(spec_out, NT * i + 2 * half + 2)
                        f = slice(2 * half, 2 * half + 2)
                        ure, uim = spec[:, f, 0, :], spec[:, f, 1, :]
                        link.mark(dve.tensor_tensor(prod[:, 0, f], ure, kre[:, f, o], ALU.mult))
                        link.mark(dve.tensor_tensor(prod[:, 1, f], uim, kim[:, f, o], ALU.mult))
                        link.mark(dve.tensor_tensor(prod[:, 2, f], ure, kim[:, f, o], ALU.mult))
                        if half == 0:
                            link.mark(dve.tensor_tensor(prod[:, 3, 0], uim[:, 0], knyq[:, o], ALU.mult))
                            link(dve.tensor_tensor(prod[:, 3, 1], uim[:, 1], kre[:, 1, o], ALU.mult))
                        else:
                            link(dve.tensor_tensor(prod[:, 3, f], uim, kre[:, f, o], ALU.mult))
                        link.mark(dve.tensor_tensor(prod[:, 0, f], prod[:, 0, f], prod[:, 1, f], ALU.subtract))
                        link(dve.tensor_tensor(prod[:, 2, f], prod[:, 2, f], prod[:, 3, f], ALU.add))
                        dve.sem_inc(prod_out, 1)
                elif step == "back":
                    for c in range(2):
                        bank = unit_full(dve, ("back", i, c))
                        if i == 0:
                            ins = dve.tensor_tensor(z0[:, 2 * c:2 * c + 2, :], bank.rearrange("p (q n) -> p q n", q=2),
                                                    x1[:, 2 * c:2 * c + 2, :], ALU.mult)
                        else:
                            ins = dve.tensor_tensor(ya[:, c, :], bank, ya[:, c, :], ALU.mult)
                        unit_read(dve, link, ins, ("back", i, c))
                        dve.sem_inc(z1_out, 1)

        @block.tensor
        def _(pe):
            def close(mm):
                mm.then_inc(misc_full, 1)

            for step, i in FIRST_STEPS:
                if step == "project":
                    project(pe, i, by_tokens=i in (1, 2))
                elif step == "states":
                    if i == 0:
                        pe.wait_ge(s5_in, 64)
                        pe.wait_ge(acc_free, 2)
                    s5_inputs(pe, i)
                elif step == "output":
                    s5_outputs(pe, i)
                elif step == "mlp":
                    bank = take_unit(pe, ("mlp", i))
                    if i == 0:
                        pe.wait_ge(hy_in, 80)
                        close(pe.matmul(bank[0:HD, :], w1[:, :], zt[:, :], start=True, stop=True))
                    else:
                        pe.wait_ge(mlp_out, 1)
                        close(pe.matmul(bank[0:HD, :], w2[:, :], f1[:, :], start=True, stop=True))
                elif step == "filter":
                    if i == 0:
                        pe.wait_ge(mlp_out, 2)
                        pe.wait_ge(pads, 1)
                    for d in range(2):
                        bank = take_unit(pe, ("filter", i, d))
                        close(pe.matmul(bank, f2[:, i * P:(i + 1) * P], w3[:, d * 512:(d + 1) * 512], start=True, stop=True))
                elif step == "norm":
                    bank = take_unit(pe, ("norm",))
                    pe.wait_ge(sum_ready, 1)
                    close(pe.matmul(bank, ones[:, :], nsum[:, :], start=True, stop=True))
                elif step == "spectrum":
                    for part, (table, taps) in enumerate(((fc, fa), (fs, fb))):
                        bank = take_unit(pe, ("spectrum", i, part))
                        if i == 0 and part == 0:
                            pe.wait_ge(tab_in, 80)
                            pe.wait_ge(tap_pair, 4)
                        for t in range(NT):
                            mm = pe.matmul(bank, table[:, t, i * P:(i + 1) * P], taps[:, t, :], start=(t == 0), stop=(t == NT - 1))
                        close(mm)
                elif step == "nyquist":
                    bank = take_unit(pe, ("nyquist",))
                    for t in range(NT):
                        mm = pe.matmul(bank[0:1, :], fs[:, t, 0:1], fa[:, t, :], start=(t == 0), stop=(t == NT - 1))
                    close(mm)
                elif step == "tokens":
                    bank = take_unit(pe, ("tokens", i))
                    if i == 0:
                        pe.wait_ge(conv_done, 2)
                    for q in range(2):
                        t = 2 * (i % 2) + q
                        for c in range(2):
                            mm = pe.transpose(bank[:, q * HYW + c * P:q * HYW + (c + 1) * P],
                                              u01[:, 2 * (i // 2) + c, t * P:(t + 1) * P], ident[:, :])
                    close(mm)
                elif step == "forward":
                    for f in range(NT):
                        bank = take_unit(pe, ("forward", i, f))
                        if f == 0:
                            if i == 0:
                                pe.wait_ge(tokens_out, 4)
                            else:
                                pe.wait_ge(z1_out, 2)
                        for part, table in enumerate((fc, fs)):
                            for t in range(NT):
                                mm = pe.matmul(bank[:, part * HYW:(part + 1) * HYW], table[:, t, f * P:(f + 1) * P],
                                               z0[:, t, :], start=(t == 0), stop=(t == NT - 1))
                        close(mm)
                elif step == "back":
                    for c in range(2):
                        bank = take_unit(pe, ("back", i, c))
                        if c == 0:
                            pe.wait_ge(prod_out, 2 * i + 1)
                        if i == 0:
                            for q in range(2):
                                t = 2 * c + q
                                for f in range(NT):
                                    if t == 0 and f == 2:
                                        pe.wait_ge(prod_out, 2)
                                    pe.matmul(bank[:, q * HYW:(q + 1) * HYW], fc[:, f, t * P:(t + 1) * P], prod[:, 0, f, :],
                                              start=(f == 0), stop=False)
                                    mm = pe.matmul(bank[:, q * HYW:(q + 1) * HYW], gs[:, f, t * P:(t + 1) * P], prod[:, 2, f, :],
                                                   start=False, stop=(f == NT - 1))
                        else:
                            for f in range(NT):
                                if c == 0 and f == 2:
                                    pe.wait_ge(prod_out, 4)
                                pe.matmul(bank, prod[:, 0, f, c * P:(c + 1) * P], fc[:, f, :], start=(f == 0), stop=False)
                                mm = pe.matmul(bank, prod[:, 2, f, c * P:(c + 1) * P], gs[:, f, :], start=False, stop=(f == NT - 1))
                        close(mm)

    def second_block(l):
        with nc.Block() as block:
            @block.sync
            def _(sp):
                sp.dma_start(gnorm[:, :], A["gq_norm_row"][l].partition_broadcast(P)).then_inc(rope_in, 16)
                sp.dma_start(rcos[:, :, :], C["c_cos"]).then_inc(rope_in, 16)
                sp.dma_start(rsin[:, :, :], C["c_sin"]).then_inc(rope_in, 16)
                sp.dma_start(gluw[:, :, :], A["s5_glu_w"][l].rearrange("(k p) n -> p k n", p=P)).then_inc(glu_in, 16)
                sp.dma_start(glub[:, :], A["s5_glu_bcol"][l]).then_inc(glu_in, 16)
                for m in range(2, N_SECOND + 2):
                    raw_load(sp, l, m)
                    if m + 8 < S5_TILES:
                        b_load(sp, l, m + 8)

            @block.gpsimd
            def _(pool):
                for g in range(2 * N_SECOND + 2):
                    split_lower(pool, g)
                    if g == 1:
                        pool.memset(qd[:, :, :], 0.0).then_inc(pads, 1)
                    if g == 3:
                        pool.memset(qg[:, :, :], 0.0).then_inc(pads, 1)

            @block.scalar
            def _(act):
                link = Link(act, act_link2)
                for step, i in SECOND_STEPS:
                    if step == "project":
                        for j in range(2):
                            act.wait_ge(acc_full, 2 * (N_FIRST + i) + j + 1)
                            c = i
                            if c < 3:
                                if i == 0 and j == 0:
                                    act.wait_ge(pads, 2)
                                tiles = lambda a: a.rearrange("p (t m) -> p t m", t=NT)
                                link.mark(act.activation(tiles(qd[0:HD, 2 * (2 * c + j), :]), apart(acc[0:HD, j, :]), ACT.Copy, scale=-(HD ** -0.5)))
                                ins = act.activation(tiles(qd[HD:P, 2 * (2 * c + j) + 1, :]), apart(acc[HD:P, j, :]), ACT.Copy, scale=-(HD ** -0.5))
                            elif c == 3:
                                ins = act.activation(kd[:, j, :], acc[:, j, :], ACT.Copy)
                            elif c < 6:
                                ins = act.activation(kd[:, 2 * (c - 3) + j, :].rearrange("p (t m) -> p t m", t=NT), apart(acc[:, j, :]), ACT.Copy)
                            else:
                                if c > 6:
                                    act.wait_ge(values_full, 2 * (c - 7) + j + 1)
                                ins = act.activation(vt[:, j, :], acc[:, j, :], ACT.Copy)
                            ins.then_inc(acc_free, 1)
                            if 2 * i + j + 2 < 2 * N_SECOND:
                                split_upper(act, 2 * i + j + 2)
                    elif step == "halves":
                        act.activation((h_upper0, h_upper1)[i // 4][:, i % 4, :], hT[:, i, :], ACT.Copy).then_inc(halves_up, 1)
                    elif step == "split":
                        split_upper(act, i)
                    elif step == "table":
                        s5_turns(act, i)
                        s5_trig(act, i, link)
                    elif step == "rms":
                        act.wait_ge(rms_sum, 1)
                        act.activation(stat[:, :], stat[:, :], ACT.Sqrt, scale=1.0 / HD, bias=eps_rms[:, :]).then_inc(rms_root, 1)
                    elif step == "heads":
                        act.wait_ge(heads_full, i + 1)
                        if i == 0:
                            act.wait_ge(pads, 3)
                        if i < 2:
                            link.mark(act.activation(qg[0:HD, i, :], misc[0:HD, i % 2, :], ACT.Copy, scale=-(HD ** -0.5)))
                            ins = act.activation(qg[HD:P, i + 2, :], misc[HD:P, i % 2, :], ACT.Copy, scale=-(HD ** -0.5))
                        else:
                            ins = act.activation(kg[:, :], misc[:, i % 2, :], ACT.Copy)
                        ins.then_inc(heads_free, 1)
                    elif step == "values":
                        for j in range(2):
                            act.wait_ge(values_full, 2 * (i - 6) + j + 1)
                            at = (i - 6) * CW + j * P
                            act.activation(vd[:, :, at:at + P], misc[:, j, :].rearrange("p (t n) -> p t n", t=NT), ACT.Copy).then_inc(values_out, 1)
                    elif step == "gelu":
                        act.wait_ge(ys_free, 2)
                        act.wait_ge(rope_done, 1)
                        act.activation(zg[:, :, :], yc[:, :, :], ACT.Gelu_apprx_tanh).then_inc(glu_z, 1)
                    elif step == "glu":
                        act.wait_ge(glu_full, i + 1)
                        if i == 0:
                            act.wait_ge(glu_in, 32)
                        act.activation(zs[:, i, :], misc[:, (i + 1) % 2, :], ACT.Sigmoid, bias=glub[:, i:i + 1]).then_inc(glu_gate, 1)

            @block.vector
            def _(dve):
                link = Link(dve, dve_link2)
                for step, i in SECOND_STEPS:
                    if step == "table":
                        s5_fractions(dve, i, link)
                    elif step == "states":
                        s5_scan(dve, i, link)
                    elif step == "output":
                        if i == S5_TILES - 1:
                            s5_collect(dve, 1, link)
                    elif step == "halves":
                        dve.wait_ge(halves_up, i + 1)
                        dve.tensor_tensor(h_lower[:, i, :], hT[:, i, :], (h_upper0, h_upper1)[i // 4][:, i % 4, :], ALU.subtract).then_inc(halves_low, 1)
                    elif step == "rms":
                        qk = gtok[:, :, 0:6 * HD]
                        link(dve.tensor_tensor(ra[:, :, :], qk, qk, ALU.mult))
                        link(dve.tensor_reduce(stat[:, :], ra[:, :, :].rearrange("p t (h d) -> p (t h) d", d=HD), AX.X, ALU.add))
                        dve.sem_inc(rms_sum, 1)
                    elif step == "rope":
                        dve.wait_ge(rms_root, 1)
                        link(dve.reciprocal(stat[:, :], stat[:, :]))
                        for t in range(NT):
                            link.mark(dve.tensor_tensor(
                                ra[:, t, :].rearrange("p (h d) -> p h d", d=HD), gtok[:, t, 0:6 * HD].rearrange("p (h d) -> p h d", d=HD),
                                stat[:, 6 * t:6 * t + 6].unsqueeze(2).to_broadcast([P, 6, HD]), ALU.mult))
                        link.hold()
                        dve.wait_ge(rope_in, 48)
                        link(dve.tensor_tensor(ra[:, :, :], ra[:, :, :], gnorm[:, :].unsqueeze(1).to_broadcast([P, NT, 6 * HD]), ALU.mult))
                        for t in range(NT):
                            x = ra[:, t, :].rearrange("p (h f b c) -> p h f b c", f=2, b=2, c=16)
                            y = rb[:, t, :].rearrange("p (h f b c) -> p h f b c", f=2, b=2, c=16)
                            s = rsin[:, t, :].rearrange("p (f b c) -> p f b c", f=2, b=2)
                            for b in range(2):
                                link.mark(dve.tensor_tensor(y[:, :, :, b, :], x[:, :, :, 1 - b, :],
                                                            s[:, :, b, :].unsqueeze(1).to_broadcast([P, 6, 2, 16]), ALU.mult))
                        link.hold()
                        for t in range(NT):
                            link.mark(dve.tensor_tensor(ra[:, t, :].rearrange("p (h d) -> p h d", d=HD),
                                                        ra[:, t, :].rearrange("p (h d) -> p h d", d=HD),
                                                        rcos[:, t:t + 1, :].to_broadcast([P, 6, HD]), ALU.mult))
                        link.hold()
                        for t in range(NT):
                            turn_heads = lambda a, s: a[:, t, 0:4 * HD].rearrange(s, a=2, b=2)
                            link.mark(dve.tensor_tensor(turn_heads(gtok, "p (b a d) -> p a b d"), turn_heads(ra, "p (a b d) -> p a b d"),
                                                        turn_heads(rb, "p (a b d) -> p a b d"), ALU.add))
                        link(dve.tensor_tensor(gtok[:, :, 4 * HD:6 * HD], ra[:, :, 4 * HD:], rb[:, :, 4 * HD:], ALU.add))
                        dve.sem_inc(rope_done, 1)
                    elif step == "glu":
                        dve.wait_ge(glu_gate, i + 1)
                        dve.tensor_tensor(yc[:, i, :], zg[:, i, :], zs[:, i, :], ALU.mult).then_inc(glu_out, 1)

            @block.tensor
            def _(pe):
                for step, i in SECOND_STEPS:
                    if step == "project":
                        for g in (2 * i, 2 * i + 1):
                            pe.wait_ge(split_low, g + 1)
                            pe.wait_ge(acc_free, 2 * N_FIRST + g - 1)
                            split_features(pe, g, (h_upper0, h_upper1)).then_inc(acc_full, 1)
                    elif step == "states":
                        s5_inputs(pe, i)
                    elif step == "output":
                        s5_outputs(pe, i)
                    elif step == "heads":
                        if i == 0:
                            pe.wait_ge(rope_done, 1)
                        if i == 2:
                            pe.wait_ge(heads_free, 1)
                        for t in range(NT):
                            mm = pe.transpose(misc[:, i % 2, t * P:(t + 1) * P], gtok[:, t, i * P:(i + 1) * P], ident[:, :])
                        mm.then_inc(heads_full, 1)
                    elif step == "values":
                        pe.wait_ge(acc_free, 2 * (N_FIRST + i) + 2)
                        if i == 6:
                            pe.wait_ge(heads_free, 3)
                        for j in range(2):
                            if i > 6:
                                pe.wait_ge(values_out, 2 * (i - 7) + j + 1)
                            for t in range(NT):
                                rows = slice(t * P, (t + 1) * P) if i == 6 else slice(t, None, NT)
                                mm = pe.transpose(misc[:, j, t * P:(t + 1) * P], vt[:, j, rows], ident[:, :])
                            mm.then_inc(values_full, 1)
                    elif step == "glu":
                        if i == 0:
                            pe.wait_ge(glu_z, 1)
                            pe.wait_ge(glu_in, 32)
                            pe.wait_ge(values_out, 6)
                        for k in range(2):
                            mm = pe.matmul(misc[:, (i + 1) % 2, :], gluw[:, k, i * P:(i + 1) * P], zg[:, k, :], start=(k == 0), stop=(k == 1))
                        mm.then_inc(glu_full, 1)

    def attend_block(l):
        with nc.Block() as block:
            @block.sync
            def _(sp):
                def gate_loads(n):
                    if n >= 2:
                        raw_load(sp, l, N_SECOND + n)
                    if n >= WB:
                        sp.wait_ge(side_full, SIDE[("gate", 2 * (n - WB) + 1)] + 1)
                    br, c = BRANCHES[n // 4], n % 4
                    src = A["w_branch"][l, br].rearrange("(k p) n -> p k n", p=P)[:, :, c * CW:(c + 1) * CW]
                    sp.dma_start(wb[:, n % WB], src).then_inc(wb_in[n % WB], 16)

                def far_load(n):
                    if n >= 2:
                        sp.wait_ge(low_done, UNITS_BY[n - 2])
                    sp.dma_start(far[:, n % 2, :], C["c_far"][HEADS[n]]).then_inc(far_in[n % 2], 16)

                far_load(0)
                for n in range(WB):
                    gate_loads(n)
                far_load(1)
                for step, i in ATTEND_STEPS:
                    if step == "scores":
                        n = UNITS[i][0]
                        if i + 1 == UNITS_BY[n] and n + 2 < DILH:
                            far_load(n + 2)
                    elif step == "gate" and i % 2 and i // 2 + WB < N_GATE:
                        gate_loads(i // 2 + WB)
                    elif step == "gate" and i == 24:
                        for c in range(OUT_CHUNKS):
                            out_load(sp, l, c)

            @block.scalar
            def _(act):
                for step, i in ATTEND_STEPS:
                    if step == "scores":
                        act.wait_ge(low_done, i + 1)
                        if i >= 2:
                            act.wait_ge(turn_full, i - 1)
                        n, b = UNITS[i]
                        src = sm if n < DILH else pair
                        if b is None:
                            for t in range(NT):
                                keys = slice(t * P, (t + 1) * P)
                                ins = act.activation(pr[:, i % 2, keys], src[:, i % 2, keys], ACT.Exp, scale=-1.0,
                                                     bias=low[:, 4 * n + t:4 * n + t + 1], accum_out=ssum[:, 4 * n + t:4 * n + t + 1])
                        else:
                            at = slice(4 * n + b, 4 * n + b + 1)
                            ins = act.activation(pr[:, i % 2, :], src[:, i % 2, :], ACT.Exp, scale=-1.0, bias=low[:, at],
                                                 accum_out=ssum[:, at])
                        ins.then_inc(exp_done, 1)
                    elif step == "y":
                        br = BRANCHES[i]
                        if i >= 1:
                            act.wait_ge(side_full, SIDE[("gate", 8 * i - 1)] + 1)
                        if ("features", (br, 1)) in SIDE:
                            act.wait_ge(side_free, SIDE[("features", (br, 1))] + 1)
                        act.activation(y_upper[:, :, :], yT[br][:, :, :], ACT.Copy).then_inc(y_up, 1)
                    elif step == "w_branch":
                        act.wait_ge(wb_in[i // 2 % WB], 16 * (i // 2 // WB + 1))
                        if i >= 2:
                            act.wait_ge(side_full, SIDE[("gate", i - 2)] + 1)
                        act.activation(wb_upper[i % 2][:, :, :], wb[:, i // 2 % WB, :, i % 2 * P:(i % 2 + 1) * P], ACT.Copy).then_inc(wb_up, 1)
                    elif step == "w_out":
                        act.wait_ge(wo_in[i], 16)
                        if i == 0:
                            act.wait_ge(mix_full, N_UNITS)
                        act.activation(wo_upper[i][:, :, :], wo_raw[:, i], ACT.Copy).then_inc(parts_up, 1)
                    elif step == "merged":
                        if i == 0:
                            act.wait_ge(split_low, 2 * len(SPLIT_CHUNKS))
                        act.wait_ge(gate_out, 2 * N_GATE - ND + i + 1)
                        act.activation(merged_upper[:, i, :], merged[:, i, :], ACT.Copy).then_inc(parts_up, 1)
                    elif step == "move":
                        act.activation(h_upper1_moved[:, i, :], h_upper1[:, i, :], ACT.Copy).then_inc(moved, 1)
                    elif step == "split":
                        split_upper(act, 2 * N_SECOND + i)
                    elif step == "turn":
                        act.wait_ge(turn_full, i + 1)
                        if i >= 2:
                            act.wait_ge(mix_full, i - 1)
                        act.activation(pT[:, i % 2, :], ys[:, i % 2, :], ACT.Copy).then_inc(turn_out, 1)
                    elif step == "combine":
                        act.wait_ge(comb_arg, i + 1)
                        act.activation(ew[:, :], ew[:, :], ACT.Exp).then_inc(comb_exp, 1)
                    elif step == "gate":
                        n, j = N_FIRST + N_SECOND + i // 2, i % 2
                        act.wait_ge(acc_full, 2 * n + j + 1)
                        if i >= 2:
                            act.wait_ge(gate_out, i - 1)
                        act.activation(th[:, j, :], acc[:, j, :], ACT.Tanh, scale=0.5).then_inc(acc_free, 1)

            @block.vector
            def _(dve):
                link = Link(dve, dve_link3)
                for step, i in ATTEND_STEPS:
                    if step == "scores":
                        n, b = UNITS[i]
                        dve.wait_ge(score_full, i + 1)
                        if n < DILH:
                            dve.wait_ge(far_in[n % 2], 16 * (n // 2 + 1))
                            if i >= 2:
                                dve.wait_ge(exp_done, i - 1)
                            if b is None:
                                v = sm[:, i % 2, :].rearrange("p (t m) -> p t m", t=NT)
                                link(dve.tensor_tensor(v, pair[:, i % 2, :].rearrange("p (t m) -> p t m", t=NT),
                                                       far[:, n % 2, 0:P].unsqueeze(1).to_broadcast([P, NT, P]), ALU.add))
                                dve.tensor_reduce(low[:, 4 * n:4 * n + 4], v, AX.X, ALU.min).then_inc(low_done, 1)
                            else:
                                dve.tensor_tensor_reduce(out=sm[:, i % 2, :], in0=pair[:, i % 2, :],
                                                         in1=far[:, n % 2, NT - 1 - b:NT - 1 - b + SEQ], scale=1.0, scalar=3e38,
                                                         op0=ALU.add, op1=ALU.min, accum_out=low[:, 4 * n + b:4 * n + b + 1]).then_inc(low_done, 1)
                        else:
                            dve.tensor_reduce(low[:, 4 * n + b:4 * n + b + 1], pair[:, i % 2, :], AX.X, ALU.min).then_inc(low_done, 1)
                    elif step == "y":
                        dve.wait_ge(y_up, i + 1)
                        y = yT[BRANCHES[i]]
                        dve.tensor_tensor(y_lower[BRANCHES[i]][:, :, :], y[:, :, :], y_upper[:, :, :], ALU.subtract).then_inc(y_low, 1)
                    elif step == "w_branch":
                        dve.wait_ge(wb_up, i + 1)
                        at = (slice(None), i // 2 % WB, slice(None), slice(i % 2 * P, (i % 2 + 1) * P))
                        dve.tensor_tensor(wb_lower[at], wb[at], wb_upper[i % 2][:, :, :], ALU.subtract).then_inc(wb_low, 1)
                    elif step == "w_out":
                        dve.wait_ge(parts_up, i + 1)
                        dve.tensor_tensor(wo_lower[:, i], wo_raw[:, i], wo_upper[i][:, :, :], ALU.subtract).then_inc(parts_low, 1)
                    elif step == "merged":
                        dve.wait_ge(parts_up, OUT_CHUNKS + i + 1)
                        dve.tensor_tensor(merged_lower[:, i, :], merged[:, i, :], merged_upper[:, i, :], ALU.subtract).then_inc(parts_low, 1)
                    elif step == "split":
                        split_lower(dve, 2 * N_SECOND + i)
                    elif step == "mix" and i + 1 == UNITS_BY[UNITS[i][0]]:
                        n = UNITS[i][0]
                        dve.wait_ge(mix_full, i + 1)
                        own = HD * (HEADS[n] % 2 if n < DILH else (n - DILH) // 2)
                        bank = misc[:, 0, :].rearrange("p (b d) -> p b d", d=P)[:, :, own:own + HD]
                        if n < DILH:
                            link(dve.tensor_copy(obuf[:, n % 3], bank))
                        else:
                            h = n - DILH
                            dve.wait_ge(exp_done, i + 1)
                            link(dve.reciprocal(rs[:, :], ssum[:, 4 * n:4 * n + 4]))
                            link(dve.tensor_tensor(yt[:, :, h * HD:(h + 1) * HD], bank, rs[:, :].unsqueeze(2).to_broadcast([P, 4, HD]), ALU.mult))
                        dve.sem_inc(o_free, 1)
                    elif step == "combine":
                        lo = low[:, 12 * i:12 * i + 12]
                        dve.wait_ge(exp_done, UNITS_BY[GROUPS * i + GROUPS - 1])
                        link(dve.tensor_tensor(rs[:, :], lo[:, 0:4], lo[:, 4:8], ALU.min))
                        link(dve.tensor_tensor(rs[:, :], rs[:, :], lo[:, 8:12], ALU.min))
                        v3 = lambda a: a.rearrange("p (g b) -> p g b", g=3)
                        link(dve.tensor_tensor(v3(ew[:, :]), rs[:, :].unsqueeze(1).to_broadcast([P, 3, 4]), v3(lo), ALU.subtract))
                        dve.sem_inc(comb_arg, 1)
                        dve.wait_ge(comb_exp, i + 1)
                        link(dve.tensor_tensor(es[:, :], ew[:, :], ssum[:, 12 * i:12 * i + 12], ALU.mult))
                        link(dve.tensor_tensor(rs[:, :], es[:, 0:4], es[:, 4:8], ALU.add))
                        link(dve.tensor_tensor(rs[:, :], rs[:, :], es[:, 8:12], ALU.add))
                        link(dve.reciprocal(rs[:, :], rs[:, :]))
                        link(dve.tensor_tensor(v3(es[:, :]), v3(ew[:, :]), rs[:, :].unsqueeze(1).to_broadcast([P, 3, 4]), ALU.mult))
                        flat = obuf[:, :, :, :].rearrange("p g b d -> p (g b) d")
                        link(dve.tensor_tensor(flat, flat, es[:, :].unsqueeze(2).to_broadcast([P, 12, HD]), ALU.mult))
                        link(dve.tensor_tensor(obuf[:, 0], obuf[:, 0], obuf[:, 1], ALU.add))
                        link(dve.tensor_tensor(yt[:, :, i * HD:(i + 1) * HD], obuf[:, 0], obuf[:, 2], ALU.add))
                    elif step == "features":
                        br, c = i
                        if c == 0:
                            dve.sem_inc(yt_ready, 1)
                        dve.wait_ge(side_full, SIDE[("features", i)] + 1)
                        if br == 1:
                            link(dve.tensor_copy(apart(yT[br][:, c, :]), misc[:, 1, :].rearrange("p (t m) -> p t m", t=NT)))
                        else:
                            link(dve.tensor_copy(yT[br][:, c, :], misc[:, 1, :]))
                        dve.sem_inc(side_free, 1)
                    elif step == "gate":
                        br, d = i // 8, i % 8
                        dve.wait_ge(acc_free, 2 * (N_FIRST + N_SECOND) + i + 1)
                        dve.wait_ge(side_full, SIDE[("gate", i)] + 1)
                        if br == 0:
                            link(dve.scalar_tensor_tensor(merged[:, d, :], th[:, i % 2, :], 1.0, misc[:, 1, :], ALU.add, ALU.mult))
                            dve.sem_inc(side_free, 1)
                        else:
                            link(dve.scalar_tensor_tensor(term[:, :], th[:, i % 2, :], 1.0, misc[:, 1, :], ALU.add, ALU.mult))
                            dve.sem_inc(side_free, 1)
                            link(dve.tensor_tensor(merged[:, d, :], merged[:, d, :], term[:, :], ALU.add))
                        if br == 3:
                            link(dve.tensor_scalar(merged[:, d, :], merged[:, d, :], 0.5, None, ALU.mult))
                        dve.sem_inc(gate_out, 1)

            @block.tensor
            def _(pe):
                for step, i in ATTEND_STEPS:
                    if step == "scores":
                        n, b = UNITS[i]
                        if i >= 2:
                            pe.wait_ge(low_done if i - 2 < N_DIL else exp_done, i - 1)
                        if n < DILH:
                            h = HEADS[n]
                            q, k = qd[:, h, :], kd[:, h // 2, :]
                        else:
                            h = n - DILH
                            q, k = qg[:, h, :], kg[:, :]
                        if b is None:
                            for t in range(NT):
                                own = slice(t * P, (t + 1) * P)
                                mm = pe.matmul(pair[:, i % 2, own], q[:, own], k[:, own], start=True, stop=True)
                        else:
                            mm = pe.matmul(pair[:, i % 2, :], q[:, b * P:(b + 1) * P], k, start=True, stop=True)
                        mm.then_inc(score_full, 1)
                    elif step == "turn":
                        pe.wait_ge(exp_done, i + 1)
                        if i >= 2:
                            pe.wait_ge(turn_out, i - 1)
                        for kc in range(NT):
                            mm = pe.transpose(ys[:, i % 2, kc * P:(kc + 1) * P], pr[:, i % 2, kc * P:(kc + 1) * P], ident[:, :])
                        mm.then_inc(turn_full, 1)
                    elif step == "mix":
                        n, b = UNITS[i]
                        pe.wait_ge(turn_out, i + 1)
                        if b in (0, None) and n >= 1:
                            pe.wait_ge(o_free, n)
                        if n < DILH:
                            h = HEADS[n]
                            v = vd[:, :, h // 2 * P:(h // 2 + 1) * P]
                        else:
                            v = gtok[:, :, 6 * HD:8 * HD]
                        for kc in range(NT):
                            if b is None:
                                mm = pe.matmul(misc[:, 0, kc * P:(kc + 1) * P], pT[:, i % 2, kc * P:(kc + 1) * P], v[:, kc, :], start=True, stop=True)
                            else:
                                mm = pe.matmul(misc[:, 0, b * P:(b + 1) * P], pT[:, i % 2, kc * P:(kc + 1) * P], v[:, kc, :], start=(kc == 0), stop=(kc == NT - 1))
                        mm.then_inc(mix_full, 1)
                    elif step == "features":
                        br, c = i
                        if c == 0:
                            pe.wait_ge(yt_ready, 1 if br == 1 else 2)
                        if SIDE[("features", i)] >= 1:
                            pe.wait_ge(side_free, SIDE[("features", i)])
                        for b in range(NT):
                            mm = pe.transpose(misc[:, 1, b * P:(b + 1) * P], yt[:, b, c * P:(c + 1) * P], ident[:, :])
                        mm.then_inc(side_full, 1)
                    elif step == "gate":
                        n, j = N_FIRST + N_SECOND + i // 2, i % 2
                        g = 2 * N_SECOND + i
                        pe.wait_ge(split_low, g + 1)
                        if i == 0:
                            pe.wait_ge(moved, 4)
                        pe.wait_ge(acc_free, 2 * N_FIRST + g - 1)
                        split_features(pe, g, (h_upper0, h_upper1_moved)).then_inc(acc_full, 1)
                        br = BRANCHES[i // 8]
                        pe.wait_ge(wb_low, i + 1)
                        if i % 8 == 0:
                            pe.wait_ge(y_low, i // 8 + 1)
                        if SIDE[("gate", i)] >= 1:
                            pe.wait_ge(side_free, SIDE[("gate", i)])
                        for k in range(2):
                            w = (wb_upper[i % 2][:, k, :], wb_lower[:, i // 2 % WB, k, j * P:(j + 1) * P])
                            mm = three_passes(pe, misc[:, 1, :], w, (y_upper[:, k, :], y_lower[br][:, k, :]), k == 0, k == 1)
                        mm.then_inc(side_full, 1)

    def norm_loads(eng, z, g, b):
        eng.dma_start(lng[:, :], g.partition_broadcast(P)).then_inc(z.loaded, 16)
        eng.dma_start(lnb[:, :], b.partition_broadcast(P)).then_inc(z.loaded, 16)

    def norm_order(stages):
        steps = []
        for t in range(NT + max(lag for _, lag in stages)):
            steps += [(name, t - lag) for name, lag in stages if 0 <= t - lag < NT]
        return steps

    def norm_vector(dve, link, z, x, lag, arrive):
        for part, t in norm_order([("stats", 0), ("product", 1), ("scale", 0)] if lag else [("stats", 0), ("scale", 0), ("product", 0)]):
            if part == "stats":
                for s in range(2):
                    arrive(t, s)
                    link.mark(dve.bn_stats(lnst[:, t, 6 * s:6 * s + 6], x[:, t, s * 512:(s + 1) * 512]))
                link.hold()
                link(dve.bn_aggr(lnmv[:, t, :], lnst[:, t, :]))
                dve.sem_inc(z.var, 1)
            elif part == "scale":
                dve.wait_ge(z.root, t + 1)
                link(dve.reciprocal(lnrs[:, t:t + 1], lnrs[:, t:t + 1]))
                dve.scalar_tensor_tensor(lnsh[:, t:t + 1], lnmv[:, t, 0:1], -1.0, lnrs[:, t:t + 1], ALU.mult, ALU.mult).then_inc(z.scale, 1)
            else:
                if t == 0:
                    dve.wait_ge(z.loaded, 32)
                dve.wait_ge(z.normed, t + 1)
                dve.tensor_tensor(h[:, t, :], h[:, t, :], lng[:, :], ALU.mult).then_inc(z.product, 1)

    def norm_pool(pool, z):
        for t in range(NT):
            pool.wait_ge(z.product, t + 1)
            pool.tensor_tensor(h[:, t, :], h[:, t, :], lnb[:, :], ALU.add).then_inc(z.out, 1)

    def norm_scalar(act, z, x, lag):
        for part, t in norm_order([("root", 0), ("apply", 0), ("copy", lag)]):
            if part == "root":
                act.wait_ge(z.var, t + 1)
                act.activation(lnrs[:, t:t + 1], lnmv[:, t, 1:2], ACT.Sqrt, bias=eps_ln[:, :]).then_inc(z.root, 1)
            elif part == "apply":
                act.wait_ge(z.scale, t + 1)
                act.activation(h[:, t, :], x[:, t, :], ACT.Identity, scale=lnrs[:, t:t + 1], bias=lnsh[:, t:t + 1]).then_inc(z.normed, 1)
            else:
                for s in range(2):
                    act.wait_ge(z.full, 2 * t + s + 1)
                    act.activation(hT[:, 4 * s:4 * s + 4, t * P:(t + 1) * P], misc[:, s, :].rearrange("p (c n) -> p c n", c=4),
                                   ACT.Copy).then_inc(z.free, 1)

    def turn_tile(pe, z, t):
        pe.wait_ge(z.out, t + 1)
        for s in range(2):
            if t >= 1:
                pe.wait_ge(z.free, 2 * t + s - 1)
            for c in range(4):
                mm = pe.transpose(misc[:, s, c * P:(c + 1) * P], h[:, t, (4 * s + c) * P:(4 * s + c + 1) * P], ident[:, :])
            mm.then_inc(z.full, 1)

    def norm_store(sp, z):
        for t in range(NT):
            sp.wait_ge(z.out, t + 1)
            sp.dma_start(out[t * P:(t + 1) * P, :], h[:, t, :]).then_inc(z.stored, 16)
        sp.wait_ge(z.stored, 16 * NT)

    USES = [("exp_w_gate", 0, 0), ("exp_w_gate", 0, 1), ("exp_w_up", 0, 0), ("exp_w_up", 0, 1),
            ("exp_w_gate", 1, 0), ("exp_w_gate", 1, 1), ("exp_w_up", 1, 0), ("exp_w_up", 1, 1),
            ("exp_w_down", 0, 0), ("exp_w_down", 1, 0), ("exp_w_down", 0, 1), ("exp_w_down", 1, 1)]

    def slot(i, u):
        g = len(USES) * i + u
        return g % SLOTS_E, g // SLOTS_E + 1

    def used(i, u):
        k, n = slot(i, u)
        return slot_used[k], n

    def expert_load(sp, l, i, u):
        w, q, half = USES[u]
        k, n = slot(i, u)
        if n >= 2:
            sp.wait_ge(slot_used[k], n - 1)
        src = A[w][l, 2 * i + q].rearrange("(c p) n -> p c n", p=P)[:, 4 * half:4 * half + 4, :]
        sp.dma_start(ering[k][:, :, :], src).then_inc(slot_in[k], 16)

    def start_block():
        z = norm_1
        with nc.Block() as block:
            @block.sync
            def _(sp):
                for t in range(NT):
                    sp.dma_start(h[:, t, :], A["x"][t * P:(t + 1) * P, :]).then_inc(rows_in[t], 16)
                sp.dma_start(ident[:, :], C["c_ident"]).then_inc(x_in, 16)
                sp.dma_start(wf[:, :], C["c_wf"]).then_inc(x_in, 16)
                norm_loads(sp, z, A["ln_in_g"], A["ln_in_b"])
                norm_store(sp, z)

            @block.gpsimd
            def _(pool):
                pool.memset(ones[:, :], 1.0)
                pool.memset(half_pi[:, :], math.pi / 2)
                pool.memset(eps_ln[:, :], LN_EPS).then_inc(pads, 1)
                pool.memset(eps_rms[:, :], RMS_EPS)
                norm_pool(pool, z)

            @block.scalar
            def _(act):
                act.wait_ge(pads, 1)
                norm_scalar(act, z, h, 1)

            @block.vector
            def _(dve):
                norm_vector(dve, Link(dve, dve_link4), z, h, 1, lambda t, s: dve.wait_ge(rows_in[t], 16))

            @block.tensor
            def _(pe):
                pe.wait_ge(x_in, 32)
                for t in range(NT):
                    turn_tile(pe, z, t)

    def finish_block(l):
        z = norm_1
        with nc.Block() as block:
            @block.sync
            def _(sp):
                sp.dma_start(h[:, :, :], out.rearrange("(t p) n -> p t n", p=P)).then_inc(x_in, 16)
                norm_loads(sp, z, A["ln1_g"][l], A["ln1_b"][l])
                sp.dma_start(rw[:, :, :], A["router_w"][l].rearrange("(c p) e -> p c e", p=P)).then_inc(rw_in, 16)
                expert_load(sp, l, 0, 5)
                sp.wait_ge(acc_full, 2 * (N_FIRST + N_SECOND + N_GATE + OUT_CHUNKS))
                for u in range(5):
                    expert_load(sp, l, 0, u)
                sp.wait_ge(route_full, 1)
                expert_load(sp, l, 0, 6)

            @block.gpsimd
            def _(pool):
                norm_pool(pool, z)

            @block.scalar
            def _(act):
                norm_scalar(act, z, h, 1)
                act.wait_ge(route_arg, 1)
                act.activation(aff[:, :, :], aff[:, :, :], ACT.Exp).then_inc(route_exp, 1)
                act.wait_ge(route_turned, 1)
                act.activation(affT[:, :], pair[0:NE, 1, :], ACT.Copy).then_inc(aff_out, 1)
                for t in range(NT):
                    act.activation(accx[:, t, :], h[:, t, :], ACT.Copy, scale=ALPHA)
                act.wait_ge(pos_turned, 1)
                act.activation(posT[:, :, :], pair[:, 0, 0:NT * NE].rearrange("p (t e) -> p t e", e=NE), ACT.Copy).then_inc(pos_out, 1)

            @block.vector
            def _(dve):
                link = Link(dve, dve_link4)

                def residual(t, s):
                    u = 2 * (N_FIRST + N_SECOND + N_GATE) + 2 * t + s
                    if t == 0 and s == 0:
                        dve.wait_ge(x_in, 16)
                    dve.wait_ge(acc_full, u + 1)
                    hs = h[:, t, s * 512:(s + 1) * 512]
                    link(dve.scalar_tensor_tensor(hs, hs, ALPHA, acc[:, s, :], ALU.mult, ALU.add))
                    dve.sem_inc(acc_free, 1)

                norm_vector(dve, link, z, h, 0, residual)
                dve.wait_ge(route_full, 1)
                lg = pair[:, 0, 0:NT * NE].rearrange("p (t e) -> p t e", e=NE)
                link(dve.tensor_reduce(rmax[:, :], lg, AX.X, ALU.max))
                link(dve.tensor_tensor(aff[:, :, :], lg, rmax[:, :].unsqueeze(2).to_broadcast([P, NT, NE]), ALU.subtract))
                dve.sem_inc(route_arg, 1)
                dve.wait_ge(route_exp, 1)
                link(dve.tensor_reduce(rmax[:, :], aff[:, :, :], AX.X, ALU.add))
                link(dve.reciprocal(rmax[:, :], rmax[:, :]))
                link(dve.tensor_tensor(aff[:, :, :], aff[:, :, :], rmax[:, :].unsqueeze(2).to_broadcast([P, NT, NE]), ALU.mult))
                dve.sem_inc(route_soft, 1)
                dve.wait_ge(aff_out, 1)
                for r in range(CAP // 8):
                    src = affT if r == 0 else work
                    link(dve.max(top8[:, :], src[:, :]))
                    if r < CAP // 8 - 1:
                        link(dve.match_replace(work[:, :], top8[:, :], src[:, :], -1.0))
                kth = top8[:, 7:8]
                every = wide(ones[0:NE, 0:1], SEQ)
                link.mark(dve.tensor_scalar(gt[:, :], affT[:, :], kth, None, ALU.is_gt))
                link(dve.tensor_scalar(eq[:, :], affT[:, :], kth, None, ALU.is_equal))
                link.mark(dve.tensor_reduce(left[:, :], gt[:, :], AX.X, ALU.add))
                link(dve.tensor_tensor_scan(work[:, :], every, eq[:, :], 0.0, ALU.mult, ALU.add))
                link(dve.tensor_scalar(left[:, :], left[:, :], -1.0, float(CAP), ALU.mult, ALU.add))
                link(dve.scalar_tensor_tensor(eq[:, :], work[:, :], left[:, 0:1], eq[:, :], ALU.is_le, ALU.mult))
                link(dve.tensor_tensor(gt[:, :], gt[:, :], eq[:, :], ALU.add))
                link(dve.tensor_tensor_scan(work[:, :], every, gt[:, :], 0.0, ALU.mult, ALU.add))
                dve.tensor_tensor(work[:, :], work[:, :], gt[:, :], ALU.mult).then_inc(pos_ready, 1)

            @block.tensor
            def _(pe):
                pe.wait_ge(parts_low, OUT_CHUNKS + ND)

                def out_tile(t):
                    for s in range(2):
                        pe.wait_ge(acc_free, 2 * (N_FIRST + N_SECOND + N_GATE) + 2 * t + s - 1)
                        for q in range(2):
                            c = 2 * s + q
                            for k in range(ND):
                                x = (merged_upper[:, k, t * P:(t + 1) * P], merged_lower[:, k, t * P:(t + 1) * P])
                                w = (wo_upper[c][:, k, :], wo_lower[:, c, k, :])
                                mm = three_passes(pe, acc[:, s, q * CW:(q + 1) * CW], x, w, k == 0, k == ND - 1)
                        mm.then_inc(acc_full, 1)

                def route_tile(t):
                    pe.wait_ge(z.free, 2 * t + 2)
                    for k in range(ND):
                        mm = pe.matmul(pair[:, 0, t * NE:(t + 1) * NE], hT[:, k, t * P:(t + 1) * P], rw[:, k, :], start=(k == 0), stop=(k == ND - 1))
                    return mm

                out_tile(0)
                out_tile(1)
                turn_tile(pe, z, 0)
                out_tile(2)
                pe.wait_ge(rw_in, 16)
                route_tile(0)
                turn_tile(pe, z, 1)
                out_tile(3)
                route_tile(1)
                turn_tile(pe, z, 2)
                route_tile(2)
                turn_tile(pe, z, 3)
                mm = route_tile(3)
                mm.then_inc(route_full, 1)
                pe.wait_ge(route_soft, 1)
                for t in range(NT):
                    mm = pe.transpose(pair[0:NE, 1, t * P:(t + 1) * P], aff[:, t, :], ident[:, :])
                mm.then_inc(route_turned, 1)
                pe.wait_ge(pos_ready, 1)
                for t in range(NT):
                    mm = pe.transpose(pair[:, 0, t * NE:(t + 1) * NE], work[:, t * P:(t + 1) * P], ident[0:NE, 0:NE])
                mm.then_inc(pos_turned, 1)

    def experts_block(l):
        z = norm_2
        PAIRS = NE // 2

        with nc.Block() as block:
            @block.sync
            def _(sp):
                norm_loads(sp, z, A["ln2_g"][l], A["ln2_b"][l])
                sp.dma_start(slots[:, :], C["c_iota"][:, 1:CAP + 1]).then_inc(slots_in, 16)
                for i in range(PAIRS):
                    for u in range(7 if i == 0 else 0, len(USES)):
                        expert_load(sp, l, i, u)
                norm_store(sp, z)

            @block.gpsimd
            def _(pool):
                for done in sems:
                    if done not in late_sems:
                        pool.sem_clear(done)
                norm_pool(pool, z)

            @block.scalar
            def _(act):
                for i in range(PAIRS):
                    act.wait_ge(gather_full, i + 1)
                    act.activation(xs[:, :, :], misc[:, :, :].rearrange("p b (c n) -> p (b c) n", n=P), ACT.Copy).then_inc(xs_out, 1)
                    act.wait_ge(pgT_full, i + 1)
                    if i >= 2:
                        act.wait_ge(spread_full, 8 * (i - 1))
                    act.activation(pgT[:, i % 2, :], misc[:, 0, :], ACT.Copy).then_inc(pgT_out, 1)
                    for q in range(2):
                        v = 2 * i + q
                        act.wait_ge(*used(i, (3, 7)[q]))
                        if v >= 1:
                            act.wait_ge(hid_out, v)
                        act.activation(sg[:, :], acc[:, 0, :], ACT.Silu).then_inc(silu_out, 1)
                        act.wait_ge(hidT_full, v + 1)
                        if v >= 2:
                            act.wait_ge(*used(i - 1, 11))
                        act.activation(hidT[:, q, :], misc[:, q, :], ACT.Copy).then_inc(hidT_out, 1)
                    act.wait_ge(*used(i, 11))
                    if i >= 1:
                        act.wait_ge(spread_full, 8 * i)
                    act.activation(oute[:, :], ys[:, :, :].rearrange("p a n -> p (a n)"), ACT.Copy).then_inc(oute_out, 1)
                norm_scalar(act, z, accx, 2)

            @block.vector
            def _(dve):
                link = Link(dve, dve_link5)
                dve.wait_ge(slots_in, 16)
                def choose(i):
                    if i >= 1:
                        dve.wait_ge(pgT_full, i)
                    e = slice(2 * i, 2 * i + 2)
                    pp4 = pp[:, :, :].rearrange("p t (e n) -> p t e n", e=2)
                    pg4 = pg[:, :, :].rearrange("p t (e n) -> p t e n", e=2)
                    for t in range(NT):
                        link.mark(dve.tensor_tensor(pp4[:, t], slots[:, :].unsqueeze(1).to_broadcast([P, 2, CAP]),
                                                    posT[:, t, e].unsqueeze(2).to_broadcast([P, 2, CAP]), ALU.is_equal))
                    link.hold()
                    for t in range(NT):
                        link.mark(dve.tensor_tensor(pg4[:, t], pp4[:, t], aff[:, t, e].unsqueeze(2).to_broadcast([P, 2, CAP]), ALU.mult))
                    link.hold()
                    dve.sem_inc(chosen, 1)

                def add_spread(i, t, n):
                    dve.wait_ge(spread_full, 8 * i + 2 * t + n + 1)
                    at = accx[:, t, n * 512:(n + 1) * 512]
                    dve.tensor_tensor(at, at, pair[:, n, :], ALU.add).then_inc(spread_free, 1)

                choose(0)
                for i in range(PAIRS):
                    if i + 1 < PAIRS:
                        choose(i + 1)
                    for q in range(2):
                        v = 2 * i + q
                        dve.wait_ge(silu_out, v + 1)
                        if v >= 1:
                            dve.wait_ge(hidT_full, v)
                        dve.tensor_tensor(hid[:, :], sg[:, :], acc[:, 1, :], ALU.mult).then_inc(hid_out, 1)
                        if q == 0 and i >= 1:
                            for t in range(NT):
                                for n in range(2):
                                    add_spread(i - 1, t, n)

                def last_spread(t, n):
                    add_spread(PAIRS - 1, t, n)
                    dve.wait_ge(spread_free, 8 * (PAIRS - 1) + 2 * t + n + 1)

                norm_vector(dve, link, z, accx, 1, last_spread)

            @block.tensor
            def _(pe):
                def gather(i):
                    pe.wait_ge(chosen, i + 1)
                    if i >= 1:
                        pe.wait_ge(hidT_out, 2 * i)
                    for c in range(ND):
                        for t in range(NT):
                            mm = pe.matmul(misc[:, c // 4, (c % 4) * P:(c % 4 + 1) * P], h[:, t, c * P:(c + 1) * P], pp[:, t, :],
                                           start=(t == 0), stop=(t == NT - 1))
                    mm.then_inc(gather_full, 1)
                    pe.wait_ge(xs_out, i + 1)
                    for t in range(NT):
                        mm = pe.transpose(misc[:, 0, t * P:(t + 1) * P], pg[:, t, :], ident[:, :])
                    mm.then_inc(pgT_full, 1)

                def hidden(i, q):
                    v = 2 * i + q
                    if v >= 1:
                        pe.wait_ge(hid_out, v)
                    for part in range(2):
                        for half in range(2):
                            u = 4 * q + 2 * part + half
                            k, used_by = slot(i, u)
                            pe.wait_ge(slot_in[k], 16 * used_by)
                            for c in range(4):
                                for n in range(2):
                                    mm = pe.matmul(acc[CAP * n:CAP * n + CAP, part, :], xs[:, 4 * half + c, q * CAP:(q + 1) * CAP],
                                                   ering[k][:, c, n * 512:(n + 1) * 512],
                                                   start=(half == 0 and c == 0), stop=(half == 1 and c == 3))
                            mm.then_inc(slot_used[k], 1)

                def turn_hidden(i, q):
                    v = 2 * i + q
                    pe.wait_ge(hid_out, v + 1)
                    if q == 0:
                        pe.wait_ge(pgT_out, i + 1)
                    for j in range(4):
                        mm = pe.transpose(misc[:, q, j * P:(j + 1) * P], hid[:, j * P:(j + 1) * P], ident[:, :])
                    mm.then_inc(hidT_full, 1)

                def down(i):
                    pe.wait_ge(hidT_out, 2 * i + 2)
                    if i >= 1:
                        pe.wait_ge(oute_out, i)
                    for half in range(2):
                        for q in range(2):
                            u = 8 + 2 * half + q
                            k, used_by = slot(i, u)
                            pe.wait_ge(slot_in[k], 16 * used_by)
                        for c in range(4):
                            for n in range(2):
                                for q in range(2):
                                    k, _ = slot(i, 8 + 2 * half + q)
                                    mm = pe.matmul(ys[CAP * q:CAP * q + CAP, n, :], hidT[:, q, c * P + half * CAP:c * P + half * CAP + CAP],
                                                   ering[k][:, c, n * 512:(n + 1) * 512],
                                                   start=(half == 0 and c == 0), stop=(half == 1 and c == 3))
                                    if c == 3 and n == 1:
                                        mm.then_inc(slot_used[k], 1)

                def spread(i, t):
                    pe.wait_ge(oute_out, i + 1)
                    for n in range(2):
                        u = 2 * t + n
                        if 8 * i + u >= 2:
                            pe.wait_ge(spread_free, 8 * i + u - 1)
                        mm = pe.matmul(pair[:, u % 2, :], pgT[:, i % 2, t * P:(t + 1) * P], oute[:, n * 512:(n + 1) * 512], start=True, stop=True)
                        mm.then_inc(spread_full, 1)

                gather(0)
                for i in range(PAIRS):
                    hidden(i, 0)
                    if i >= 1:
                        for t in range(NT):
                            spread(i - 1, t)
                    turn_hidden(i, 0)
                    hidden(i, 1)
                    turn_hidden(i, 1)
                    down(i)
                    if i + 1 < PAIRS:
                        gather(i + 1)
                for t in range(NT + 2):
                    if t < NT:
                        spread(PAIRS - 1, t)
                    if t >= 2:
                        turn_tile(pe, z, t - 2)

    def clear_block(which):
        with nc.Block() as block:
            @block.gpsimd
            def _(pool):
                for s in which:
                    pool.sem_clear(s)

    start_block()
    clear_block(norm_1.all + [pads, x_in, dve_link4] + rows_in)
    with nc.Fori(0, DEPTH) as l:
        first_block(l)
        second_block(l)
        attend_block(l)
        finish_block(l)
        experts_block(l)
        clear_block(late_sems)


def kernel(**inputs):
    import numpy as _np
    import concourse.bacc as _bacc
    from concourse import mybir as _mybir
    from concourse.bass_utils import run_bass_kernel_spmd as _run

    nc = _bacc.Bacc("TRN2", target_bir_lowering=False, num_devices=1)
    arrays, A = {}, {}

    def give(name, a):
        a = _np.ascontiguousarray(a)
        arrays[f"in_{name}_dram"] = a
        return nc.dram_tensor(f"in_{name}_dram", a.shape, _mybir.dt.from_np(a.dtype), kind="ExternalInput").ap()

    for name, a in lay_out(inputs).items():
        A[name] = give(name, a)
    A["const"] = {name: give(name, a) for name, a in constants().items()}
    out = nc.dram_tensor("out_0_dram", (1, SEQ, DM), F32, kind="ExternalOutput").ap()
    build(nc, A, out[0])
    r = _run(nc, [arrays], core_ids=[0])
    return r.results[0]["out_0_dram"]
```
